# Optimizing a Trainium2 kernel written in Bass

```python
import jax, jax.numpy as jnp
from jax import lax
import numpy as np

D_MODEL = 1024
BATCH = 1
SEQ = 1024
DEPTH = 1
DEC_BATCH = 8
DEC_SEQ = 1
PAST_LEN = 4096
PAGE_SIZE = 128

MLA_HEADS = 8
MLA_NOPE = 64
MLA_ROPE = 32
MLA_VDIM = 64
MLA_Q_RANK = 256
MLA_KV_RANK = 128
MLA_SCALE = (MLA_NOPE + MLA_ROPE) ** -0.5
ROPE_THETA = 10000.0
Q_BLOCK = 128
GLA_HEADS = 4
GLA_DK = 64
GLA_DV = 128
GLA_GATE_RANK = 16
GLA_TAU = 16.0
GLA_CHUNK = 64

MLA_WIDTH = MLA_HEADS * MLA_VDIM
GLA_WIDTH = GLA_HEADS * GLA_DV
MIX_WIDTH = MLA_WIDTH + GLA_WIDTH
IN_SPLITS = (MLA_Q_RANK, MLA_KV_RANK, MLA_ROPE, MLA_WIDTH, GLA_HEADS * GLA_DK, GLA_HEADS * GLA_DK, GLA_WIDTH, GLA_GATE_RANK, GLA_WIDTH)
IN_WIDTH = MLA_Q_RANK + MLA_KV_RANK + MLA_ROPE + MLA_WIDTH + 2 * GLA_HEADS * GLA_DK + GLA_WIDTH + GLA_GATE_RANK + GLA_WIDTH
DEEPNORM_ALPHA = (2 * DEPTH) ** 0.25
DEEPNORM_BETA = (8 * DEPTH) ** -0.25
NORM_EPS = 1e-6

kernel_name = "hybrid_mla_gla_deepnorm_adaln_step"

F32 = jnp.float32

def rms_norm(x, g):
    xf = x.astype(F32)
    y = xf * lax.rsqrt(jnp.mean(xf * xf, axis=-1, keepdims=True) + NORM_EPS)
    return (y * g.astype(F32)).astype(x.dtype)

def layer_norm(x, g, b):
    xf = x.astype(F32)
    mu = jnp.mean(xf, axis=-1, keepdims=True)
    var = jnp.mean(jnp.square(xf - mu), axis=-1, keepdims=True)
    y = (xf - mu) * lax.rsqrt(var + NORM_EPS)
    return (y * g.astype(F32) + b.astype(F32)).astype(x.dtype)

def rope_cos_sin(pos):
    inv = ROPE_THETA ** (-jnp.arange(0, MLA_ROPE, 2, dtype=F32) / MLA_ROPE)
    ang = pos.astype(F32)[:, None] * inv[None, :]
    return jnp.cos(ang), jnp.sin(ang)

def apply_rope(x, cos, sin):
    half = MLA_ROPE // 2
    xf = x.astype(F32)
    x1, x2 = xf[..., :half], xf[..., half:]
    return jnp.concatenate([x1 * cos - x2 * sin, x2 * cos + x1 * sin], axis=-1).astype(x.dtype)

def ada_modulation(c, w_ada, b_ada):
    mod = jax.nn.silu(c) @ w_ada + b_ada
    shift, scale, gate = jnp.split(mod, 3, axis=-1)
    return shift, scale, gate

def project(h, cos, sin, w_in, q_norm_g, w_uq, kv_norm_g, w_gate_up, b_gate):
    B, S = h.shape[0], h.shape[1]
    z = h @ w_in
    offs = [int(o) for o in np.cumsum(IN_SPLITS)[:-1]]
    cq, ckv, kr, g_mla, gq, gk, gv, glr, g_gla = jnp.split(z, offs, axis=-1)
    q = (rms_norm(cq, q_norm_g) @ w_uq).reshape(B, S, MLA_HEADS, MLA_NOPE + MLA_ROPE)
    q_nope = q[..., :MLA_NOPE]
    q_rope = apply_rope(q[..., MLA_NOPE:], cos[:, None, :], sin[:, None, :])
    ckv = rms_norm(ckv, kv_norm_g)
    kr = apply_rope(kr, cos, sin)
    gla_q = gq.reshape(B, S, GLA_HEADS, GLA_DK) * (GLA_DK ** -0.5)
    gla_k = gk.reshape(B, S, GLA_HEADS, GLA_DK)
    gla_v = gv.reshape(B, S, GLA_HEADS, GLA_DV)
    log_a = jax.nn.log_sigmoid((glr @ w_gate_up + b_gate).astype(F32)) / GLA_TAU
    log_a = log_a.reshape(B, S, GLA_HEADS, GLA_DK)
    return q_nope, q_rope, ckv, kr, g_mla, gla_q, gla_k, gla_v, log_a, g_gla

def mla_prompt(q_nope, q_rope, ckv, kr, w_uk, w_uv):
    B, S = q_nope.shape[0], q_nope.shape[1]
    k_nope = jnp.einsum('bsr,rhn->bshn', ckv, w_uk)
    v = jnp.einsum('bsr,rhv->bshv', ckv, w_uv)
    nb = S // Q_BLOCK
    qn_b = q_nope.reshape(B, nb, Q_BLOCK, MLA_HEADS, MLA_NOPE).transpose(1, 0, 2, 3, 4)
    qr_b = q_rope.reshape(B, nb, Q_BLOCK, MLA_HEADS, MLA_ROPE).transpose(1, 0, 2, 3, 4)
    key_pos = jnp.arange(S)

    def block(args):
        i, qn, qr = args
        s = jnp.einsum('bqhn,bkhn->bhqk', qn, k_nope) + jnp.einsum('bqhp,bkp->bhqk', qr, kr)
        s = s.astype(F32) * MLA_SCALE
        q_pos = i * Q_BLOCK + jnp.arange(Q_BLOCK)
        s = jnp.where(key_pos[None, :] <= q_pos[:, None], s, -jnp.inf)
        p = jax.nn.softmax(s, axis=-1).astype(v.dtype)
        return jnp.einsum('bhqk,bkhv->bqhv', p, v)

    o = lax.map(block, (jnp.arange(nb), qn_b, qr_b))
    return o.transpose(1, 0, 2, 3, 4).reshape(B, S, MLA_HEADS, MLA_VDIM)

def mla_sample(q_nope, q_rope, ckv_new, kr_new, cache_lat, cache_kr, page_table, w_uk, w_uv):
    Bd, Sd = q_nope.shape[0], q_nope.shape[1]
    lat_past = cache_lat[page_table].reshape(Bd, -1, MLA_KV_RANK)
    kr_past = cache_kr[page_table].reshape(Bd, -1, MLA_ROPE)
    q_lat = jnp.einsum('bshn,rhn->bshr', q_nope, w_uk)
    s_past = jnp.einsum('bshr,btr->bhst', q_lat, lat_past) + jnp.einsum('bshp,btp->bhst', q_rope, kr_past)
    s_new = jnp.einsum('bshr,btr->bhst', q_lat, ckv_new) + jnp.einsum('bshp,btp->bhst', q_rope, kr_new)
    causal = jnp.tril(jnp.ones((Sd, Sd), dtype=bool))
    s_new = jnp.where(causal, s_new.astype(F32), -jnp.inf)
    s = jnp.concatenate([s_past.astype(F32), s_new], axis=-1) * MLA_SCALE
    lat_all = jnp.concatenate([lat_past, ckv_new], axis=1)
    p = jax.nn.softmax(s, axis=-1).astype(lat_all.dtype)
    o_lat = jnp.einsum('bhst,btr->bshr', p, lat_all)
    return jnp.einsum('bshr,rhv->bshv', o_lat, w_uv)

def gla_chunked(q, k, v, log_a):
    B, S = q.shape[0], q.shape[1]
    nc = S // GLA_CHUNK

    def to_chunks(t):
        d = t.shape[-1]
        return t.astype(F32).reshape(B, nc, GLA_CHUNK, GLA_HEADS, d).transpose(1, 0, 3, 2, 4)

    xs = (to_chunks(q), to_chunks(k), to_chunks(v), to_chunks(log_a))
    causal = jnp.tril(jnp.ones((GLA_CHUNK, GLA_CHUNK), dtype=bool))

    def step(state, inp):
        qc, kc, vc, gc = inp
        b = jnp.cumsum(gc, axis=2)
        o_inter = jnp.einsum('bhcd,bhde->bhce', qc * jnp.exp(b), state)
        diff = b[:, :, :, None, :] - b[:, :, None, :, :]
        dec = jnp.exp(jnp.where(causal[None, None, :, :, None], diff, -jnp.inf))
        att = jnp.einsum('bhid,bhjd,bhijd->bhij', qc, kc, dec)
        o_intra = jnp.einsum('bhij,bhje->bhie', att, vc)
        b_last = b[:, :, -1:, :]
        new_state = jnp.exp(b_last[:, :, 0, :])[..., None] * state + jnp.einsum('bhcd,bhce->bhde', kc * jnp.exp(b_last - b), vc)
        return new_state, o_inter + o_intra

    s0 = jnp.zeros((B, GLA_HEADS, GLA_DK, GLA_DV), F32)
    s_fin, o = lax.scan(step, s0, xs)
    o = o.transpose(1, 0, 3, 2, 4).reshape(B, S, GLA_HEADS, GLA_DV)
    return o.astype(v.dtype), s_fin.astype(v.dtype)

def gla_recurrent(q, k, v, log_a, state0):
    xs = tuple(t.astype(F32).transpose(1, 0, 2, 3) for t in (q, k, v, log_a))

    def step(state, inp):
        qt, kt, vt, gt = inp
        state = jnp.exp(gt)[..., None] * state + kt[..., None] * vt[..., None, :]
        return state, jnp.einsum('bhd,bhde->bhe', qt, state)

    s_fin, o = lax.scan(step, state0.astype(F32), xs)
    return o.transpose(1, 0, 2, 3).astype(v.dtype), s_fin.astype(state0.dtype)

def finish(x, mla_o, gla_o, g_mla, g_gla, gla_norm_g, w_out, gate_c, ln_g, ln_b):
    B, S = x.shape[0], x.shape[1]
    mla = mla_o.reshape(B, S, MLA_WIDTH) * jax.nn.silu(g_mla)
    gla = rms_norm(gla_o, gla_norm_g).reshape(B, S, GLA_WIDTH) * jax.nn.silu(g_gla)
    sub = jnp.concatenate([mla, gla], axis=-1) @ w_out
    return layer_norm(DEEPNORM_ALPHA * x + gate_c[:, None, :] * sub, ln_g, ln_b)

def setup_inputs(seed: int = 0) -> dict:
    key = jax.random.key(seed)
    ks = jax.random.split(key, 24)
    n_pages = PAST_LEN // PAGE_SIZE
    n_used = DEC_BATCH * n_pages
    n_phys = n_used + max(1, n_used // 4)
    nrm = jax.random.normal
    page_table = jax.random.permutation(ks[0], n_phys)[:n_used].reshape(DEC_BATCH, n_pages).astype(jnp.int32)
    return {
        "x_prompt": nrm(ks[1], (BATCH, SEQ, D_MODEL), F32),
        "x_sample": nrm(ks[2], (DEC_BATCH, DEC_SEQ, D_MODEL), F32),
        "cache_kv_latent": nrm(ks[3], (DEPTH, n_phys, PAGE_SIZE, MLA_KV_RANK), F32),
        "cache_k_rope": nrm(ks[4], (DEPTH, n_phys, PAGE_SIZE, MLA_ROPE), F32),
        "state_gla": nrm(ks[5], (DEPTH, DEC_BATCH, GLA_HEADS, GLA_DK, GLA_DV), F32),
        "page_table": page_table,
        "c_prompt": nrm(ks[6], (BATCH, D_MODEL), F32),
        "c_sample": nrm(ks[7], (DEC_BATCH, D_MODEL), F32),
        "w_ada": nrm(ks[8], (DEPTH, D_MODEL, 3 * D_MODEL), F32) * (0.5 * D_MODEL ** -0.5),
        "b_ada": nrm(ks[9], (DEPTH, 3 * D_MODEL), F32) * 0.02,
        "w_in": nrm(ks[10], (DEPTH, D_MODEL, IN_WIDTH), F32) * D_MODEL ** -0.5,
        "q_norm_g": 1.0 + 0.01 * nrm(ks[11], (DEPTH, MLA_Q_RANK), F32),
        "w_uq": nrm(ks[12], (DEPTH, MLA_Q_RANK, MLA_HEADS * (MLA_NOPE + MLA_ROPE)), F32) * MLA_Q_RANK ** -0.5,
        "kv_norm_g": 1.0 + 0.01 * nrm(ks[13], (DEPTH, MLA_KV_RANK), F32),
        "w_uk": nrm(ks[14], (DEPTH, MLA_KV_RANK, MLA_HEADS, MLA_NOPE), F32) * MLA_KV_RANK ** -0.5,
        "w_uv": nrm(ks[15], (DEPTH, MLA_KV_RANK, MLA_HEADS, MLA_VDIM), F32) * MLA_KV_RANK ** -0.5,
        "w_gate_up": nrm(ks[16], (DEPTH, GLA_GATE_RANK, GLA_HEADS * GLA_DK), F32) * GLA_GATE_RANK ** -0.5,
        "b_gate": nrm(ks[17], (DEPTH, GLA_HEADS * GLA_DK), F32) * 0.02,
        "gla_norm_g": 1.0 + 0.01 * nrm(ks[18], (DEPTH, GLA_HEADS, GLA_DV), F32),
        "w_out": nrm(ks[19], (DEPTH, MIX_WIDTH, D_MODEL), F32) * (MIX_WIDTH ** -0.5 * DEEPNORM_BETA),
        "ln_g": 1.0 + 0.01 * nrm(ks[20], (DEPTH, D_MODEL), F32),
        "ln_b": 0.01 * nrm(ks[21], (DEPTH, D_MODEL), F32),
    }

def reference(x_prompt, x_sample, cache_kv_latent, cache_k_rope, state_gla, page_table, c_prompt, c_sample,
              w_ada, b_ada, w_in, q_norm_g, w_uq, kv_norm_g, w_uk, w_uv, w_gate_up, b_gate, gla_norm_g,
              w_out, ln_g, ln_b):
    cos_p, sin_p = rope_cos_sin(jnp.arange(x_prompt.shape[1], dtype=jnp.int32))
    past_len = page_table.shape[1] * PAGE_SIZE
    cos_s, sin_s = rope_cos_sin(past_len + jnp.arange(x_sample.shape[1], dtype=jnp.int32))
    xp, xs = x_prompt, x_sample
    lat_p, kr_p, st_p, lat_s, kr_s, st_s = [], [], [], [], [], []
    for l in range(DEPTH):
        shift, scale, gate = ada_modulation(c_prompt, w_ada[l], b_ada[l])
        h = xp * (1.0 + scale[:, None, :]) + shift[:, None, :]
        qn, qr, ckv, kr, g_mla, gq, gk, gv, la, g_gla = project(h, cos_p, sin_p, w_in[l], q_norm_g[l], w_uq[l], kv_norm_g[l], w_gate_up[l], b_gate[l])
        mla_o = mla_prompt(qn, qr, ckv, kr, w_uk[l], w_uv[l])
        gla_o, s_fin = gla_chunked(gq, gk, gv, la)
        xp = finish(xp, mla_o, gla_o, g_mla, g_gla, gla_norm_g[l], w_out[l], gate, ln_g[l], ln_b[l])
        lat_p.append(ckv)
        kr_p.append(kr)
        st_p.append(s_fin)
        shift, scale, gate = ada_modulation(c_sample, w_ada[l], b_ada[l])
        h = xs * (1.0 + scale[:, None, :]) + shift[:, None, :]
        qn, qr, ckv, kr, g_mla, gq, gk, gv, la, g_gla = project(h, cos_s, sin_s, w_in[l], q_norm_g[l], w_uq[l], kv_norm_g[l], w_gate_up[l], b_gate[l])
        mla_o = mla_sample(qn, qr, ckv, kr, cache_kv_latent[l], cache_k_rope[l], page_table, w_uk[l], w_uv[l])
        gla_o, s_fin = gla_recurrent(gq, gk, gv, la, state_gla[l])
        xs = finish(xs, mla_o, gla_o, g_mla, g_gla, gla_norm_g[l], w_out[l], gate, ln_g[l], ln_b[l])
        lat_s.append(ckv)
        kr_s.append(kr)
        st_s.append(s_fin)
    return (xp, xs, jnp.stack(lat_p), jnp.stack(kr_p), jnp.stack(st_p), jnp.stack(lat_s), jnp.stack(kr_s), jnp.stack(st_s))


_drawn_inputs = setup_inputs


def setup_inputs(seed=0):
    import zlib

    import numpy as np

    out = dict(_drawn_inputs(seed))
    spreads = {}
    factors = {'cache_kv_latent': 8.0,
     'cache_k_rope': 8.0,
     'q_norm_g': 8.0,
     'w_uq': 7.979,
     'kv_norm_g': 5.37,
     'w_uk': 8.0,
     'w_uv': 2.831,
     'b_gate': 6.489,
     'gla_norm_g': 8.0,
     'ln_g': 5.776,
     'ln_b': 5.49}
    for name, (base, spread) in spreads.items():
        noise = np.random.default_rng([zlib.crc32(name.encode()), seed]).standard_normal(out[name].shape)
        drawn = base * np.exp(spread * noise) if base else spread * noise
        out[name] = __import__('jax').numpy.asarray(drawn.astype(out[name].dtype))
    for name, factor in factors.items():
        out[name] = (out[name] * factor).astype(out[name].dtype)
    return out
```

```python
from contextlib import ExitStack

import numpy as np

import concourse.bass as bass
from concourse import mybir

F32 = mybir.dt.float32
I32 = mybir.dt.int32
U8 = mybir.dt.uint8
ALU = mybir.AluOpType
ACT = mybir.ActivationFunctionType
AX_X = mybir.AxisListType.X

P = 128
D = 1024
SEQ = 1024
NB = 8
PAST, PAGE = 4096, 128
H, NOPE, ROPE, VD = 8, 64, 32, 64
QK = NOPE + ROPE
QR, KVR = 256, 128
GH, DK, DV, GR = 4, 64, 128, 16
W_CQ, W_CKV, W_KR, W_GM, W_GQ, W_GK, W_GV, W_GL, W_GG, W_END = (
    int(v) for v in np.cumsum([0, QR, KVR, ROPE, H * VD, GH * DK, GH * DK, GH * DV, GR, GH * DV]))
EPS = 1e-6
ALPHA = 2.0 ** 0.25
MLA_SCALE = float(QK) ** -0.5
GLA_SCALE = float(DK) ** -0.5
TAU = 16.0
T = SEQ // P
KT = D // P
CH = 496
NCH = W_END // CH
LEVELS = 7
ROWS = 4
SUBS = PAGE // ROWS
SLOTS = 4
HALF = 4
NSTEP = PAST // (P * ROWS)
CN = 8432
NEG = -1.0e30
LN_EXP_SET = 6


def shape_constants():
    r = np.arange(P)
    c = {}
    c["ident"] = np.eye(P, dtype=np.float32)
    c["upto"] = (r[:, None] <= r[None, :]).astype(np.float32)
    c["after"] = (r[:, None] > r[None, :]).astype(np.float32)
    c["future"] = np.where(r[None, :] > r[:, None], NEG, 0).astype(np.float32)
    m = np.zeros((P, LEVELS, P), np.float32)
    for lv in range(LEVELS):
        s = P >> (lv + 1)
        same = (r[:, None] // (2 * s)) == (r[None, :] // (2 * s))
        m[:, lv] = same & ((r[:, None] // s) % 2 == 0) & ((r[None, :] // s) % 2 == 1)
    c["pairs"] = m
    inv = (np.float32(10000.0) ** (-np.arange(0, ROPE, 2, dtype=np.float32) / np.float32(ROPE))).astype(np.float32)
    pos = np.concatenate([np.arange(SEQ), np.full(P, PAST)]).astype(np.float32)
    ang = (pos[:, None] * inv[None, :]).astype(np.float32)
    cos, sin = np.cos(ang), np.sin(ang)
    t = np.stack([np.concatenate([cos, cos], 1), np.concatenate([-sin, sin], 1)], 1)
    c["rope"] = np.ascontiguousarray(
        t.reshape(T + 1, P, 2, ROPE).transpose(1, 0, 2, 3)).astype(np.float32)
    fold = np.zeros((P, 32), np.float32)
    spread = np.zeros((NB, 2, P), np.float32)
    for g in range(4):
        for b in range(NB):
            fold[32 * g + b, b] = 1
        for hf in range(2):
            spread[HALF * hf + g, hf, 32 * g:32 * g + 32] = 1
    c["fold"] = fold
    c["spread"] = spread
    g1 = np.zeros((64, 2, P + 32), np.float32)
    for ch in range(2):
        g1[32 * ch + NB, ch, :P] = 1
        for b in range(NB):
            g1[32 * ch + b, ch, P + b] = 1
    c["pick"] = g1
    own = np.zeros((P, NB, NB), np.float32)
    own[:, np.arange(NB), np.arange(NB)] = 1
    c["own"] = own
    own8 = np.zeros((NB, NB), np.float32)
    own8[np.arange(NB), np.arange(NB)] = 1
    c["own8"] = own8
    c["sub"] = (np.arange(P) % SUBS).astype(np.float32)[:, None]
    return c


def hybrid_step(nc, a, o):
    with ExitStack() as ctx:
        def sb(name, shape, dt=F32):
            return ctx.enter_context(nc.sbuf_tensor("s_" + name, shape, dt))

        def sem(name):
            return ctx.enter_context(nc.semaphore(name))

        z = sb("z", [P, T, W_END])
        kt_buf = sb("kt", [P, H * SEQ])
        act_buf = sb("actT", [P, KT, SEQ])
        C = sb("temps", [P, CN])
        zs = sb("zs", [NB, W_END])
        x_all = kt_buf[:].rearrange("p (t d) -> p t d", t=T)
        KTh = kt_buf[0:QK, :].rearrange("p (h s) -> p h s", h=H)
        w_out = kt_buf[:].rearrange("p (k n) -> p k n", k=KT)
        hT = act_buf
        mixT = act_buf

        ident = sb("ident", [P, P])
        upto = sb("upto", [P, P])
        after = sb("after", [P, P])
        future = sb("future", [P, P])
        pairs = sb("pairs", [P, LEVELS, P], U8)
        rope = sb("rope", [P, T + 1, 2, ROPE])
        fold = sb("fold", [P, 32])
        own = sb("own", [P, NB, NB])
        own8 = sb("own8", [NB, NB])
        sub = sb("sub", [P, 1])
        w_uq = sb("w_uq", [P, 2, H * QK])
        w_uk = sb("w_uk", [P, H * NOPE])
        w_uv = sb("w_uv", [P, H * VD])
        w_gu = sb("w_gu", [GR, GH * DK])
        g_q = sb("g_q", [P, QR])
        g_kv = sb("g_kv", [P, KVR])
        b_gt = sb("b_gt", [P, GH * DK])
        g_gla = sb("g_gla", [P, GH * DV])
        modB = sb("modB", [64, 512])
        hsT = sb("hsT", [P, KT, 32])
        eps_t = sb("eps_t", [P, 1])
        mixTs = hsT
        banks = ctx.enter_context(nc.psum_tensor("banks", [P, 8, 512], F32))

        taken = [0]

        def carve(n, *dims, rows=P, at=None, region=None):
            region = C if region is None else region
            start = taken[0] if at is None else at
            taken[0] = start + n
            v = region[0:rows, start:start + n]
            if len(dims) > 1:
                names = "abcd"[:len(dims)]
                v = v.rearrange(f"p ({' '.join(names)}) -> p {' '.join(names)}",
                                **{k: d for k, d in zip(names, dims)})
            return v

        z_flat = z[:].rearrange("p t n -> p (t n)")
        NADA = 6
        ada_ring = [z_flat[:, i * 3 * D:(i + 1) * 3 * D] for i in range(NADA)]
        taken[0] = 0
        c_in = carve(D, rows=9)
        c_act = carve(D, rows=9)
        cT = carve(KT * 32, KT, 32)
        x_s = carve(D, rows=NB)
        xsT = carve(KT * NB, KT, NB)
        b_adaA = carve(512)
        b_adaB = carve(512)
        modA = carve(512)
        shT = carve(KT)
        scT = carve(KT)
        shsT = carve(KT * NB, KT, NB)
        scsT = carve(KT * NB, KT, NB)
        hs_tmp = carve(KT * NB, KT, NB)
        pairs_f = carve(LEVELS * P, LEVELS, P)
        assert taken[0] <= CN

        w_ring = [carve(KT * CH, KT, CH, at=i * KT * CH) for i in range(2)]
        zs_part = carve(CH)
        assert taken[0] <= CN

        taken[0] = 0
        junk = carve(512)
        ss = carve(2)
        lnss = carve(2)
        rstd = carve(2)
        cqn = carve(QR)
        ckvn = carve(KVR)
        kr96 = carve(QK)
        rtmp = carve(ROPE)
        ckvT = carve(P)
        qk_st = carve(1024)
        gl_st = carve(GR)
        glT = carve(P, rows=GR)
        qkT = carve(4 * P, 4, P)
        zg = carve(256)
        zneg = carve(256)
        zmin = carve(256)
        la = carve(256)
        bT = carve(256)
        eb = carve(256)
        qb = carve(256)
        esuf = carve(256)
        kdec = carve(256)
        dl = [carve(256) for _ in range(2)]
        xl = [carve(256) for _ in range(2)]
        attm = carve(512, 2, 2, P)
        gated = carve(512)
        gg = carve(512)
        ss4 = carve(4)
        rstd4 = carve(4)
        S = carve(2 * DV, 2, DV)
        assert taken[0] <= CN, taken[0]

        taken[0] = 0
        q_tok = carve(H * QK)
        q_rt = carve(H * ROPE)
        QTb = [carve(H * P, H, P, rows=QK) for _ in range(2)]
        Pm = [carve(SEQ) for _ in range(2)] + [z[:, 0, W_GV:W_GV + SEQ]]
        PTb = [carve(T * P, T, P) for _ in range(3)]
        nmx = carve(4)
        rsum = carve(4)
        rinv = carve(4)
        assert taken[0] <= CN, taken[0]

        zr = z_flat
        taken[0] = 0
        LAT = HALF * ROWS * KVR
        RO = HALF * ROWS * ROPE
        lat = [carve(LAT, HALF, ROWS * KVR, region=zr) for _ in range(SLOTS)]
        kro = [carve(RO, HALF, ROWS * ROPE, region=zr) for _ in range(SLOTS)]
        sc = carve(512, region=zr)
        pT = carve(512, 4, P, region=zr)
        o_acc = carve(2 * KVR, 2, KVR, region=zr)
        m_run = carve(2, region=zr)
        l_run = carve(2, region=zr)
        st = carve(8, region=zr)
        qls = carve(NB * 32, NB, 32, region=zr)
        qrs = carve(NB * 4 * 32, NB, 4, 32, region=zr)
        knT = carve(NB, region=zr)
        krnT = carve(NB, region=zr)
        sq = carve(H * QK, region=zr, rows=NB)
        sq_r = carve(H * ROPE, region=zr, rows=NB)
        s_cqn = carve(QR, region=zr, rows=NB)
        s_ckvn = carve(KVR, region=zr, rows=NB)
        s_kr = carve(ROPE, region=zr, rows=NB)
        s_kr4 = carve(4 * ROPE, 4, ROPE, region=zr, rows=NB)
        s_cqT = carve(2 * 32, 2, 32, region=zr)
        s_ql = carve(H * NB, H, NB, region=zr, rows=NOPE)
        w_ukT = carve(H * P, H, P, region=zr, rows=NOPE)
        s_ss = carve(8, region=zr, rows=NB)
        s_zg = carve(256, region=zr, rows=NB)
        s_zn = carve(256, region=zr, rows=NB)
        s_zm = carve(256, region=zr, rows=NB)
        s_la = carve(256, region=zr, rows=NB)
        s_glT = carve(NB, region=zr, rows=GR)
        s_decT = carve(2 * NB, 2, NB, region=zr)
        s_qgT = carve(2 * NB, 2, NB, region=zr)
        s_gg = carve(512, region=zr, rows=NB)
        s_qz = carve(2 * NB * 32, 2, NB, 32, region=zr)
        oT_lat = carve(2 * P, 2, P, region=zr)
        o_n = carve(2 * KVR, 2, KVR, region=zr)
        spread = carve(2 * P, 2, P, region=zr, rows=NB)
        pick = carve(2 * (P + 32), 2, P + 32, region=zr, rows=64)
        s_gmT = carve(4 * NB, 4, NB, region=zr)
        pt_i = ctx.enter_context(nc.sbuf_tensor("s_pt", [P, NB * NSTEP], I32))
        idx = ctx.enter_context(nc.sbuf_tensor("s_idx", [P, NB * NSTEP], I32))
        idx_st = [sb(f"idx_st{i}", [P, HALF], I32) for i in range(SLOTS)]
        mst = [carve(KT * P, KT, P, region=zr)]
        assert taken[0] <= T * W_END

        taken[0] = 0
        state = carve(NB * 2 * DV, NB, 2, DV)
        s_kz = carve(NB * 256, NB, 256, rows=NB)
        latT = [carve(LAT, HALF, ROWS * KVR)]
        kroT = [carve(RO, HALF, ROWS * ROPE)]
        sq4 = carve(H * 4 * ROPE, H, 4, ROPE, rows=NB)
        s_junk = carve(512, rows=NB)
        s_gl = s_junk
        assert taken[0] <= CN

        taken[0] = 0
        latT.append(carve(LAT, HALF, ROWS * KVR))
        kroT.append(carve(RO, HALF, ROWS * ROPE))

        taken[0] = 0
        mst.append(carve(KT * P, KT, P))
        r_t = carve(D)
        y_t = carve(D)
        x_t = carve(D)
        g_ln = carve(D)
        b_ln = carve(D)
        gateP = carve(D)
        gateS = carve(D, rows=NB)
        bst = carve(12)
        bag = carve(2)
        lr = carve(2)
        assert taken[0] <= CN, taken[0]

        const_in = sem("const_in")
        held = sem("held")
        x_in = [sem(f"x_in{i}") for i in range(2)]
        ada_in = [sem(f"ada_in{i}") for i in range(6)]
        w_in_in = [sem(f"w_in_in{i}") for i in range(2)]
        padded = sem("padded")
        masks_ready = sem("masks_ready")
        chain_d = sem("chain_d")
        chain_a = sem("chain_a")
        c_ready = sem("c_ready")
        x_transposed = sem("x_transposed")
        x_copied = sem("x_copied")
        c_transposed = sem("c_transposed")
        cT_ready = sem("cT_ready")
        ada_used = sem("ada_used")
        sproj_part = sem("sproj_part")
        mod_ready = sem("mod_ready")
        modT_done = sem("modT_done")
        h_ready = sem("h_ready")
        proj_done = sem("proj_done")
        proj_copied = sem("proj_copied")
        sproj_done = sem("sproj_done")
        sproj_copied = sem("sproj_copied")
        silu_done = sem("silu_done")
        staged = sem("staged")
        gg_ready = sem("gg_ready")
        rstd_ready = sem("rstd_ready")
        normed = sem("normed")
        kv_out = sem("kv_out")
        a_transposed = sem("a_transposed")
        a_copied = sem("a_copied")
        qk_transposed = sem("qk_transposed")
        glT_copied = sem("glT_copied")
        qkT_copied = sem("qkT_copied")
        gate_done = sem("gate_done")
        gate_copied = sem("gate_copied")
        zneg_ready = sem("zneg_ready")
        lnz_ready = sem("lnz_ready")
        la_ready = sem("la_ready")
        kv_done = sem("kv_done")
        k_copied = sem("k_copied")
        v_copied = sem("v_copied")
        cum_done = sem("cum_done")
        bT_copied = sem("bT_copied")
        e_ready = sem("e_ready")
        kdec_ready = sem("kdec_ready")
        qb_ready = sem("qb_ready")
        d_ready = sem("d_ready")
        el_ready = sem("el_ready")
        x_ready = sem("x_ready")
        att_done = sem("att_done")
        att_copied = sem("att_copied")
        o_done = sem("o_done")
        state_done = sem("state_done")
        S_ready = sem("S_ready")
        r4_ready = sem("r4_ready")
        gated_ready = sem("gated_ready")
        gated_T = sem("gated_T")
        mix_copied = sem("mix_copied")
        S_out = sem("S_out")
        qp_done = sem("qp_done")
        qp_copied = sem("qp_copied")
        q_roped = sem("q_roped")
        qt_done = sem("qt_done")
        qt_copied = sem("qt_copied")
        gt_done = sem("gt_done")
        gt_copied = sem("gt_copied")
        sc_done = sem("sc_done")
        mx_ready = sem("mx_ready")
        p_ready = sem("p_ready")
        pn_ready = sem("pn_ready")
        pt_done = sem("pt_done")
        pt_copied = sem("pt_copied")
        pv_done = sem("pv_done")
        mixed = sem("mixed")
        def samp(name):
            return sem("samp_" + name)
        p_padded = samp("padded")
        p_idx = samp("idx")
        p_pt = samp("pt")
        p_state_in = samp("state_in")
        p_tabs = samp("tabs")
        p_rstd = samp("rstd")
        p_norm = samp("norm")
        p_out = samp("out")
        p_T1 = samp("T1")
        p_T1c = samp("T1c")
        p_wTc = samp("wTc")
        p_q = samp("q")
        p_qc = samp("qc")
        p_zn = samp("zn")
        p_ln = samp("ln")
        p_la = samp("la")
        p_dec = samp("dec")
        p_q4 = samp("q4")
        p_qT = samp("qT")
        p_qTc = samp("qTc")
        p_qlat = samp("qlat")
        p_qls = samp("qls")
        p_init = samp("init")
        p_initc = samp("initc")
        p_kz = samp("kz")
        p_T2 = samp("T2")
        p_T2c = samp("T2c")
        p_kv = samp("kv")
        p_state = samp("state")
        p_o = samp("o")
        p_r4 = samp("r4")
        p_gl = samp("gl")
        p_T3 = samp("T3")
        p_T3c = samp("T3c")
        f_idx = samp("f_idx")
        f_in = [samp(f"f_in{i}") for i in range(SLOTS)]
        f_T = samp("f_T")
        f_Ta = samp("f_Ta")
        f_Td = samp("f_Td")
        f_sc = samp("f_sc")
        f_mx = samp("f_mx")
        f_p = samp("f_p")
        f_pT = samp("f_pT")
        f_pTc = samp("f_pTc")
        f_o = samp("f_o")
        f_acc = samp("f_acc")
        f_on = samp("f_on")
        f_oT = samp("f_oT")
        f_oTc = samp("f_oTc")
        f_v = samp("f_v")
        f_mix = samp("f_mix")
        w_out_in = sem("w_out_in")
        ln_in = sem("ln_in")
        gate_b = sem("gate_b")
        gate_bc = sem("gate_bc")
        m_staged = sem("m_staged")
        xt_in = sem("xt_in")
        y_proj = sem("y_proj")
        y_read = sem("y_read")
        y_var = sem("y_var")
        y_rstd = sem("y_rstd")
        y_scaled = sem("y_scaled")
        y_ready = sem("y_ready")
        y_out = sem("y_out")

        FROM_ONE = (S_ready, a_copied, a_transposed, cum_done, f_Ta, f_Td, f_acc, f_p, f_pT, f_pTc, f_sc, gated_T, gated_ready, kv_done, kv_out, mix_copied, normed, state_done, y_out, y_proj, y_read)

        LAG = 2
        STEPS = [(i, h) for i in range(T) for h in range(H)]

        NSTEPS = 2 * NSTEP

        def groups(s):
            return sum(i // 4 + 1 for i, _ in STEPS[:s])

        def gla_out(h):
            return banks[:, (7, 1)[h % 2], P * (h // 2):P * (h // 2) + P]

        def V(j, h):
            return z[:, j, W_GQ + VD * h:W_GQ + VD * h + VD]

        def gT(i):
            return z[:, i, W_GM:W_GQ].rearrange("p (h s) -> p h s", h=4)

        def score_bank(s):
            return banks[:, 2 * (s % 2):2 * (s % 2) + 2, :].rearrange("p b n -> p (b n)")

        def halves(v, s):
            w = v.rearrange("p (b two s) -> p b two s", two=2, s=s)
            return w[:, :, 0, :], w[:, :, 1, :]

        def rope_of(n):
            return rope[:, n, 0, :], rope[:, n, 1, :]

        lat_rows = a["cache_kv_latent"].rearrange("n (s r) d -> (n s) (r d)", r=ROWS)
        kro_rows = a["cache_k_rope"].rearrange("n (s r) d -> (n s) (r d)", r=ROWS)

        block = ctx.enter_context(nc.Block())

        def hold(eng):
            eng.sem_inc(held, 1)

        CONSTS = [
            (ident[:], a["c_ident"]), (upto[:], a["c_upto"]), (after[:], a["c_after"]),
            (future[:], a["c_future"]), (pairs_f, a["c_pairs"]), (rope[:], a["c_rope"]),
            (fold[:], a["c_fold"]),
            (own[:], a["c_own"]), (own8[:], a["c_own8"]), (sub[:], a["c_sub"]),
            (w_uq[:], a["w_uq"].rearrange("(k p) n -> p k n", p=P)),
            (w_uk[:], a["w_uk"].rearrange("r h n -> r (h n)")),
            (w_uv[:], a["w_uv"].rearrange("r h n -> r (h n)")),
            (w_gu[:], a["w_gate_up"]),
            (g_q[:], a["q_norm_g"].to_broadcast([P, QR])),
            (g_kv[:], a["kv_norm_g"].to_broadcast([P, KVR])),
            (b_gt[:], a["b_gate"].to_broadcast([P, GH * DK])),
            (g_gla[:], a["gla_norm_g"].rearrange("h v -> (h v)").unsqueeze(0).to_broadcast([P, GH * DV])),
        ]
        EARLY = [(c_in[0:NB, :], a["c_sample"]), (c_in[NB:NB + 1, :], a["c_prompt"]),
                 (x_s[:], a["x_sample"])]
        for g in range(4):
            EARLY.append((b_adaA[32 * g:32 * g + 32, :], a["b_ada"][:, 512 * g:512 * g + 512].to_broadcast([32, 512])))
        for g in range(2):
            EARLY.append((b_adaB[32 * g:32 * g + 32, :],
                          a["b_ada"][:, 2048 + 512 * g:2560 + 512 * g].to_broadcast([32, 512])))
        early_in = sem("early_in")
        ident_in = sem("ident_in")
        N_EARLY, N_CONST = 16 * len(EARLY), 16 * (len(CONSTS) - 1)
        w_ada = a["w_ada"].rearrange("(k p) n -> k p n", p=P)
        w_in = a["w_in"].rearrange("(k p) n -> p k n", p=P)
        x_p = a["x_prompt"].rearrange("(t p) d -> p t d", p=P)

        @block.sync
        def _(sp):
            for s_ in FROM_ONE:
                sp.sem_inc(s_, 1)
            sp.dma_start(CONSTS[0][0], CONSTS[0][1]).then_inc(ident_in, 16)
            for dst, src in EARLY:
                sp.dma_start(dst, src).then_inc(early_in, 16)
            for half in range(2):
                for t in range(half * 4, half * 4 + 4):
                    sp.dma_start(x_all[:, t, :], x_p[:, t, :]).then_inc(x_in[half], 16)
            for k in range(KT):
                if k >= NADA:
                    sp.wait_ge(ada_used, k - NADA + 1)
                sp.dma_start(ada_ring[k % NADA], w_ada[k]).then_inc(ada_in[k % NADA], 16)
                if k == 3:
                    for dst, src in CONSTS[1:]:
                        sp.dma_start(dst, src).then_inc(const_in, 16)
            sp.wait_ge(h_ready, KT + 1)
            sp.wait_ge(masks_ready, 1)
            for c in range(NCH):
                if c >= 2:
                    sp.wait_ge(proj_done, 8 * (c - 1))
                sp.dma_start(w_ring[c % 2], w_in[:, :, CH * c:CH * c + CH]).then_inc(w_in_in[c % 2], 16)
            with sp.Fori(0, T, 1) as t:
                sp.wait_ge(normed, t + 2)
                sp.dma_start(o["kv_prompt"][0, 0, bass.ds(t * P, P), :], ckvn).then_inc(kv_out, 16)
                sp.dma_start(o["kr_prompt"][0, 0, bass.ds(t * P, P), :], kr96[:, NOPE:QK]).then_inc(kv_out, 16)
            sp.wait_ge(S_ready, 2 * T + 1)
            st_p = o["st_prompt"][0, 0].rearrange("(hp par) d e -> par d hp e", par=2)
            for par in range(2):
                sp.dma_start(st_p[par], S[64 * par:64 * par + 64, :, :]).then_inc(S_out, 16)
            with nc.allow_non_contiguous_dma(reason="page numbers"):
                for b in range(NB):
                    tab = a["page_table"][b:b + 1, :].rearrange("b (c g) -> g (b c)", g=4)
                    for g in range(4):
                        c0 = (b // HALF) * NSTEP * HALF + b % HALF
                        sp.dma_start(pt_i[SUBS * g:SUBS * g + SUBS, c0:c0 + (NSTEP - 1) * HALF + 1:HALF],
                                     tab[g:g + 1, :].to_broadcast([SUBS, NSTEP])).then_inc(p_pt, 16)
            sp.wait_ge(sc_done, len(STEPS))
            sp.dma_start(w_out, a["w_out"].rearrange("(k p) n -> p k n", p=P)).then_inc(w_out_in, 16)
            sp.wait_ge(mixed, len(STEPS) // 2)
            for par in range(2):
                sp.dma_start(state[64 * par:64 * par + 64, :, :, :].rearrange("d b hp e -> d (b hp) e"),
                             a["state_gla"].rearrange("b (hp par) d e -> par d (b hp) e", par=2)[par]).then_inc(p_state_in, 16)
            sp.dma_start(spread, a["c_spread"]).then_inc(p_tabs, 16)
            sp.dma_start(pick, a["c_pick"]).then_inc(p_tabs, 16)
            sp.wait_ge(p_norm, 1)
            sp.dma_start(o["kv_sample"][0, :, 0, :], s_ckvn).then_inc(p_out, 16)
            sp.dma_start(o["kr_sample"][0, :, 0, :], s_kr).then_inc(p_out, 16)
            sp.wait_ge(p_state, 2 * NB)
            for par in range(2):
                sp.dma_start(o["st_sample"][0].rearrange("b (hp par) d e -> par d (b hp) e", par=2)[par],
                             state[64 * par:64 * par + 64, :, :, :].rearrange("d b hp e -> d (b hp) e")).then_inc(p_out, 16)
            sp.wait_ge(mixed, len(STEPS) // 2)
            sp.wait_ge(p_o, 1)
            sp.wait_ge(p_out, 64)
            sp.wait_ge(f_on, 2)
            sp.dma_start(g_ln, a["ln_g"].to_broadcast([P, D])).then_inc(ln_in, 16)
            sp.dma_start(b_ln, a["ln_b"].to_broadcast([P, D])).then_inc(ln_in, 16)
            sp.dma_start(x_t, x_p[:, 0, :]).then_inc(xt_in, 16)
            with sp.Fori(0, T - 1, 1) as t:
                sp.wait_ge(y_var, t + 1)
                sp.dma_start(x_t, x_p[:, bass.ds(t + 1, 1), :]).then_inc(xt_in, 16)
                sp.wait_ge(y_ready, t + 1)
                sp.dma_start(o["y_prompt"][0, bass.ds(t * P, P), :], y_t).then_inc(y_out, 16)
            sp.wait_ge(y_var, T)
            sp.dma_start(x_t[0:NB, :], a["x_sample"]).then_inc(xt_in, 16)
            sp.wait_ge(y_ready, T)
            sp.dma_start(o["y_prompt"][0, (T - 1) * P:, :], y_t).then_inc(y_out, 16)
            sp.wait_ge(y_ready, T + 1)
            sp.dma_start(o["y_sample"][:, 0, :], y_t[0:NB, :]).then_inc(y_out, 16)
            sp.wait_ge(y_out, 16 * (T + 1) + 1)
            sp.wait_ge(p_out, 64)
            sp.wait_ge(S_out, 32)
            sp.wait_ge(kv_out, 32 * T + 1)

        @block.gpsimd
        def _(pool):
            nc.gpsimd.memset(cT, 0.0).then_inc(padded, 1)
            nc.gpsimd.memset(hsT[:], 0.0).then_inc(padded, 1)
            nc.gpsimd.memset(eps_t[:], EPS).then_inc(padded, 1)
            pool.wait_ge(const_in, N_CONST)
            nc.gpsimd.tensor_copy(pairs[:], pairs_f).then_inc(masks_ready, 1)
            pool.wait_ge(silu_done, 4)
            nc.gpsimd.memset(kr96, 0.0).then_inc(padded, 1)
            nc.gpsimd.memset(S, 0.0).then_inc(padded, 1)
            with pool.Fori(0, T, 1) as t:
                pool.wait_ge(state_done, t + 1)
                nc.gpsimd.tensor_copy(qk_st, z[:, bass.ds(t, 1), W_GQ:W_GL]).then_inc(staged, 1)
                nc.gpsimd.tensor_copy(gl_st, z[:, bass.ds(t, 1), W_GL:W_GG]).then_inc(staged, 1)
                pool.wait_ge(gated_ready, t + 1)
                nc.gpsimd.tensor_tensor(gg, z[:, bass.ds(t, 1), W_GG:W_END], g_gla[:].unsqueeze(1), ALU.mult).then_inc(gg_ready, 1)
            pool.wait_ge(p_pt, 16 * 4 * NB)
            pool.wait_ge(const_in, N_CONST)
            nc.gpsimd.tensor_scalar(idx[:], pt_i[:], float(SUBS), sub[:, 0:1], ALU.mult, ALU.add).then_inc(p_idx, 1)
            pool.wait_ge(mixed, len(STEPS) // 2)
            for v in (qls, qrs, s_cqT, s_qz):
                nc.gpsimd.memset(v, 0.0).then_inc(p_padded, 1)
            nc.gpsimd.tensor_tensor(s_kz, zs[:, W_GK:W_GV].unsqueeze(1).to_broadcast([NB, NB, 256]),
                                    own8[:].unsqueeze(2).to_broadcast([NB, NB, 256]), ALU.mult).then_inc(p_kz, 1)
            pool.wait_ge(p_idx, 1)

            def gather(n, u):
                nc.gpsimd.tensor_copy(idx_st[u][:], idx[:, bass.ds(n * HALF, HALF)]).then_inc(f_idx, 1)
                pool.wait_ge(f_idx, n + 1)
                hold(pool)
                for bb in range(HALF):
                    at = bass.IndirectOffsetOnAxis(ap=idx_st[u][:, bb:bb + 1], axis=0)
                    nc.gpsimd.indirect_dma_start(lat[u][:, bb, :], None, lat_rows, at).then_inc(f_in[u], 16)
                    nc.gpsimd.indirect_dma_start(kro[u][:, bb, :], None, kro_rows, at).then_inc(f_in[u], 16)

            for u in range(SLOTS):
                gather(u, u)
            with pool.Fori(0, NSTEPS // SLOTS - 1, 1) as j:
                for u in range(SLOTS):
                    pool.wait_ge(f_o, j * SLOTS + (u + 1))
                    gather(j * SLOTS + (u + SLOTS), u)
            pool.wait_ge(p_o, 1)
            pool.wait_ge(p_out, 64)
            for t in range(2):
                if t == 1:
                    pool.wait_ge(f_on, 2)
                nc.gpsimd.tensor_copy(mst[t], mixT[:, :, P * t:P * t + P]).then_inc(m_staged, 1)
            with pool.Fori(1, T // 2, 1) as j:
                for u in range(2):
                    pool.wait_ge(y_proj, j * 2 + u)
                    nc.gpsimd.tensor_copy(mst[u], mixT[:, :, bass.ds(j * (2 * P) + u * P, P)]).then_inc(m_staged, 1)

        @block.scalar
        def _(act):
            act.wait_ge(early_in, N_EARLY)
            nc.scalar.activation(c_act, c_in, ACT.Silu).then_inc(c_ready, 1)
            def copy_chunk(c):
                for t in range(T):
                    act.wait_ge(proj_done, 8 * c + t + 1)
                    hold(act)
                    nc.scalar.activation(z[:, t, bass.ds(c * CH, CH)], banks[:, t % 6, 0:CH],
                                         ACT.Copy).then_inc(proj_copied, 1)
                act.wait_ge(sproj_done, 2 * c + 2)
                hold(act)
                nc.scalar.activation(zs[:, bass.ds(c * CH, CH)], banks[0:NB, 7, 0:CH],
                                     ACT.Copy).then_inc(sproj_copied, 1)

            copy_chunk(0)
            with act.Fori(1, NCH, 1) as c:
                copy_chunk(c)
            act.wait_ge(proj_copied, T * NCH)
            act.wait_ge(sproj_copied, NCH)
            for w in (W_GM, W_GG):
                nc.scalar.activation(z[:, :, w:w + 512], z[:, :, w:w + 512], ACT.Silu).then_inc(silu_done, 1)
                nc.scalar.activation(zs[:, w:w + 512], zs[:, w:w + 512], ACT.Silu).then_inc(silu_done, 1)
            act.wait_ge(silu_done, 4)
            act.wait_ge(padded, 3)
            act.add_instruction(mybir.InstLoadActFuncSet(name=nc.get_next_instruction_name(), act_func_set_id=LN_EXP_SET,
                                                         ins=[], outs=[]))
            with act.Fori(0, T, 1) as t:
                hold(act)
                nc.scalar.activation(junk[:, 0:QR], z[:, bass.ds(t, 1), W_CQ:W_CKV], ACT.Square, accum_out=ss[:, 0:1]).then_inc(chain_a, 1)
                nc.scalar.activation(junk[:, QR:QR + KVR], z[:, bass.ds(t, 1), W_CKV:W_KR], ACT.Square, accum_out=ss[:, 1:2]).then_inc(chain_a, 1)
                act.wait_ge(chain_a, t * 7 + 2)
                nc.scalar.activation(lnss[:, 0:1], ss[:, 0:1], ACT.Ln, bias=eps_t[:], scale=1.0 / QR).then_inc(chain_a, 1)
                nc.scalar.activation(lnss[:, 1:2], ss[:, 1:2], ACT.Ln, bias=eps_t[:], scale=1.0 / KVR).then_inc(chain_a, 1)
                act.wait_ge(chain_a, t * 7 + 4)
                act.wait_ge(normed, t + 1)
                nc.scalar.activation(rstd, lnss, ACT.Exp, scale=-0.5).then_inc(rstd_ready, 1)
                act.wait_ge(a_transposed, t + 2)
                hold(act)
                nc.scalar.activation(z[:, bass.ds(t, 1), 0:QR], banks[:, 0, 0:QR], ACT.Copy).then_inc(a_copied, 1)
                act.wait_ge(kv_done, t + 1)
                nc.scalar.activation(ckvT, banks[:, 0, QR:QR + P], ACT.Copy).then_inc(a_copied, 1)
                hold(act)
                nc.scalar.activation(KTh[NOPE:QK, :, bass.ds(t * P, P)],
                                     banks[NOPE:QK, 0, 384:512].unsqueeze(1).to_broadcast([ROPE, H, P]), ACT.Copy).then_inc(a_copied, 1)
                act.wait_ge(zneg_ready, t + 1)
                nc.scalar.activation(zneg, zneg, ACT.Exp).then_inc(chain_a, 1)
                act.wait_ge(chain_a, t * 7 + 5)
                nc.scalar.activation(zneg, zneg, ACT.Ln, bias=1.0).then_inc(lnz_ready, 1)
                act.wait_ge(kv_done, t + 2)
                hold(act)
                for q in range(2):
                    nc.scalar.activation(KTh[0:NOPE, 4 * q:4 * q + 4, bass.ds(t * P, P)],
                                         banks[0:NOPE, 3 + q, :].rearrange("p (h s) -> p h s", h=4), ACT.Copy).then_inc(k_copied, 1)
                act.wait_ge(staged, t * 2 + 2)
                hold(act)
                nc.scalar.activation(z[:, bass.ds(t, 1), W_GQ:W_GV], banks[:, 5, :], ACT.Copy).then_inc(v_copied, 1)
                act.wait_ge(bT_copied, t + 1)
                act.wait_ge(cum_done, t + 2)
                nc.scalar.activation(eb, bT, ACT.Exp).then_inc(e_ready, 1)
                nc.scalar.activation(esuf, banks[:, 6, 256:512], ACT.Exp).then_inc(e_ready, 1)
                for lv in range(LEVELS):
                    act.wait_ge(d_ready, t * LEVELS + lv + 1)
                    nc.scalar.activation(dl[lv % 2], dl[lv % 2], ACT.Exp).then_inc(el_ready, 1)
                act.wait_ge(o_done, t + 1)
                for h in range(GH):
                    last = nc.scalar.activation(junk[:, P * h:P * h + P], gla_out(h), ACT.Square, accum_out=ss4[:, h:h + 1])
                    if h == GH - 1:
                        last.then_inc(chain_a, 1)
                act.wait_ge(chain_a, t * 7 + 6)
                nc.scalar.activation(ss4, ss4, ACT.Ln, bias=eps_t[:], scale=1.0 / DV).then_inc(chain_a, 1)
                act.wait_ge(chain_a, t * 7 + 7)
                act.wait_ge(gated_ready, t + 1)
                nc.scalar.activation(rstd4, ss4, ACT.Exp, scale=-0.5).then_inc(r4_ready, 1)
                act.wait_ge(gated_T, t + 2)
                hold(act)
                nc.scalar.activation(mixT[:, 4:8, bass.ds(t * P, P)], banks[:, 2, :].rearrange("p (h s) -> p h s", h=4), ACT.Copy).then_inc(mix_copied, 1)

            def q_half(i, q):
                act.wait_ge(qp_done, 2 * i + q + 1)
                if i > 0:
                    act.wait_ge(qt_done, 2 * i)
                nc.scalar.activation(q_tok[:, 384 * q:384 * q + 384], banks[:, 7, 0:384], ACT.Copy).then_inc(qp_copied, 1)

            def qt_half(i, q):
                act.wait_ge(qt_done, 2 * i + q + 1)
                if i > 1:
                    act.wait_ge(sc_done, H * (i - 1))
                nc.scalar.activation(QTb[i % 2][:, 4 * q:4 * q + 4, :], banks[0:QK, 7, :].rearrange("p (h s) -> p h s", h=4),
                                     ACT.Copy).then_inc(qt_copied, 1)

            act.wait_ge(gated_T, T + 1)
            act.wait_ge(kv_out, 32 * T + 1)
            act.wait_ge(S_out, 32)
            for q in range(2):
                q_half(0, q)
            for q in range(2):
                qt_half(0, q)
            for s in range(len(STEPS) + LAG):
                if s < len(STEPS):
                    i, h = STEPS[s]
                    w = P * (i + 1)
                    if h == 2:
                        act.wait_ge(gt_done, i + 1)
                        nc.scalar.activation(gT(i), banks[:, 7, :].rearrange("p (h s) -> p h s", h=4), ACT.Copy).then_inc(gt_copied, 1)
                    act.wait_ge(mx_ready, s + 1)
                    if s >= 3:
                        act.wait_ge(pt_done, groups(s - 2))
                    nc.scalar.activation(Pm[s % 3][:, 0:w], score_bank(s)[:, 0:w], ACT.Exp, bias=nmx[:, s % 4:s % 4 + 1],
                                         scale=MLA_SCALE, accum_out=rsum[:, s % 4:s % 4 + 1]).then_inc(p_ready, 1)
                if s >= LAG:
                    r = s - LAG
                    i1 = STEPS[r][0]
                    if r >= 3:
                        act.wait_ge(pv_done, (r - 3) // 2 + 1)
                    for g in range(i1 // 4 + 1):
                        n = min(4, i1 + 1 - 4 * g)
                        act.wait_ge(pt_done, groups(r) + g + 1)
                        nc.scalar.activation(PTb[r % 3][:, 4 * g:4 * g + n, :],
                                             banks[:, 4 + (groups(r) + g) % 2, 0:P * n].rearrange("p (j q) -> p j q", j=n),
                                             ACT.Copy).then_inc(pt_copied, 1)
                if s < len(STEPS) and i + 1 < T:
                    if h in (3, 4):
                        q_half(i + 1, h - 3)
                    if h in (6, 7):
                        qt_half(i + 1, h - 6)

            act.wait_ge(mixed, len(STEPS) // 2)
            n_a = T * 7
            nc.scalar.activation(s_junk[:, 0:QR], zs[:, W_CQ:W_CKV], ACT.Square, accum_out=s_ss[:, 0:1]).then_inc(chain_a, 1)
            nc.scalar.activation(s_junk[:, QR:QR + KVR], zs[:, W_CKV:W_KR], ACT.Square, accum_out=s_ss[:, 1:2]).then_inc(chain_a, 1)
            act.wait_ge(chain_a, n_a + 2)
            nc.scalar.activation(s_ss[:, 2:3], s_ss[:, 0:1], ACT.Ln, bias=eps_t[0:NB], scale=1.0 / QR).then_inc(chain_a, 1)
            nc.scalar.activation(s_ss[:, 3:4], s_ss[:, 1:2], ACT.Ln, bias=eps_t[0:NB], scale=1.0 / KVR).then_inc(chain_a, 1)
            act.wait_ge(chain_a, n_a + 4)
            nc.scalar.activation(s_ss[:, 4:6], s_ss[:, 2:4], ACT.Exp, scale=-0.5).then_inc(p_rstd, 1)
            act.wait_ge(p_T1, 1)
            for q in range(2):
                nc.scalar.activation(w_ukT[:, 4 * q:4 * q + 4, :], banks[0:NOPE, 1 + q, :].rearrange("p (h r) -> p h r", h=4), ACT.Copy).then_inc(p_wTc, 1)
            act.wait_ge(p_q, 1)
            for q in range(2):
                nc.scalar.activation(sq[:, 384 * q:384 * q + 384], banks[0:NB, 3 + q, 0:384], ACT.Copy).then_inc(p_qc, 1)
            act.wait_ge(p_zn, 1)
            nc.scalar.activation(s_zn, s_zn, ACT.Exp).then_inc(chain_a, 1)
            act.wait_ge(chain_a, n_a + 5)
            nc.scalar.activation(s_zn, s_zn, ACT.Ln, bias=1.0).then_inc(p_ln, 1)
            act.wait_ge(p_la, 1)
            nc.scalar.activation(s_la, s_la, ACT.Exp).then_inc(p_dec, 1)
            act.wait_ge(p_o, 1)
            for h in range(GH):
                nc.scalar.activation(s_junk[:, P * h:P * h + P], banks[0:NB, 5 + h % 2, P * (h // 2):P * (h // 2) + P], ACT.Square,
                                     accum_out=s_ss[:, h:h + 1]).then_inc(chain_a, 1)
            act.wait_ge(chain_a, n_a + 9)
            nc.scalar.activation(s_ss[:, 0:4], s_ss[:, 0:4], ACT.Ln, bias=eps_t[0:NB], scale=1.0 / DV).then_inc(chain_a, 1)
            act.wait_ge(chain_a, n_a + 10)
            nc.scalar.activation(s_ss[:, 4:8], s_ss[:, 0:4], ACT.Exp, scale=-0.5).then_inc(p_r4, 1)

            def keys_out(n, u):
                act.wait_ge(f_T, n * 5 + 1)
                hold(act)
                nc.scalar.activation(latT[u][:, 0, :], banks[:, 0, :], ACT.Copy).then_inc(f_Ta, 1)
                act.wait_ge(f_T, n * 5 + 3)
                hold(act)
                nc.scalar.activation(latT[u][:, 2, :], banks[:, 2, :], ACT.Copy).then_inc(f_Ta, 1)
                act.wait_ge(f_T, n * 5 + 5)
                hold(act)
                nc.scalar.activation(kroT[u], banks[:, 4, :].rearrange("p (b t) -> p b t", b=HALF), ACT.Copy).then_inc(f_Ta, 1)

            def weights(n, hf):
                act.wait_ge(f_mx, n + 1)
                act.wait_ge(f_pT, n + 1)
                nc.scalar.activation(sc, banks[:, 5, :], ACT.Exp, bias=st[:, 2:3], scale=MLA_SCALE, accum_out=st[:, 4:5]).then_inc(f_p, 1)
                nc.scalar.activation(st[:, 3:4], m_run[:, hf:hf + 1], ACT.Exp, bias=st[:, 2:3], scale=MLA_SCALE).then_inc(f_p, 1)

            act.wait_ge(p_out, 64)
            keys_out(0, 0)
            for hf in range(2):
                with act.Fori(4 * hf, 4 * hf + 4 - hf, 1) as j:
                    for u in range(2):
                        weights(j * 2 + u, hf)
                        keys_out(j * 2 + (u + 1), 1 - u)
            weights(NSTEPS - 2, 1)
            keys_out(NSTEPS - 1, 1)
            weights(NSTEPS - 1, 1)

            for q in range(2):
                act.wait_ge(gate_b, 1)
                nc.scalar.activation(gateP[:, 512 * q:512 * q + 512], banks[:, 2 + q, :], ACT.Copy).then_inc(gate_bc, 1)
                nc.scalar.activation(gateS[:, 512 * q:512 * q + 512], banks[0:NB, 4 + q, :], ACT.Copy).then_inc(gate_bc, 1)

            def deviation(t, rows):
                act.wait_ge(y_var, t + 1)
                nc.scalar.activation(lr[0:rows, 0:1], bag[0:rows, 1:2], ACT.Ln, bias=eps_t[0:rows], scale=1.0).then_inc(chain_a, 1)
                act.wait_ge(chain_a, t + (n_a + 11))
                nc.scalar.activation(lr[0:rows, 1:2], lr[0:rows, 0:1], ACT.Exp, scale=-0.5).then_inc(y_rstd, 1)

            with act.Fori(0, T, 1) as t:
                deviation(t, P)
            deviation(T, NB)

        @block.vector
        def _(dve):
            for n in range(2 * KT):
                k, half = n // 2, n % 2
                dve.wait_ge(x_transposed, n + 1)
                nc.vector.tensor_copy(hT[:, k, 512 * half:512 * half + 512], banks[:, n % 4, :]).then_inc(x_copied, 1)
            dve.wait_ge(x_transposed, 2 * KT + 1)
            nc.vector.tensor_copy(xsT, banks[:, 4, 0:KT * NB].rearrange("p (k b) -> p k b", k=KT)).then_inc(x_copied, 1)
            dve.wait_ge(c_transposed, 1)
            dve.wait_ge(padded, 1)
            nc.vector.tensor_copy(cT[:, :, 0:9], banks[:, 5, 0:KT * 9].rearrange("p (k b) -> p k b", k=KT)).then_inc(cT_ready, 1)
            dve.wait_ge(ada_used, KT)
            nc.vector.tensor_tensor(modA, banks[:, 6, :], b_adaA, ALU.add).then_inc(mod_ready, 1)
            nc.vector.tensor_tensor(modB[:], banks[0:64, 7, :], b_adaB[0:64, :], ALU.add).then_inc(mod_ready, 1)
            dve.wait_ge(modT_done, 1)
            mt = banks[:, 0, :].rearrange("p (s g r) -> p s g r", s=4, g=4)
            kv = lambda t_: t_.rearrange("p (g s) -> p g s", g=2)
            kvb = lambda t_: t_.rearrange("p (g s) b -> p g s b", g=2)
            nc.vector.tensor_copy(kv(shT), mt[:, :, 0:2, NB].rearrange("p s g -> p g s")).then_inc(chain_d, 1)
            nc.vector.tensor_scalar(kv(scT), mt[:, :, 2:4, NB].rearrange("p s g -> p g s"), 1.0, None, ALU.add).then_inc(chain_d, 1)
            for g in range(2):
                nc.vector.tensor_copy(shsT[:, 4 * g:4 * g + 4, :], mt[:, :, g, 0:NB]).then_inc(chain_d, 1)
                nc.vector.tensor_scalar(scsT[:, 4 * g:4 * g + 4, :], mt[:, :, 2 + g, 0:NB], 1.0, None, ALU.add).then_inc(chain_d, 1)
            dve.wait_ge(chain_d, 6)
            dve.wait_ge(x_copied, 2 * KT + 1)
            for k in range(KT):
                nc.vector.tensor_scalar(hT[:, k, :], hT[:, k, :], scT[:, k:k + 1], shT[:, k:k + 1],
                                        ALU.mult, ALU.add).then_inc(h_ready, 1)
            nc.vector.tensor_tensor(hs_tmp, xsT, scsT, ALU.mult).then_inc(chain_d, 1)
            dve.wait_ge(chain_d, 7)
            dve.wait_ge(padded, 2)
            nc.vector.tensor_tensor(hsT[:, :, 0:NB], hs_tmp, shsT, ALU.add).then_inc(h_ready, 1)

            def fold_chunk(c):
                dve.wait_ge(sproj_done, 2 * c + 1)
                nc.vector.tensor_copy(zs_part, banks[:, 6, 0:CH]).then_inc(sproj_part, 1)

            fold_chunk(0)
            with dve.Fori(1, NCH, 1) as c:
                fold_chunk(c)
            n_d = 7
            dve.wait_ge(silu_done, 4)
            dve.wait_ge(const_in, N_CONST)
            dve.wait_ge(padded, 5)
            dve.wait_ge(masks_ready, 1)
            PER_T = 2
            with dve.Fori(0, T, 1) as t:
                at = lambda c: t * PER_T + (n_d + c)
                tz = bass.ds(t, 1)
                dve.wait_ge(rstd_ready, t + 1)
                dve.wait_ge(a_transposed, t + 1)
                dve.wait_ge(kv_out, t * 32 + 1)
                nc.vector.scalar_tensor_tensor(out=cqn, in0=z[:, tz, W_CQ:W_CKV], scalar=rstd[:, 0:1], in1=g_q[:], op0=ALU.mult, op1=ALU.mult)
                nc.vector.scalar_tensor_tensor(out=ckvn, in0=z[:, tz, W_CKV:W_KR], scalar=rstd[:, 1:2], in1=g_kv[:], op0=ALU.mult, op1=ALU.mult)
                kr = z[:, tz, W_KR:W_GM].rearrange("p o e -> p (o e)")
                cs, sn = (rope[:, tz, q, :].rearrange("p o e -> p (o e)") for q in range(2))
                hr = ROPE // 2
                nc.vector.tensor_tensor(kr96[:, NOPE:QK], kr, cs, ALU.mult)
                nc.vector.tensor_tensor(rtmp[:, 0:hr], kr[:, hr:ROPE], sn[:, 0:hr], ALU.mult)
                nc.vector.tensor_tensor(rtmp[:, hr:ROPE], kr[:, 0:hr], sn[:, hr:ROPE], ALU.mult).then_inc(chain_d, 1)
                dve.wait_ge(chain_d, at(1))
                nc.vector.tensor_tensor(kr96[:, NOPE:QK], kr96[:, NOPE:QK], rtmp, ALU.add).then_inc(normed, 1)
                dve.wait_ge(qk_transposed, t + 1)
                nc.vector.tensor_copy(glT, banks[0:GR, 2, 0:P]).then_inc(glT_copied, 1)
                nc.vector.tensor_scalar(qkT[:, 0:2, :], banks[:, 1, 0:256].rearrange("p (a s) -> p a s", a=2), GLA_SCALE, None, ALU.mult)
                nc.vector.tensor_copy(qkT[:, 2:4, :], banks[:, 1, 256:512].rearrange("p (a s) -> p a s", a=2)).then_inc(qkT_copied, 1)
                dve.wait_ge(gate_done, t + 1)
                nc.vector.tensor_tensor(zg, banks[:, 2, 256:512], b_gt[:], ALU.add).then_inc(gate_copied, 1)
                dve.wait_ge(gate_copied, t + 1)
                nc.vector.scalar_tensor_tensor(out=zneg, in0=zg, scalar=-1.0, in1=zg, op0=ALU.mult, op1=ALU.min).then_inc(zneg_ready, 1)
                nc.vector.tensor_scalar(zmin, zg, 0.0, 1.0 / TAU, ALU.min, ALU.mult).then_inc(chain_d, 1)
                dve.wait_ge(lnz_ready, t + 1)
                dve.wait_ge(chain_d, at(2))
                dve.wait_ge(cum_done, t + 1)
                nc.vector.scalar_tensor_tensor(out=la, in0=zneg, scalar=-1.0 / TAU, in1=zmin, op0=ALU.mult, op1=ALU.add).then_inc(la_ready, 1)
                dve.wait_ge(cum_done, t + 2)
                nc.vector.tensor_copy(bT, banks[:, 6, 0:256]).then_inc(bT_copied, 1)
                dve.wait_ge(bT_copied, t + 1)
                dve.wait_ge(qkT_copied, t + 1)
                def level_d(lv):
                    s = P >> (lv + 1)
                    b1, b2 = halves(bT, s)
                    d1, d2 = halves(dl[lv % 2], s)
                    ref = b1[:, :, s - 1:s].to_broadcast([P, P // s, s])
                    nc.vector.tensor_tensor(d1, ref, b1, ALU.subtract)
                    nc.vector.tensor_tensor(d2, b2, ref, ALU.subtract).then_inc(d_ready, 1)

                qf = qkT[:, 0:2, :].rearrange("p a s -> p (a s)")
                kf = qkT[:, 2:4, :].rearrange("p a s -> p (a s)")

                def level_x(lv):
                    s = P >> (lv + 1)
                    e1, e2 = halves(dl[lv % 2], s)
                    x1, x2 = halves(xl[lv % 2], s)
                    dve.wait_ge(el_ready, t * LEVELS + lv + 1)
                    if lv >= 2:
                        dve.wait_ge(att_done, t * (LEVELS + 1) + lv)
                    nc.vector.tensor_tensor(x1, e1, halves(kf, s)[0], ALU.mult)
                    nc.vector.tensor_tensor(x2, e2, halves(qf, s)[1], ALU.mult).then_inc(x_ready, 1)

                pair4 = lambda n: (banks[:, 3:5, 0:256] if n % 2 == 0 else banks[:, 5:8:2, 0:256]).rearrange("p b (h i) -> p b h i", h=2)
                mask4 = lambda m: m.unsqueeze(1).unsqueeze(1).to_broadcast([P, 2, 2, P])
                level_d(0)
                level_d(1)
                dve.wait_ge(att_done, t * (LEVELS + 1) + 1)
                nc.vector.tensor_tensor(attm, pair4(0), mask4(ident[:]), ALU.mult).then_inc(att_copied, 1)
                level_x(0)
                dve.wait_ge(e_ready, t * 2 + 2)
                nc.vector.tensor_tensor(qb, eb, qf, ALU.mult).then_inc(qb_ready, 1)
                nc.vector.tensor_tensor(kdec, esuf, qk_st[:, 256:512], ALU.mult).then_inc(kdec_ready, 1)
                for lv in range(LEVELS):
                    if lv + 1 < LEVELS:
                        level_x(lv + 1)
                    if lv + 2 < LEVELS:
                        dve.wait_ge(x_ready, t * LEVELS + lv + 1)
                        level_d(lv + 2)
                    dve.wait_ge(att_done, t * (LEVELS + 1) + lv + 2)
                    dve.wait_ge(att_copied, t * (LEVELS + 1) + lv + 1)
                    hold(dve)
                    nc.vector.copy_predicated(attm, mask4(pairs[:, lv, :]), pair4(lv + 1)).then_inc(att_copied, 1)
                dve.wait_ge(state_done, t + 2)
                dve.wait_ge(o_done, t + 1)
                for hp in range(2):
                    nc.vector.scalar_tensor_tensor(out=S[:, hp, :], in0=S[:, hp, :], scalar=eb[:, P * hp + P - 1:P * hp + P],
                                                   in1=banks[:, 5, P * hp:P * hp + P], op0=ALU.mult, op1=ALU.add).then_inc(S_ready, 1)
                dve.wait_ge(r4_ready, t + 1)
                dve.wait_ge(gg_ready, t + 1)
                dve.wait_ge(gated_T, t + 1)
                for h in range(GH):
                    last = nc.vector.scalar_tensor_tensor(out=gated[:, P * h:P * h + P], in0=gla_out(h),
                                                          scalar=rstd4[:, h:h + 1], in1=gg[:, P * h:P * h + P], op0=ALU.mult, op1=ALU.mult)
                last.then_inc(gated_ready, 1)

            n_d = n_d + PER_T * T

            def rotate(q3, tmp3, cs, sn, rows, n0):
                hr = ROPE // 2
                nh = q3.shape[1]
                bc = lambda v: v.unsqueeze(1).to_broadcast([rows, nh, hr])
                nc.vector.tensor_tensor(tmp3[:, :, 0:hr], q3[:, :, hr:ROPE], bc(sn[:, 0:hr]), ALU.mult).then_inc(chain_d, 1)
                nc.vector.tensor_tensor(tmp3[:, :, hr:ROPE], q3[:, :, 0:hr], bc(sn[:, hr:ROPE]), ALU.mult).then_inc(chain_d, 1)
                dve.wait_ge(chain_d, n0 + 2)
                nc.vector.tensor_tensor(q3, q3, cs.unsqueeze(1).to_broadcast([rows, nh, ROPE]), ALU.mult).then_inc(chain_d, 1)
                dve.wait_ge(chain_d, n0 + 3)
                return nc.vector.tensor_tensor(q3, q3, tmp3, ALU.add)

            def rope_queries(i, n0):
                dve.wait_ge(qp_copied, 2 * i + 2)
                q3 = q_tok.rearrange("p (h e) -> p h e", h=H)[:, :, NOPE:QK]
                rotate(q3, q_rt.rearrange("p (h e) -> p h e", h=H), rope[:, i, 0, :], rope[:, i, 1, :], P, n0).then_inc(q_roped, 1)
                return n0 + 3

            def mix(p):
                i, hp = p // 4, p % 4
                dve.wait_ge(pv_done, p + 1)
                dve.wait_ge(gt_copied, i + 1)
                nc.vector.tensor_tensor(mixT[:, hp, P * i:P * i + P], banks[:, 6, 0:P], gT(i)[:, hp, :], ALU.mult).then_inc(mixed, 1)

            dve.wait_ge(gated_T, T + 1)
            dve.wait_ge(kv_out, 32 * T + 1)
            dve.wait_ge(S_out, 32)
            n_d = rope_queries(0, n_d)
            for s in range(len(STEPS) + 5):
                if s >= 6 and s % 2 == 0:
                    mix((s - 6) // 2)
                if s < len(STEPS):
                    i, h = STEPS[s]
                    w = P * (i + 1)
                    if h == 5 and i + 1 < T:
                        n_d = rope_queries(i + 1, n_d)
                    c = s % 4
                    dve.wait_ge(sc_done, s + 1)
                    diag = score_bank(s)[:, P * i:P * i + P]
                    nc.vector.tensor_tensor(diag, diag, future[:], ALU.add).then_inc(chain_d, 1)
                    dve.wait_ge(chain_d, n_d + 1)
                    nc.vector.reduce_max(nmx[:, c:c + 1], score_bank(s)[:, 0:w], AX_X).then_inc(chain_d, 1)
                    dve.wait_ge(chain_d, n_d + 2)
                    nc.vector.tensor_scalar(nmx[:, c:c + 1], nmx[:, c:c + 1], -MLA_SCALE, None, ALU.mult).then_inc(mx_ready, 1)
                    n_d += 2
                if 1 <= s <= len(STEPS):
                    c, w1 = (s - 1) % 4, P * (STEPS[s - 1][0] + 1)
                    dve.wait_ge(p_ready, s)
                    nc.vector.reciprocal(rinv[:, c:c + 1], rsum[:, c:c + 1]).then_inc(chain_d, 1)
                    n_d += 1
                    dve.wait_ge(chain_d, n_d)
                    nc.vector.tensor_scalar(Pm[(s - 1) % 3][:, 0:w1], Pm[(s - 1) % 3][:, 0:w1], rinv[:, c:c + 1], None, ALU.mult).then_inc(pn_ready, 1)

            r8 = slice(0, NB)
            cs_s, sn_s = rope[0:NB, T, 0, :], rope[0:NB, T, 1, :]
            dve.wait_ge(p_rstd, 1)
            nc.vector.scalar_tensor_tensor(out=s_cqn, in0=zs[:, W_CQ:W_CKV], scalar=s_ss[:, 4:5], in1=g_q[r8], op0=ALU.mult, op1=ALU.mult)
            nc.vector.scalar_tensor_tensor(out=s_ckvn, in0=zs[:, W_CKV:W_KR], scalar=s_ss[:, 5:6], in1=g_kv[r8], op0=ALU.mult, op1=ALU.mult)
            nc.vector.tensor_copy(s_kr, zs[:, W_KR:W_GM]).then_inc(chain_d, 1)
            dve.wait_ge(chain_d, n_d + 1)
            rotate(s_kr.unsqueeze(1), s_kr4[:, 0:1, :], cs_s, sn_s, NB, n_d + 1).then_inc(chain_d, 1)
            n_d += 5
            dve.wait_ge(chain_d, n_d)
            nc.vector.tensor_copy(s_kr4, s_kr.unsqueeze(1).to_broadcast([NB, 4, ROPE])).then_inc(p_norm, 1)
            dve.wait_ge(p_T1, 1)
            dve.wait_ge(p_padded, 4)
            nc.vector.tensor_copy(s_cqT[:, :, 0:NB], banks[:, 0, 0:16].rearrange("p (k b) -> p k b", k=2))
            nc.vector.tensor_copy(knT, banks[:, 0, 16:24])
            nc.vector.tensor_copy(krnT, banks[:, 0, 24:32])
            nc.vector.tensor_copy(s_glT, banks[0:GR, 0, 32:40])
            nc.vector.tensor_copy(s_qgT, banks[:, 0, 96:112].rearrange("p (k b) -> p k b", k=2)).then_inc(chain_d, 1)
            nc.vector.tensor_copy(s_gmT, banks[:, 0, 64:96].rearrange("p (k b) -> p k b", k=4)).then_inc(p_T1c, 1)
            n_d += 1
            dve.wait_ge(p_q, 1)
            nc.vector.tensor_tensor(s_zg, banks[0:NB, 5, 0:256], b_gt[r8], ALU.add).then_inc(chain_d, 1)
            dve.wait_ge(chain_d, n_d + 1)
            nc.vector.scalar_tensor_tensor(out=s_zn, in0=s_zg, scalar=-1.0, in1=s_zg, op0=ALU.mult, op1=ALU.min).then_inc(p_zn, 1)
            nc.vector.tensor_scalar(s_zm, s_zg, 0.0, 1.0 / TAU, ALU.min, ALU.mult).then_inc(chain_d, 1)
            dve.wait_ge(chain_d, n_d + 2)
            dve.wait_ge(p_ln, 1)
            nc.vector.scalar_tensor_tensor(out=s_la, in0=s_zn, scalar=-1.0 / TAU, in1=s_zm, op0=ALU.mult, op1=ALU.add).then_inc(p_la, 1)
            n_d += 2
            dve.wait_ge(p_qc, 2)
            sq3 = sq.rearrange("p (h e) -> p h e", h=H)[:, :, NOPE:QK]
            rotate(sq3, sq_r.rearrange("p (h e) -> p h e", h=H), cs_s, sn_s, NB, n_d).then_inc(chain_d, 1)
            n_d += 4
            dve.wait_ge(chain_d, n_d)
            for r in range(4):
                nc.vector.tensor_copy(sq4[:, :, r, :], sq3).then_inc(p_q4, 1)
            dve.wait_ge(p_qT, 1)
            nc.vector.tensor_copy(s_ql, banks[0:NOPE, 6, 0:64].rearrange("p (h b) -> p h b", h=H)).then_inc(p_qTc, 1)
            for r in range(4):
                nc.vector.tensor_copy(qrs[32 * r:32 * r + 32, :, r, 0:H],
                                      banks[32 * r:32 * r + 32, 7, 0:64].rearrange("p (h b) -> p b h", h=H)).then_inc(p_qTc, 1)
            dve.wait_ge(p_qlat, 1)
            nc.vector.tensor_copy(qls[:, :, 0:H], banks[:, 0, 0:64].rearrange("p (h b) -> p b h", h=H)).then_inc(p_qls, 1)
            dve.wait_ge(p_init, 1)
            nc.vector.tensor_copy(m_run, banks[:, 1, 0:2]).then_inc(p_initc, 1)
            nc.vector.memset(l_run, 1.0).then_inc(p_initc, 1)
            nc.vector.tensor_copy(o_acc, banks[:, 1, 128:384].rearrange("p (f r) -> p f r", f=2)).then_inc(p_initc, 1)
            dve.wait_ge(p_T2, 1)
            nc.vector.tensor_copy(s_decT, banks[:, 0, 0:16].rearrange("p (k b) -> p k b", k=2)).then_inc(chain_d, 1)
            for hp in range(2):
                nc.vector.scalar_tensor_tensor(out=s_qz[:, hp, :, 0:NB], in0=s_qgT[:, hp, :].unsqueeze(1).to_broadcast([P, NB, NB]),
                                               scalar=GLA_SCALE, in1=own[:], op0=ALU.mult, op1=ALU.mult).then_inc(p_T2c, 1)
            n_d += 1
            dve.wait_ge(chain_d, n_d)
            dve.wait_ge(p_kv, 1)
            dve.wait_ge(p_state_in, 32)
            for b in range(NB):
                for hp in range(2):
                    c0 = 256 * (b % 2) + P * hp
                    nc.vector.scalar_tensor_tensor(out=state[:, b, hp, :], in0=state[:, b, hp, :], scalar=s_decT[:, hp, b:b + 1],
                                                   in1=banks[:, 1 + b // 2, c0:c0 + P], op0=ALU.mult, op1=ALU.add).then_inc(p_state, 1)
            dve.wait_ge(p_r4, 1)
            nc.vector.tensor_tensor(s_gg, zs[:, W_GG:W_END], g_gla[r8], ALU.mult).then_inc(chain_d, 1)
            n_d += 1
            dve.wait_ge(chain_d, n_d)
            for h in range(GH):
                nc.vector.scalar_tensor_tensor(out=s_gl[:, P * h:P * h + P], in0=banks[0:NB, 5 + h % 2, P * (h // 2):P * (h // 2) + P],
                                               scalar=s_ss[:, 4 + h:5 + h], in1=s_gg[:, P * h:P * h + P], op0=ALU.mult, op1=ALU.mult).then_inc(p_gl, 1)
            dve.wait_ge(p_T3, 1)
            nc.vector.tensor_copy(mixTs[:, 4:8, 0:NB], banks[:, 0, 0:32].rearrange("p (k b) -> p k b", k=4)).then_inc(p_T3c, 1)

            def keys_out(n, u):
                dve.wait_ge(f_T, n * 5 + 2)
                hold(dve)
                nc.vector.tensor_copy(latT[u][:, 1, :], banks[:, 1, :]).then_inc(f_Td, 1)
                dve.wait_ge(f_T, n * 5 + 4)
                hold(dve)
                nc.vector.tensor_copy(latT[u][:, 3, :], banks[:, 3, :]).then_inc(f_Td, 1)

            def running(n, u, hf, last):
                dve.wait_ge(f_sc, n + 2)
                hold(dve)
                nc.vector.reduce_max(st[:, 0:1], banks[:, 5, :], AX_X).then_inc(chain_d, 1)
                dve.wait_ge(chain_d, n * 3 + (n_d + 1))
                nc.vector.tensor_tensor(st[:, 1:2], st[:, 0:1], m_run[:, hf:hf + 1], ALU.max).then_inc(chain_d, 1)
                dve.wait_ge(chain_d, n * 3 + (n_d + 2))
                nc.vector.tensor_scalar(st[:, 2:3], st[:, 1:2], -MLA_SCALE, None, ALU.mult).then_inc(f_mx, 1)
                if not last:
                    keys_out(n + 1, 1 - u)
                dve.wait_ge(f_p, n * 2 + 3)
                nc.vector.tensor_copy(m_run[:, hf:hf + 1], st[:, 1:2])
                nc.vector.scalar_tensor_tensor(out=l_run[:, hf:hf + 1], in0=l_run[:, hf:hf + 1], scalar=st[:, 3:4], in1=st[:, 4:5],
                                               op0=ALU.mult, op1=ALU.add).then_inc(chain_d, 1)
                dve.wait_ge(f_pT, n + 2)
                nc.vector.tensor_copy(pT, banks[:, 6, :].rearrange("p (r q) -> p r q", r=4)).then_inc(f_pTc, 1)
                dve.wait_ge(f_o, n + 1)
                nc.vector.scalar_tensor_tensor(out=o_acc[:, hf, :], in0=o_acc[:, hf, :], scalar=st[:, 3:4], in1=banks[:, 7, 0:KVR],
                                               op0=ALU.mult, op1=ALU.add).then_inc(f_acc, 1)
                dve.wait_ge(f_acc, n + 2)

            dve.wait_ge(p_out, 64)
            keys_out(0, 0)
            for hf in range(2):
                with dve.Fori(4 * hf, 4 * hf + 4 - hf, 1) as j:
                    for u in range(2):
                        running(j * 2 + u, u, hf, False)
            running(NSTEPS - 2, 0, 1, False)
            running(NSTEPS - 1, 1, 1, True)
            n_d += 3 * 16
            dve.wait_ge(chain_d, n_d)
            nc.vector.reciprocal(st[:, 6:8], l_run).then_inc(chain_d, 1)
            n_d += 1
            dve.wait_ge(chain_d, n_d)
            for hf in range(2):
                nc.vector.tensor_scalar(o_n[:, hf, :], o_acc[:, hf, :], st[:, 6 + hf:7 + hf], None, ALU.mult).then_inc(f_on, 1)
            dve.wait_ge(f_oT, 1)
            nc.vector.tensor_copy(oT_lat, banks[:, 0, 0:256].rearrange("p (f q) -> p f q", f=2)).then_inc(f_oTc, 1)
            dve.wait_ge(f_v, 1)
            nc.vector.tensor_tensor(mixTs[:, 0:4, 0:NB], banks[:, 1, 0:32].rearrange("p (k b) -> p k b", k=4), s_gmT, ALU.mult).then_inc(f_mix, 1)

            dve.wait_ge(p_kv, 1)
            dve.wait_ge(ln_in, 32)
            dve.wait_ge(gate_bc, 4)

            def norm_out(t, rows, gate, bk):
                v = slice(0, rows)
                at = lambda c: t * 5 + (n_d + c)
                dve.wait_ge(y_proj, t + 2)
                nc.vector.tensor_tensor(r_t[v], banks[v, bk:bk + 2, :].rearrange("p b n -> p (b n)"), gate, ALU.mult).then_inc(y_read, 1)
                dve.wait_ge(y_read, t + 2)
                dve.wait_ge(xt_in, t * 16 + 16)
                nc.vector.scalar_tensor_tensor(out=r_t[v], in0=x_t[v], scalar=ALPHA, in1=r_t[v], op0=ALU.mult, op1=ALU.add).then_inc(chain_d, 1)
                dve.wait_ge(chain_d, at(1))
                for q in range(2):
                    nc.vector.bn_stats(bst[v, 6 * q:6 * q + 6], r_t[v, 512 * q:512 * q + 512]).then_inc(chain_d, 1)
                dve.wait_ge(chain_d, at(3))
                hold(dve)
                nc.vector.bn_aggr(bag[v], bst[v]).then_inc(y_var, 1)
                dve.wait_ge(y_rstd, t + 1)
                dve.wait_ge(y_out, t * 16 + 1)
                nc.vector.tensor_scalar(y_t[v], r_t[v], bag[v, 0:1], lr[v, 1:2], ALU.subtract, ALU.mult).then_inc(chain_d, 1)
                dve.wait_ge(chain_d, at(4))
                nc.vector.tensor_tensor(y_t[v], y_t[v], g_ln[v], ALU.mult).then_inc(chain_d, 1)
                dve.wait_ge(chain_d, at(5))
                nc.vector.tensor_tensor(y_t[v], y_t[v], b_ln[v], ALU.add).then_inc(y_ready, 1)

            with dve.Fori(0, T // 2, 1) as j:
                for u in range(2):
                    norm_out(j * 2 + u, P, gateP, 2 * u)
            norm_out(T, NB, gateS, 4)

        @block.tensor
        def _(pe):
            pe.wait_ge(ident_in, 16)
            for n in range(2 * KT):
                k, half = n // 2, n % 2
                if n < 2:
                    pe.wait_ge(x_in[half], 64)
                if n >= 4:
                    pe.wait_ge(x_copied, n - 3)
                for t in range(4):
                    last = nc.tensor.transpose(banks[:, n % 4, P * t:P * t + P],
                                               x_all[:, 4 * half + t, P * k:P * k + P], ident[:])
                last.then_inc(x_transposed, 1)
            pe.wait_ge(early_in, N_EARLY)
            for k in range(KT):
                last = nc.tensor.transpose(banks[:, 4, NB * k:NB * k + NB], x_s[:, P * k:P * k + P], ident[0:NB, 0:NB])
            last.then_inc(x_transposed, 1)
            pe.wait_ge(c_ready, 1)
            for k in range(KT):
                last = nc.tensor.transpose(banks[:, 5, 9 * k:9 * k + 9], c_act[:, P * k:P * k + P], ident[0:9, 0:9])
            last.then_inc(c_transposed, 1)
            pe.wait_ge(cT_ready, 1)
            for k in range(KT):
                pe.wait_ge(ada_in[k % NADA], 16 * (k // NADA + 1))
                for ch in range(6):
                    g = ch % 4
                    last = nc.tensor.matmul(banks[32 * g:32 * g + 32, 6 + ch // 4, :], cT[:, k, :],
                                            ada_ring[k % NADA][:, 512 * ch:512 * ch + 512],
                                            start=(k == 0), stop=(k == KT - 1))
                last.then_inc(ada_used, 1)
            pe.wait_ge(mod_ready, 2)
            for s_ in range(4):
                last = nc.tensor.transpose(banks[:, 0, P * s_:P * s_ + P], modA[:, P * s_:P * s_ + P], ident[:])
            last.then_inc(modT_done, 1)

            def chunk(c, slot, peeled):
                w = w_ring[slot]
                if peeled:
                    pe.wait_ge(h_ready, KT + 1)
                    pe.wait_ge(w_in_in[0], 16)
                if not peeled:
                    pe.wait_ge(sproj_part, c)
                for kk in range(2):
                    for g in range(4):
                        last = nc.tensor.matmul(banks[32 * g:32 * g + 32, 6, 0:CH], hsT[:, 4 * kk + g, :],
                                                w[:, 4 * kk + g, :], start=(kk == 0), stop=(kk == 1))
                last.then_inc(sproj_done, 1)
                for t in range(T):
                    if peeled:
                        if t >= 6:
                            pe.wait_ge(proj_copied, t - 5)
                    elif t < 2:
                        pe.wait_ge(proj_copied, 8 * c + t - 1)
                    elif t < 6:
                        pe.wait_ge(proj_copied, 8 * c + t - 7)
                    else:
                        pe.wait_ge(proj_copied, 8 * c + t - 5)
                    for k in range(KT):
                        last = nc.tensor.matmul(banks[:, t % 6, 0:CH], hT[:, k, P * t:P * t + P], w[:, k, :],
                                                start=(k == 0), stop=(k == KT - 1))
                    last.then_inc(proj_done, 1)
                    if t == 0:
                        pe.wait_ge(sproj_part, c + 1)
                        if not peeled:
                            pe.wait_ge(sproj_copied, c)
                        nc.tensor.matmul(banks[0:32, 7, 0:CH], fold[:], zs_part, start=True, stop=True).then_inc(sproj_done, 1)

            pe.wait_ge(const_in, N_CONST)
            chunk(0, 0, True)
            with pe.Fori(0, 2, 1) as i:
                pe.wait_ge(w_in_in[1], i * 16 + 16)
                chunk(i * 2 + 1, 1, False)
                pe.wait_ge(w_in_in[0], i * 16 + 32)
                chunk(i * 2 + 2, 0, False)
            pe.wait_ge(proj_copied, T * NCH)
            pe.wait_ge(sproj_copied, NCH)
            with pe.Fori(0, T, 1) as t:
                pe.wait_ge(normed, t + 2)
                pe.wait_ge(a_copied, t * 3 + 1)
                for q in range(2):
                    nc.tensor.transpose(banks[:, 0, P * q:P * q + P], cqn[:, P * q:P * q + P], ident[:])
                nc.tensor.transpose(banks[:, 0, 256:384], ckvn, ident[:])
                nc.tensor.transpose(banks[0:QK, 0, 384:512], kr96, ident[:]).then_inc(a_transposed, 1)
                pe.wait_ge(staged, t * 2 + 2)
                pe.wait_ge(mix_copied, t + 1)
                for q in range(4):
                    nc.tensor.transpose(banks[:, 1, P * q:P * q + P], qk_st[:, P * q:P * q + P], ident[:])
                nc.tensor.transpose(banks[0:GR, 2, 0:P], gl_st, ident[:]).then_inc(qk_transposed, 1)
                pe.wait_ge(glT_copied, t + 1)
                nc.tensor.matmul(banks[:, 2, 256:512], glT, w_gu[:], start=True, stop=True).then_inc(gate_done, 1)
                pe.wait_ge(a_copied, t * 3 + 4)
                for h in range(H):
                    nc.tensor.matmul(banks[0:NOPE, 3 + h // 4, P * (h % 4):P * (h % 4) + P], w_uk[:, NOPE * h:NOPE * h + NOPE], ckvT,
                                     start=True, stop=True)
                nc.tensor.matmul(banks[:, 5, :], ckvT, w_uv[:], start=True, stop=True).then_inc(kv_done, 1)
                pe.wait_ge(la_ready, t + 1)
                for q in range(2):
                    nc.tensor.matmul(banks[:, 6, P * q:P * q + P], la[:, P * q:P * q + P], upto[:], start=True, stop=True)
                nc.tensor.matmul(banks[:, 6, 256:512], after[:], la, start=True, stop=True).then_inc(cum_done, 1)
                pe.wait_ge(qkT_copied, t + 1)
                pe.wait_ge(k_copied, t * 2 + 2)
                for n in range(LEVELS + 1):
                    if n > 0:
                        pe.wait_ge(x_ready, t * LEVELS + n)
                    if n == 1:
                        pe.wait_ge(v_copied, t + 1)
                    if n >= 2:
                        pe.wait_ge(att_copied, t * (LEVELS + 1) + n - 1)
                    for h in range(GH):
                        rows = slice(64 * (h % 2), 64 * (h % 2) + 64)
                        bk = (3, 4)[h % 2] if n % 2 == 0 else (5, 7)[h % 2]
                        if n == 0:
                            left, right = qkT[rows, 2 + h // 2, :], qkT[rows, h // 2, :]
                        else:
                            left = right = xl[(n - 1) % 2][rows, P * (h // 2):P * (h // 2) + P]
                        last = nc.tensor.matmul(banks[:, bk, P * (h // 2):P * (h // 2) + P], left, right, start=True, stop=True)
                    last.then_inc(att_done, 1)
                pe.wait_ge(att_copied, t * (LEVELS + 1) + LEVELS + 1)
                pe.wait_ge(qb_ready, t + 1)
                pe.wait_ge(S_ready, t * 2 + 1)
                for h in range(GH):
                    rows = slice(64 * (h % 2), 64 * (h % 2) + 64)
                    nc.tensor.matmul(gla_out(h), attm[:, h % 2, h // 2, :], qk_st[:, 512 + P * h:512 + P * h + P],
                                     start=True, stop=False)
                    last = nc.tensor.matmul(gla_out(h), qb[rows, P * (h // 2):P * (h // 2) + P], S[rows, h // 2, :],
                                            start=False, stop=True)
                last.then_inc(o_done, 1)
                pe.wait_ge(kdec_ready, t + 1)
                for h in range(GH):
                    rows = slice(64 * (h % 2), 64 * (h % 2) + 64)
                    last = nc.tensor.matmul(banks[rows, 5, P * (h // 2):P * (h // 2) + P], kdec[:, 64 * h:64 * h + 64],
                                            qk_st[:, 512 + P * h:512 + P * h + P], start=True, stop=True)
                last.then_inc(state_done, 1)
                pe.wait_ge(gated_ready, t + 2)
                for h in range(GH):
                    last = nc.tensor.transpose(banks[:, 2, P * h:P * h + P], gated[:, P * h:P * h + P], ident[:])
                last.then_inc(gated_T, 1)

            pe.wait_ge(mix_copied, T + 1)
            pe.wait_ge(S_ready, 2 * T + 1)

            def q_proj(i, q):
                if i > 0 or q > 0:
                    pe.wait_ge(qp_copied, 2 * i + q)
                if i > 0:
                    pe.wait_ge(qt_copied, 2 * i)
                    pe.wait_ge(gt_copied, i)
                for k in range(2):
                    last = nc.tensor.matmul(banks[:, 7, 0:384], z[:, i, P * k:P * k + P], w_uq[:, k, 384 * q:384 * q + 384],
                                            start=(k == 0), stop=(k == 1))
                last.then_inc(qp_done, 1)

            def q_transpose(i, q):
                pe.wait_ge(q_roped, i + 1)
                if q > 0:
                    pe.wait_ge(qt_copied, 2 * i + q)
                for h in range(4):
                    last = nc.tensor.transpose(banks[0:QK, 7, P * h:P * h + P], q_tok[:, QK * (4 * q + h):QK * (4 * q + h) + QK], ident[:])
                last.then_inc(qt_done, 1)

            def products(p):
                i = STEPS[2 * p][0]
                hp = p % 4
                pe.wait_ge(pt_copied, groups(2 * p + 2))
                if p > 0:
                    pe.wait_ge(mixed, p)
                for j in range(i + 1):
                    for par in range(2):
                        last = nc.tensor.matmul(banks[64 * par:64 * par + 64, 6, 0:P], V(j, 2 * hp + par), PTb[(2 * p + par) % 3][:, j, :],
                                                start=(j == 0), stop=(j == i))
                last.then_inc(pv_done, 1)

            for q in range(2):
                q_proj(0, q)
            for q in range(2):
                q_transpose(0, q)
            for s in range(len(STEPS) + LAG):
                if s < len(STEPS):
                    i, h = STEPS[s]
                    w = P * (i + 1)
                    if h == 2:
                        pe.wait_ge(qt_copied, 2 * i + 2)
                        for q in range(4):
                            last = nc.tensor.transpose(banks[:, 7, P * q:P * q + P], z[:, i, W_GM + P * q:W_GM + P * q + P], ident[:])
                        last.then_inc(gt_done, 1)
                    pe.wait_ge(qt_copied, 2 * i + 2)
                    if s >= 2:
                        pe.wait_ge(p_ready, s - 1)
                    for n0 in range(0, w, 512):
                        n1 = min(w, n0 + 512)
                        last = nc.tensor.matmul(score_bank(s)[:, n0:n1], QTb[i % 2][:, h, :], KTh[:, h, n0:n1], start=True, stop=True)
                    last.then_inc(sc_done, 1)
                if s >= LAG:
                    r = s - LAG
                    i1 = STEPS[r][0]
                    pe.wait_ge(pn_ready, r + 1)
                    for g in range(i1 // 4 + 1):
                        k0 = groups(r) + g
                        if k0 >= 2:
                            pe.wait_ge(pt_copied, k0 - 1)
                        for j in range(4 * g, min(4 * g + 4, i1 + 1)):
                            last = nc.tensor.transpose(banks[:, 4 + k0 % 2, P * (j % 4):P * (j % 4) + P], Pm[r % 3][:, P * j:P * j + P], ident[:])
                        last.then_inc(pt_done, 1)
                    if r % 2 == 0 and r >= 2:
                        products((r - 2) // 2)
                if s < len(STEPS) and i + 1 < T:
                    if h in (3, 4):
                        q_proj(i + 1, h - 3)
                    if h in (6, 7):
                        q_transpose(i + 1, h - 6)
            products(len(STEPS) // 2 - 1)

            pe.wait_ge(p_norm, 1)
            pe.wait_ge(mixed, len(STEPS) // 2)
            i8 = ident[0:NB, 0:NB]
            for q in range(2):
                nc.tensor.transpose(banks[:, 0, NB * q:NB * q + NB], s_cqn[:, P * q:P * q + P], i8)
            nc.tensor.transpose(banks[:, 0, 16:24], s_ckvn, i8)
            nc.tensor.transpose(banks[:, 0, 24:32], s_kr4.rearrange("p a e -> p (a e)"), i8)
            nc.tensor.transpose(banks[0:GR, 0, 32:40], zs[:, W_GL:W_GG], i8)
            for q in range(4):
                nc.tensor.transpose(banks[:, 0, 64 + NB * q:64 + NB * q + NB], zs[:, W_GM + P * q:W_GM + P * q + P], i8)
            for q in range(2):
                nc.tensor.transpose(banks[:, 0, 96 + NB * q:96 + NB * q + NB], zs[:, W_GQ + P * q:W_GQ + P * q + P], i8)
            for h in range(H):
                last = nc.tensor.transpose(banks[0:NOPE, 1 + h // 4, P * (h % 4):P * (h % 4) + P], w_uk[:, NOPE * h:NOPE * h + NOPE], ident[:])
            last.then_inc(p_T1, 1)
            pe.wait_ge(p_T1c, 1)
            for q in range(2):
                for k in range(2):
                    nc.tensor.matmul(banks[0:32, 3 + q, 0:384], s_cqT[:, k, :], w_uq[:, k, 384 * q:384 * q + 384], start=(k == 0), stop=(k == 1))
            nc.tensor.matmul(banks[0:NB, 5, 0:256], s_glT, w_gu[:], start=True, stop=True).then_inc(p_q, 1)
            pe.wait_ge(p_q4, 4)
            for h in range(H):
                nc.tensor.transpose(banks[0:NOPE, 6, NB * h:NB * h + NB], sq[:, QK * h:QK * h + NOPE], i8)
            for h in range(H):
                last = nc.tensor.transpose(banks[:, 7, NB * h:NB * h + NB], sq4[:, h, :, :].rearrange("p a e -> p (a e)"), i8)
            last.then_inc(p_qT, 1)
            pe.wait_ge(p_qTc, 5)
            pe.wait_ge(p_wTc, 2)
            for h in range(H):
                last = nc.tensor.matmul(banks[:, 0, NB * h:NB * h + NB], w_ukT[:, h, :], s_ql[:, h, :], start=True, stop=True)
            last.then_inc(p_qlat, 1)
            pe.wait_ge(p_qls, 1)
            pe.wait_ge(p_tabs, 32)
            for hf in range(2):
                for bb in range(HALF):
                    b = HALF * hf + bb
                    dst = banks[32 * bb:32 * bb + 32, 1, hf:hf + 1]
                    nc.tensor.matmul(dst, qls[:, b, :], knT[:, b:b + 1], start=True, stop=False)
                    nc.tensor.matmul(dst, qrs[:, b, 0, :], krnT[:, b:b + 1], start=False, stop=True)
            for hf in range(2):
                last = nc.tensor.matmul(banks[:, 1, P + P * hf:2 * P + P * hf], spread[:, hf, :], s_ckvn, start=True, stop=True)
            last.then_inc(p_init, 1)
            pe.wait_ge(p_dec, 1)
            for q in range(2):
                last = nc.tensor.transpose(banks[:, 0, NB * q:NB * q + NB], s_la[:, P * q:P * q + P], i8)
            last.then_inc(p_T2, 1)
            pe.wait_ge(p_kz, 1)
            pe.wait_ge(p_initc, 3)
            pe.wait_ge(p_qc, 2)
            for b in range(NB):
                for h in range(GH):
                    rows = slice(64 * (h % 2), 64 * (h % 2) + 64)
                    c0 = 256 * (b % 2) + P * (h // 2)
                    last = nc.tensor.matmul(banks[rows, 1 + b // 2, c0:c0 + P], s_kz[:, b, 64 * h:64 * h + 64],
                                            zs[:, W_GV + P * h:W_GV + P * h + P], start=True, stop=True)
            last.then_inc(p_kv, 1)
            pe.wait_ge(p_T2c, 2)
            pe.wait_ge(p_state, 2 * NB)
            pe.wait_ge(p_zn, 1)
            for par in range(2):
                rows = slice(64 * par, 64 * par + 64)
                for hp in range(2):
                    for b in range(NB):
                        last = nc.tensor.matmul(banks[0:32, 5 + par, P * hp:P * hp + P], s_qz[rows, hp, b, :], state[rows, b, hp, :],
                                                start=(b == 0), stop=(b == NB - 1))
            last.then_inc(p_o, 1)
            pe.wait_ge(p_gl, 4)
            for q in range(4):
                last = nc.tensor.transpose(banks[:, 0, NB * q:NB * q + NB], s_gl[:, P * q:P * q + P], i8)
            last.then_inc(p_T3, 1)
            pe.wait_ge(p_T3c, 1)
            def rows_transposed(n, v):
                for bb in range(HALF):
                    if bb % 2 == 0:
                        pe.wait_ge(f_Ta, n * 3 + 1)
                    else:
                        pe.wait_ge(f_Td, n * 2 + 1)
                    for r in range(ROWS):
                        last = nc.tensor.transpose(banks[:, bb, P * r:P * r + P], lat[v][:, bb, KVR * r:KVR * r + KVR], ident[:])
                    last.then_inc(f_T, 1)
                for bb in range(HALF):
                    last = nc.tensor.transpose(banks[:, 4, P * bb:P * bb + P], kro[v][:, bb, :], ident[:])
                last.then_inc(f_T, 1)

            def scores(n, u, hf):
                pe.wait_ge(f_Ta, n * 3 + 4)
                pe.wait_ge(f_Td, n * 2 + 3)
                pe.wait_ge(f_p, n * 2 + 1)
                for bb in range(HALF):
                    nc.tensor.matmul(banks[32 * bb:32 * bb + 32, 5, :], qls[:, HALF * hf + bb, :], latT[u][:, bb, :], start=True, stop=False)
                for r in range(ROWS):
                    for bb in range(HALF):
                        last = nc.tensor.matmul(banks[32 * bb:32 * bb + 32, 5, P * r:P * r + P], qrs[:, HALF * hf + bb, r, :], kroT[u][:, bb, :],
                                                start=False, stop=(r == ROWS - 1))
                last.then_inc(f_sc, 1)

            def weighted(n, v):
                pe.wait_ge(f_p, n * 2 + 3)
                pe.wait_ge(f_pTc, n + 1)
                for r in range(ROWS):
                    last = nc.tensor.transpose(banks[:, 6, P * r:P * r + P], sc[:, P * r:P * r + P], ident[:])
                last.then_inc(f_pT, 1)
                pe.wait_ge(f_pTc, n + 2)
                pe.wait_ge(f_acc, n + 1)
                for r in range(ROWS):
                    for bb in range(HALF):
                        last = nc.tensor.matmul(banks[32 * bb:32 * bb + 32, 7, 0:KVR], pT[:, r, 32 * bb:32 * bb + 32],
                                                lat[v][:, bb, KVR * r:KVR * r + KVR], start=(r == 0), stop=(r == ROWS - 1))
                last.then_inc(f_o, 1)

            ARRIVED = 16 * 2 * HALF
            pe.wait_ge(f_in[0], ARRIVED)
            rows_transposed(0, 0)
            for hf in range(2):
                with pe.Fori(2 * hf, 2 * hf + 2 - hf, 1) as j:
                    for v in range(SLOTS):
                        n = j * SLOTS + v
                        scores(n, v % 2, hf)
                        pe.wait_ge(f_in[(v + 1) % SLOTS], j * ARRIVED + ARRIVED * (1 + (v + 1) // SLOTS))
                        rows_transposed(n + 1, (v + 1) % SLOTS)
                        weighted(n, v)
            for v in range(SLOTS):
                n = NSTEPS - SLOTS + v
                scores(n, v % 2, 1)
                if v + 1 < SLOTS:
                    pe.wait_ge(f_in[v + 1], ARRIVED * (NSTEPS // SLOTS))
                    rows_transposed(n + 1, v + 1)
                weighted(n, v)
            pe.wait_ge(f_on, 2)
            for hf in range(2):
                last = nc.tensor.transpose(banks[:, 0, P * hf:P * hf + P], o_n[:, hf, :], ident[:])
            last.then_inc(f_oT, 1)
            pe.wait_ge(f_oTc, 1)
            for h in range(H):
                heads = oT_lat.rearrange("p f (b q) -> p f b q", b=HALF)[:, :, :, h].rearrange("p f b -> p (f b)")
                last = nc.tensor.matmul(banks[64 * (h % 2):64 * (h % 2) + 64, 1, NB * (h // 2):NB * (h // 2) + NB],
                                        w_uv[:, VD * h:VD * h + VD], heads, start=True, stop=True)
            last.then_inc(f_v, 1)

            for q in range(2):
                nc.tensor.matmul(banks[:, 2 + q, :], pick[:, q, 0:P], modB[:], start=True, stop=True)
                last = nc.tensor.matmul(banks[0:32, 4 + q, :], pick[:, q, P:P + 32], modB[:], start=True, stop=True)
            last.then_inc(gate_b, 1)
            pe.wait_ge(w_out_in, 16)
            pe.wait_ge(f_mix, 1)
            pe.wait_ge(gate_bc, 4)
            def project_out(t, u, first):
                pe.wait_ge(m_staged, t + 1)
                if not first:
                    pe.wait_ge(y_read, t)
                for q in range(2):
                    for k in range(KT):
                        last = nc.tensor.matmul(banks[:, 2 * u + q, :], mst[u][:, k, :], w_out[:, k, 512 * q:512 * q + 512],
                                                start=(k == 0), stop=(k == KT - 1))
                last.then_inc(y_proj, 1)

            for t in range(2):
                project_out(t, t, True)
            with pe.Fori(1, T // 2, 1) as j:
                for u in range(2):
                    project_out(j * 2 + u, u, False)
            for q in range(2):
                for k in range(KT):
                    last = nc.tensor.matmul(banks[0:32, 4 + q, :], mixTs[:, k, :], w_out[:, k, 512 * q:512 * q + 512], start=(k == 0), stop=(k == KT - 1))
            last.then_inc(y_proj, 1)


_OUTS = [
    ("y_prompt", (1, SEQ, D)), ("y_sample", (NB, 1, D)), ("kv_prompt", (1, 1, SEQ, KVR)),
    ("kr_prompt", (1, 1, SEQ, ROPE)), ("st_prompt", (1, 1, GH, DK, DV)), ("kv_sample", (1, NB, 1, KVR)),
    ("kr_sample", (1, NB, 1, ROPE)), ("st_sample", (1, NB, GH, DK, DV)),
]
_INS = ["x_prompt", "x_sample", "cache_kv_latent", "cache_k_rope", "state_gla", "page_table", "c_prompt",
        "c_sample", "w_ada", "b_ada", "w_in", "q_norm_g", "w_uq", "kv_norm_g", "w_uk", "w_uv", "w_gate_up",
        "b_gate", "gla_norm_g", "w_out", "ln_g", "ln_b"]


def kernel(**inputs):
    import numpy as _np
    import concourse.bacc as _bacc
    from concourse.bass_utils import run_bass_kernel_spmd as _run

    nc = _bacc.Bacc("TRN2", target_bir_lowering=False, num_devices=1,
                    dynamic_dma_scratch_size=8192)
    arrays, args, outs = {}, {}, {}
    given = {n: _np.ascontiguousarray(inputs[n]) for n in _INS}
    given.update({"c_" + n: _np.ascontiguousarray(v) for n, v in shape_constants().items()})
    lead = {"x_prompt", "cache_kv_latent", "cache_k_rope", "state_gla", "w_ada", "w_in", "w_uq", "w_uk", "w_uv",
            "w_gate_up", "gla_norm_g", "w_out"}
    for name, v in given.items():
        arrays["in_" + name] = v
        ap = nc.dram_tensor("in_" + name, v.shape, mybir.dt.from_np(v.dtype), kind="ExternalInput").ap()
        if name in lead:
            ap = ap[0]
        elif name == "x_sample":
            ap = ap.rearrange("b s d -> (b s) d")
        args[name] = ap
    for name, shape in _OUTS:
        outs[name] = nc.dram_tensor("out_" + name, shape, F32, kind="ExternalOutput").ap()
    hybrid_step(nc, args, outs)
    r = _run(nc, [arrays], core_ids=[0])
    return tuple(r.results[0]["out_" + name] for name, _ in _OUTS)
```

```python
from contextlib import ExitStack

import numpy as np

import concourse.bass as bass
from concourse import mybir

F32 = mybir.dt.float32
F32R = mybir.dt.float32r
I32 = mybir.dt.int32
U8 = mybir.dt.uint8
ALU = mybir.AluOpType
ACT = mybir.ActivationFunctionType
AX_X = mybir.AxisListType.X

P = 128
D = 1024
SEQ = 1024
NB = 8
PAST, PAGE = 4096, 128
H, NOPE, ROPE, VD = 8, 64, 32, 64
QK = NOPE + ROPE
QR, KVR = 256, 128
GH, DK, DV, GR = 4, 64, 128, 16
W_CQ, W_CKV, W_KR, W_GM, W_GQ, W_GK, W_GV, W_GL, W_GG, W_END = (
    int(v) for v in np.cumsum([0, QR, KVR, ROPE, H * VD, GH * DK, GH * DK, GH * DV, GR, GH * DV]))
EPS = 1e-6
ALPHA = 2.0 ** 0.25
MLA_SCALE = float(QK) ** -0.5
GLA_SCALE = float(DK) ** -0.5
TAU = 16.0
T = SEQ // P
KT = D // P
CH = 248
NCH = W_END // CH
LEVELS = 7
WIDE = 2
ROWS = 4
SUBS = PAGE // ROWS
SLOTS = 4
HALF = 4
NSTEP = PAST // (P * ROWS)
CN = 8432
NEG = -1.0e30
LN_EXP_SET = 6


def shape_constants():
    r = np.arange(P)
    c = {}
    c["ident"] = np.eye(P, dtype=np.float32)
    c["upto"] = (r[:, None] <= r[None, :]).astype(np.float32)
    c["after"] = (r[:, None] > r[None, :]).astype(np.float32)
    c["future"] = np.where(r[None, :] > r[:, None], NEG, 0).astype(np.float32)
    m = np.zeros((P, LEVELS, P), np.float32)
    for lv in range(LEVELS):
        s = P >> (lv + 1)
        same = (r[:, None] // (2 * s)) == (r[None, :] // (2 * s))
        m[:, lv] = same & ((r[:, None] // s) % 2 == 0) & ((r[None, :] // s) % 2 == 1)
    low = np.stack([m[32 * g:32 * g + 32, WIDE:, 32 * g:32 * g + 32] for g in range(4)]).reshape(P, -1)
    c["pairs"] = np.ascontiguousarray(np.concatenate([m[:, :WIDE].reshape(P, -1), low], 1))
    c["near"] = (r[:, None] % 32 == r[None, :32]).astype(np.float32)
    inv = (np.float32(10000.0) ** (-np.arange(0, ROPE, 2, dtype=np.float32) / np.float32(ROPE))).astype(np.float32)
    pos = np.concatenate([np.arange(SEQ), np.full(P, PAST)]).astype(np.float32)
    ang = (pos[:, None] * inv[None, :]).astype(np.float32)
    cos, sin = np.cos(ang), np.sin(ang)
    t = np.stack([np.concatenate([cos, cos], 1), np.concatenate([-sin, sin], 1)], 1)
    c["rope"] = np.ascontiguousarray(
        t.reshape(T + 1, P, 2, ROPE).transpose(1, 0, 2, 3)).astype(np.float32)
    fold = np.zeros((P, 32), np.float32)
    spread = np.zeros((NB, 2, P), np.float32)
    for g in range(4):
        for b in range(NB):
            fold[32 * g + b, b] = 1
        for hf in range(2):
            spread[HALF * hf + g, hf, 32 * g:32 * g + 32] = 1
    c["fold"] = fold
    c["spread"] = spread
    g1 = np.zeros((64, 2, P + 32), np.float32)
    for ch in range(2):
        g1[32 * ch + NB, ch, :P] = 1
        for b in range(NB):
            g1[32 * ch + b, ch, P + b] = 1
    c["pick"] = g1
    own = np.zeros((P, NB, NB), np.float32)
    own[:, np.arange(NB), np.arange(NB)] = 1
    c["own"] = own
    own8 = np.zeros((NB, NB), np.float32)
    own8[np.arange(NB), np.arange(NB)] = 1
    c["own8"] = own8
    c["sub"] = (np.arange(P) % SUBS).astype(np.float32)[:, None]
    return c


def hybrid_step(nc, a, o):
    with ExitStack() as ctx:
        def sb(name, shape, dt=F32):
            return ctx.enter_context(nc.sbuf_tensor("s_" + name, shape, dt))

        def sem(name):
            return ctx.enter_context(nc.semaphore(name))

        z = sb("z", [P, T, W_END])

        def in_turn(*uses):
            views = []
            for name, shape, dt in uses[:-1]:
                with nc.sbuf_tensor("s_" + name, shape, dt) as v:
                    views.append(v)
            return views + [sb(*uses[-1])]

        x_buf, h_hi, kt_buf = in_turn(("x", [P, KT * SEQ], F32), ("h_hi", [P, KT, SEQ], F32R), ("kt", [P, H * SEQ], F32))
        hT, h_lo, act_buf = in_turn(("hT", [P, KT, SEQ], F32), ("h_lo", [P, KT, SEQ], F32R), ("mixT", [P, KT, SEQ], F32))
        C_parts, C = in_turn(("w_parts", [P, CN], F32R), ("temps", [P, CN], F32))
        zs = sb("zs", [NB, W_END])
        x_all = x_buf[:].rearrange("p (t d) -> p t d", t=T)
        KTh = kt_buf[0:QK, :].rearrange("p (h s) -> p h s", h=H)
        w_out = kt_buf[:].rearrange("p (k n) -> p k n", k=KT)
        mixT = act_buf

        ident = sb("ident", [P, P])
        upto = sb("upto", [P, P])
        after = sb("after", [P, P])
        future = sb("future", [P, P])
        N_PAIRS = WIDE * P + (LEVELS - WIDE) * 32
        masks = sb("pairs", [P, N_PAIRS], U8)
        pairs = masks[:, 0:WIDE * P].rearrange("p (l i) -> p l i", l=WIDE)
        pairs_low = masks[:, WIDE * P:].rearrange("p (l i) -> p l i", l=LEVELS - WIDE)
        near = sb("near", [P, 32])
        rope = sb("rope", [P, T + 1, 2, ROPE])
        fold = sb("fold", [P, 32])
        own = sb("own", [P, NB, NB])
        own8 = sb("own8", [NB, NB])
        sub = sb("sub", [P, 1])
        w_uq = sb("w_uq", [P, 2, H * QK])
        w_uk = sb("w_uk", [P, H * NOPE])
        w_uv = sb("w_uv", [P, H * VD])
        w_gu = sb("w_gu", [GR, GH * DK])
        g_q = sb("g_q", [P, QR])
        g_kv = sb("g_kv", [P, KVR])
        b_gt = sb("b_gt", [P, GH * DK])
        g_gla = sb("g_gla", [P, GH * DV])
        modB = sb("modB", [64, 512])
        hsT = sb("hsT", [P, KT, 32])
        eps_t = sb("eps_t", [P, 1])
        mixTs = hsT
        banks = ctx.enter_context(nc.psum_tensor("banks", [P, 8, 512], F32))

        taken = [0]

        def carve(n, *dims, rows=P, at=None, region=None):
            region = C if region is None else region
            start = taken[0] if at is None else at
            taken[0] = start + n
            v = region[0:rows, start:start + n]
            if len(dims) > 1:
                names = "abcd"[:len(dims)]
                v = v.rearrange(f"p ({' '.join(names)}) -> p {' '.join(names)}",
                                **{k: d for k, d in zip(names, dims)})
            return v

        z_flat = z[:].rearrange("p t n -> p (t n)")
        NADA = 6
        ada_ring = [z_flat[:, i * 3 * D:(i + 1) * 3 * D] for i in range(NADA)]
        taken[0] = 0
        c_in = carve(D, rows=9)
        c_act = carve(D, rows=9)
        cT = carve(KT * 32, KT, 32)
        x_s = carve(D, rows=NB)
        xsT = carve(KT * NB, KT, NB)
        b_adaA = carve(512)
        b_adaB = carve(512)
        modA = carve(512)
        shT = carve(KT)
        scT = carve(KT)
        shsT = carve(KT * NB, KT, NB)
        scsT = carve(KT * NB, KT, NB)
        hs_tmp = carve(KT * NB, KT, NB)
        pairs_f = carve(N_PAIRS)
        assert taken[0] <= CN

        assert taken[0] <= CN - KT * CH
        w_hi = [carve(KT * CH, KT, CH, at=i * KT * CH, region=C_parts) for i in (0, 2)]
        w_raw, w_lo = ([carve(KT * CH, KT, CH, at=i, region=reg) for i in (CN - KT * CH, KT * CH)]
                       for reg in (C, C_parts))
        zs_part = carve(CH, at=6100)

        taken[0] = 0
        junk = carve(512)
        ss = carve(2)
        lnss = carve(2)
        rstd = carve(2)
        cqn = carve(QR)
        ckvn = carve(KVR)
        kr96 = carve(QK)
        rtmp = carve(ROPE)
        ckvT = carve(P)
        qk_st = carve(512)
        v_st = carve(512)
        gl_st = carve(GR)
        glT = carve(P, rows=GR)
        qkT = carve(4 * P, 4, P)
        zg = carve(256)
        zneg = carve(256)
        zmin = carve(256)
        la = carve(256)
        bT = carve(256)
        eb = carve(256)
        qb = carve(256)
        esuf = carve(256)
        kdec = carve(256)
        dl = [carve(256) for _ in range(2)]
        xl = [carve(256) for _ in range(2)]
        attm = carve(512, 2, 2, P)
        attn = carve(4 * 32, 2, 2, 32)
        gated = carve(512)
        gg = carve(512)
        ss4 = carve(4)
        rstd4 = carve(4)
        S = carve(2 * DV, 2, DV)
        assert taken[0] <= CN, taken[0]

        taken[0] = 0
        q_tok = carve(H * QK)
        q_rt = carve(H * ROPE)
        QTb = [carve(H * P, H, P, rows=QK) for _ in range(2)]
        Pm = [carve(SEQ) for _ in range(2)] + [z[:, 0, W_GV:W_GV + SEQ]]
        PTb = [carve(T * P, T, P) for _ in range(3)]
        nmx = carve(4)
        rsum = carve(4)
        rinv = carve(4)
        assert taken[0] <= CN, taken[0]

        zr = z_flat
        taken[0] = 0
        LAT = HALF * ROWS * KVR
        RO = HALF * ROWS * ROPE
        lat = [carve(LAT, HALF, ROWS * KVR, region=zr) for _ in range(SLOTS)]
        kro = [carve(RO, HALF, ROWS * ROPE, region=zr) for _ in range(SLOTS)]
        sc = carve(512, region=zr)
        pT = carve(512, 4, P, region=zr)
        o_acc = carve(2 * KVR, 2, KVR, region=zr)
        m_run = carve(2, region=zr)
        l_run = carve(2, region=zr)
        st = carve(8, region=zr)
        qls = carve(NB * 32, NB, 32, region=zr)
        qrs = carve(NB * 4 * 32, NB, 4, 32, region=zr)
        knT = carve(NB, region=zr)
        krnT = carve(NB, region=zr)
        sq = carve(H * QK, region=zr, rows=NB)
        sq_r = carve(H * ROPE, region=zr, rows=NB)
        s_cqn = carve(QR, region=zr, rows=NB)
        s_ckvn = carve(KVR, region=zr, rows=NB)
        s_kr = carve(ROPE, region=zr, rows=NB)
        s_kr4 = carve(4 * ROPE, 4, ROPE, region=zr, rows=NB)
        s_cqT = carve(2 * 32, 2, 32, region=zr)
        s_ql = carve(H * NB, H, NB, region=zr, rows=NOPE)
        w_ukT = carve(H * P, H, P, region=zr, rows=NOPE)
        s_ss = carve(8, region=zr, rows=NB)
        s_zg = carve(256, region=zr, rows=NB)
        s_zn = carve(256, region=zr, rows=NB)
        s_zm = carve(256, region=zr, rows=NB)
        s_la = carve(256, region=zr, rows=NB)
        s_glT = carve(NB, region=zr, rows=GR)
        s_decT = carve(2 * NB, 2, NB, region=zr)
        s_qgT = carve(2 * NB, 2, NB, region=zr)
        s_gg = carve(512, region=zr, rows=NB)
        s_qz = carve(2 * NB * 32, 2, NB, 32, region=zr)
        oT_lat = carve(2 * P, 2, P, region=zr)
        o_n = carve(2 * KVR, 2, KVR, region=zr)
        spread = carve(2 * P, 2, P, region=zr, rows=NB)
        pick = carve(2 * (P + 32), 2, P + 32, region=zr, rows=64)
        s_gmT = carve(4 * NB, 4, NB, region=zr)
        pt_i = ctx.enter_context(nc.sbuf_tensor("s_pt", [P, NB * NSTEP], I32))
        idx = ctx.enter_context(nc.sbuf_tensor("s_idx", [P, NB * NSTEP], I32))
        idx_st = [sb(f"idx_st{i}", [P, HALF], I32) for i in range(SLOTS)]
        mst = [carve(KT * P, KT, P, region=zr)]
        assert taken[0] <= T * W_END

        taken[0] = 0
        state = carve(NB * 2 * DV, NB, 2, DV)
        s_kz = carve(NB * 256, NB, 256, rows=NB)
        latT = [carve(LAT, HALF, ROWS * KVR)]
        kroT = [carve(RO, HALF, ROWS * ROPE)]
        sq4 = carve(H * 4 * ROPE, H, 4, ROPE, rows=NB)
        s_junk = carve(512, rows=NB)
        s_gl = s_junk
        assert taken[0] <= CN

        taken[0] = 0
        latT.append(carve(LAT, HALF, ROWS * KVR))
        kroT.append(carve(RO, HALF, ROWS * ROPE))

        taken[0] = 0
        mst.append(carve(KT * P, KT, P))
        r_t = carve(D)
        y_t = carve(D)
        x_t = carve(D)
        g_ln = carve(D)
        b_ln = carve(D)
        gateP = carve(D)
        gateS = carve(D, rows=NB)
        bst = carve(12)
        bag = carve(2)
        lr = carve(2)
        assert taken[0] <= CN, taken[0]

        const_in = sem("const_in")
        held = sem("held")
        x_in = [sem(f"x_in{i}") for i in range(2)]
        ada_in = [sem(f"ada_in{i}") for i in range(6)]
        w_in_in = [sem(f"w_in_in{i}") for i in range(2)]
        padded = sem("padded")
        masks_ready = sem("masks_ready")
        chain_d = sem("chain_d")
        chain_a = sem("chain_a")
        x_transposed = sem("x_transposed")
        x_copied = sem("x_copied")
        c_transposed = sem("c_transposed")
        ada_used = sem("ada_used")
        sproj_part = sem("sproj_part")
        mod_ready = sem("mod_ready")
        modT_done = sem("modT_done")
        hs_ready = sem("hs_ready")
        hf_ready = sem("hf_ready")
        hf2_ready = sem("hf2_ready")
        h_hi_ready = sem("h_hi_ready")
        h_ready = sem("h_ready")
        w_hi_ready = sem("w_hi_ready")
        w_ready = sem("w_ready")
        proj_done = sem("proj_done")
        proj_copied = sem("proj_copied")
        sproj_done = sem("sproj_done")
        sproj_copied = sem("sproj_copied")
        silu_done = sem("silu_done")
        staged = sem("staged")
        vg_ready = sem("vg_ready")
        rstd_ready = sem("rstd_ready")
        normed = sem("normed")
        kv_out = sem("kv_out")
        a_transposed = sem("a_transposed")
        a_copied = sem("a_copied")
        qk_transposed = sem("qk_transposed")
        glT_copied = sem("glT_copied")
        qkT_copied = sem("qkT_copied")
        gate_done = sem("gate_done")
        gate_copied = sem("gate_copied")
        zneg_ready = sem("zneg_ready")
        lnz_ready = sem("lnz_ready")
        la_ready = sem("la_ready")
        kv_done = sem("kv_done")
        k_done = sem("k_done")
        k_copied = sem("k_copied")
        v_copied = sem("v_copied")
        cum_done = sem("cum_done")
        bT_copied = sem("bT_copied")
        e_ready = sem("e_ready")
        kdec_ready = sem("kdec_ready")
        qb_ready = sem("qb_ready")
        d_ready = sem("d_ready")
        el_ready = sem("el_ready")
        x_ready = sem("x_ready")
        att_done = sem("att_done")
        att_copied = sem("att_copied")
        blocks_in = sem("blocks_in")
        o_done = sem("o_done")
        state_done = sem("state_done")
        S_ready = sem("S_ready")
        r4_ready = sem("r4_ready")
        gated_ready = sem("gated_ready")
        gated_T = sem("gated_T")
        mix_copied = sem("mix_copied")
        S_out = sem("S_out")
        qp_done = sem("qp_done")
        qp_copied = sem("qp_copied")
        q_roped = sem("q_roped")
        rope_step = sem("rope_step")
        qt_done = sem("qt_done")
        qt_copied = sem("qt_copied")
        gt_done = sem("gt_done")
        gt_copied = sem("gt_copied")
        sc_done = sem("sc_done")
        mx_ready = sem("mx_ready")
        p_ready = sem("p_ready")
        pn_ready = sem("pn_ready")
        pt_done = sem("pt_done")
        pt_copied = sem("pt_copied")
        pv_done = sem("pv_done")
        mixed = sem("mixed")
        def samp(name):
            return sem("samp_" + name)
        p_padded = samp("padded")
        p_idx = samp("idx")
        p_pt = samp("pt")
        p_state_in = samp("state_in")
        p_tabs = samp("tabs")
        p_rstd = samp("rstd")
        p_norm = samp("norm")
        p_out = samp("out")
        p_T1 = samp("T1")
        p_T1c = samp("T1c")
        p_wTc = samp("wTc")
        p_q = samp("q")
        p_qc = samp("qc")
        p_zn = samp("zn")
        p_ln = samp("ln")
        p_la = samp("la")
        p_dec = samp("dec")
        p_q4 = samp("q4")
        p_qT = samp("qT")
        p_qTc = samp("qTc")
        p_qlat = samp("qlat")
        p_qls = samp("qls")
        p_init = samp("init")
        p_initc = samp("initc")
        p_kz = samp("kz")
        p_T2 = samp("T2")
        p_T2c = samp("T2c")
        p_kv = samp("kv")
        p_state = samp("state")
        p_o = samp("o")
        p_r4 = samp("r4")
        p_gl = samp("gl")
        p_T3 = samp("T3")
        p_T3c = samp("T3c")
        f_idx = samp("f_idx")
        f_in = [samp(f"f_in{i}") for i in range(SLOTS)]
        f_T = samp("f_T")
        f_Ta = samp("f_Ta")
        f_Td = samp("f_Td")
        f_sc = samp("f_sc")
        f_mx = samp("f_mx")
        f_p = samp("f_p")
        f_pT = samp("f_pT")
        f_pTc = samp("f_pTc")
        f_o = samp("f_o")
        f_acc = samp("f_acc")
        f_on = samp("f_on")
        f_oT = samp("f_oT")
        f_oTc = samp("f_oTc")
        f_v = samp("f_v")
        f_mix = samp("f_mix")
        w_out_in = sem("w_out_in")
        ln_in = sem("ln_in")
        gate_b = sem("gate_b")
        gate_bc = sem("gate_bc")
        m_staged = sem("m_staged")
        xt_in = sem("xt_in")
        y_proj = sem("y_proj")
        y_read = sem("y_read")
        y_var = sem("y_var")
        y_rstd = sem("y_rstd")
        y_ready = sem("y_ready")
        y_out = sem("y_out")

        FROM_ONE = (S_ready, a_copied, a_transposed, cum_done, f_Ta, f_Td, f_acc, f_p, f_pT, f_pTc, f_sc, gated_T, gated_ready, kv_done, kv_out, mix_copied, normed, state_done, y_out, y_proj, y_read)

        LAG = 2
        STEPS = [(i, h) for i in range(T) for h in range(H)]

        NSTEPS = 2 * NSTEP

        def groups(s):
            return sum(i // 4 + 1 for i, _ in STEPS[:s])

        def gla_out(h):
            return banks[:, (7, 4)[h % 2], P * (h // 2):P * (h // 2) + P]

        def V(j, h):
            return z[:, j, W_GQ + VD * h:W_GQ + VD * h + VD]

        def gT(i):
            return z[:, i, W_GM:W_GQ].rearrange("p (h s) -> p h s", h=4)

        def score_bank(s):
            return banks[:, 2 * (s % 2):2 * (s % 2) + 2, :].rearrange("p b n -> p (b n)")

        def halves(v, s):
            w = v.rearrange("p (b two s) -> p b two s", two=2, s=s)
            return w[:, :, 0, :], w[:, :, 1, :]

        def rope_of(n):
            return rope[:, n, 0, :], rope[:, n, 1, :]

        lat_rows = a["cache_kv_latent"].rearrange("n (s r) d -> (n s) (r d)", r=ROWS)
        kro_rows = a["cache_k_rope"].rearrange("n (s r) d -> (n s) (r d)", r=ROWS)

        block = ctx.enter_context(nc.Block())

        def hold(eng):
            eng.sem_inc(held, 1)

        CONSTS = [
            (ident[:], a["c_ident"]), (upto[:], a["c_upto"]), (after[:], a["c_after"]),
            (future[:], a["c_future"]), (pairs_f, a["c_pairs"]), (rope[:], a["c_rope"]),
            (near[:], a["c_near"]),
            (own[:], a["c_own"]), (own8[:], a["c_own8"]), (sub[:], a["c_sub"]),
            (w_uq[:], a["w_uq"].rearrange("(k p) n -> p k n", p=P)),
            (w_uk[:], a["w_uk"].rearrange("r h n -> r (h n)")),
            (w_uv[:], a["w_uv"].rearrange("r h n -> r (h n)")),
            (w_gu[:], a["w_gate_up"]),
            (g_q[:], a["q_norm_g"].to_broadcast([P, QR])),
            (g_kv[:], a["kv_norm_g"].to_broadcast([P, KVR])),
            (b_gt[:], a["b_gate"].to_broadcast([P, GH * DK])),
            (g_gla[:], a["gla_norm_g"].rearrange("h v -> (h v)").unsqueeze(0).to_broadcast([P, GH * DV])),
        ]
        EARLY = [(fold[:], a["c_fold"]), (c_in[0:NB, :], a["c_sample"]), (c_in[NB:NB + 1, :], a["c_prompt"]),
                 (x_s[:], a["x_sample"])]
        for g in range(4):
            EARLY.append((b_adaA[32 * g:32 * g + 32, :], a["b_ada"][:, 512 * g:512 * g + 512].to_broadcast([32, 512])))
        for g in range(2):
            EARLY.append((b_adaB[32 * g:32 * g + 32, :],
                          a["b_ada"][:, 2048 + 512 * g:2560 + 512 * g].to_broadcast([32, 512])))
        early_in = sem("early_in")
        ident_in = sem("ident_in")
        N_EARLY, N_CONST = 16 * len(EARLY), 16 * (len(CONSTS) - 1)
        w_ada = a["w_ada"].rearrange("(k p) n -> k p n", p=P)
        w_in = a["w_in"].rearrange("(k p) n -> p k n", p=P)
        x_p = a["x_prompt"].rearrange("(t p) d -> p t d", p=P)

        @block.sync
        def _(sp):
            for s_ in FROM_ONE:
                sp.sem_inc(s_, 1)
            sp.dma_start(CONSTS[0][0], CONSTS[0][1]).then_inc(ident_in, 16)
            for dst, src in EARLY:
                sp.dma_start(dst, src).then_inc(early_in, 16)
            for half in range(2):
                for t in range(half * 4, half * 4 + 4):
                    sp.dma_start(x_all[:, t, :], x_p[:, t, :]).then_inc(x_in[half], 16)
            for k in range(KT):
                if k >= NADA:
                    sp.wait_ge(ada_used, k - NADA + 1)
                sp.dma_start(ada_ring[k % NADA], w_ada[k]).then_inc(ada_in[k % NADA], 16)
            for c in range(NCH):
                if c == 1:
                    sp.wait_ge(h_ready, 2 * KT)
                    sp.wait_ge(masks_ready, 1)
                if c >= 2:
                    sp.wait_ge(proj_done, 8 * (c - 1))
                sp.dma_start(w_raw[c % 2], w_in[:, :, CH * c:CH * c + CH]).then_inc(w_in_in[c % 2], 16)
                if c == 0:
                    for dst, src in CONSTS[1:]:
                        sp.dma_start(dst, src).then_inc(const_in, 16)
            with sp.Fori(0, T, 1) as t:
                sp.wait_ge(normed, t + 2)
                sp.dma_start(o["kv_prompt"][0, 0, bass.ds(t * P, P), :], ckvn).then_inc(kv_out, 16)
                sp.dma_start(o["kr_prompt"][0, 0, bass.ds(t * P, P), :], kr96[:, NOPE:QK]).then_inc(kv_out, 16)
            sp.wait_ge(S_ready, 2 * T + 1)
            st_p = o["st_prompt"][0, 0].rearrange("(hp par) d e -> par d hp e", par=2)
            for par in range(2):
                sp.dma_start(st_p[par], S[64 * par:64 * par + 64, :, :]).then_inc(S_out, 16)
            with nc.allow_non_contiguous_dma(reason="page numbers"):
                for b in range(NB):
                    tab = a["page_table"][b:b + 1, :].rearrange("b (c g) -> g (b c)", g=4)
                    for g in range(4):
                        c0 = (b // HALF) * NSTEP * HALF + b % HALF
                        sp.dma_start(pt_i[SUBS * g:SUBS * g + SUBS, c0:c0 + (NSTEP - 1) * HALF + 1:HALF],
                                     tab[g:g + 1, :].to_broadcast([SUBS, NSTEP])).then_inc(p_pt, 16)
            sp.wait_ge(sc_done, len(STEPS))
            sp.dma_start(w_out, a["w_out"].rearrange("(k p) n -> p k n", p=P)).then_inc(w_out_in, 16)
            sp.wait_ge(mixed, len(STEPS) // 2)
            for par in range(2):
                sp.dma_start(state[64 * par:64 * par + 64, :, :, :].rearrange("d b hp e -> d (b hp) e"),
                             a["state_gla"].rearrange("b (hp par) d e -> par d (b hp) e", par=2)[par]).then_inc(p_state_in, 16)
            sp.dma_start(spread, a["c_spread"]).then_inc(p_tabs, 16)
            sp.dma_start(pick, a["c_pick"]).then_inc(p_tabs, 16)
            sp.wait_ge(p_norm, 1)
            sp.dma_start(o["kv_sample"][0, :, 0, :], s_ckvn).then_inc(p_out, 16)
            sp.dma_start(o["kr_sample"][0, :, 0, :], s_kr).then_inc(p_out, 16)
            sp.wait_ge(p_state, 2 * NB)
            for par in range(2):
                sp.dma_start(o["st_sample"][0].rearrange("b (hp par) d e -> par d (b hp) e", par=2)[par],
                             state[64 * par:64 * par + 64, :, :, :].rearrange("d b hp e -> d (b hp) e")).then_inc(p_out, 16)
            sp.wait_ge(mixed, len(STEPS) // 2)
            sp.wait_ge(p_o, 1)
            sp.wait_ge(p_out, 64)
            sp.wait_ge(f_on, 2)
            sp.dma_start(g_ln, a["ln_g"].to_broadcast([P, D])).then_inc(ln_in, 16)
            sp.dma_start(b_ln, a["ln_b"].to_broadcast([P, D])).then_inc(ln_in, 16)
            sp.dma_start(x_t, x_p[:, 0, :]).then_inc(xt_in, 16)
            with sp.Fori(0, T - 1, 1) as t:
                sp.wait_ge(y_var, t + 1)
                sp.dma_start(x_t, x_p[:, bass.ds(t + 1, 1), :]).then_inc(xt_in, 16)
                sp.wait_ge(y_ready, t + 1)
                sp.dma_start(o["y_prompt"][0, bass.ds(t * P, P), :], y_t).then_inc(y_out, 16)
            sp.wait_ge(y_var, T)
            sp.dma_start(x_t[0:NB, :], a["x_sample"]).then_inc(xt_in, 16)
            sp.wait_ge(y_ready, T)
            sp.dma_start(o["y_prompt"][0, (T - 1) * P:, :], y_t).then_inc(y_out, 16)
            sp.wait_ge(y_ready, T + 1)
            sp.dma_start(o["y_sample"][:, 0, :], y_t[0:NB, :]).then_inc(y_out, 16)
            sp.wait_ge(y_out, 16 * (T + 1) + 1)
            sp.wait_ge(p_out, 64)
            sp.wait_ge(S_out, 32)
            sp.wait_ge(kv_out, 32 * T + 1)

        @block.gpsimd
        def _(pool):
            nc.gpsimd.memset(cT, 0.0).then_inc(padded, 1)
            nc.gpsimd.memset(hsT[:], 0.0).then_inc(padded, 1)
            nc.gpsimd.memset(eps_t[:], EPS).then_inc(padded, 1)
            pool.wait_ge(hs_ready, 1)
            for k in range(KT):
                nc.gpsimd.tensor_scalar(hT[:, k, 512:], hT[:, k, 512:], scT[:, k:k + 1], shT[:, k:k + 1],
                                        ALU.mult, ALU.add).then_inc(hf2_ready, 1)
            pool.wait_ge(const_in, N_CONST)
            nc.gpsimd.tensor_copy(masks[:], pairs_f).then_inc(masks_ready, 1)
            pool.wait_ge(silu_done, 5)
            pool.wait_ge(proj_copied, T * NCH)
            pool.wait_ge(sproj_copied, NCH)
            nc.gpsimd.memset(kr96, 0.0).then_inc(padded, 1)
            nc.gpsimd.memset(S, 0.0).then_inc(padded, 1)
            nc.gpsimd.memset(attm, 0.0).then_inc(padded, 1)

            def stage(k):
                nc.gpsimd.tensor_copy(qk_st, z[:, bass.ds(k, 1), W_GQ:W_GV]).then_inc(staged, 1)
                nc.gpsimd.tensor_copy(gl_st, z[:, bass.ds(k, 1), W_GL:W_GG]).then_inc(staged, 1)

            def gains(t):
                pool.wait_ge(state_done, t + 1)
                hold(pool)
                nc.gpsimd.tensor_copy(v_st, z[:, bass.ds(t, 1), W_GV:W_GL]).then_inc(vg_ready, 1)
                pool.wait_ge(gated_ready, t + 1)
                hold(pool)
                nc.gpsimd.tensor_tensor(gg, z[:, bass.ds(t, 1), W_GG:W_END], g_gla[:].unsqueeze(1), ALU.mult).then_inc(vg_ready, 1)

            stage(0)
            with pool.Fori(0, T - 1, 1) as t:
                gains(t)
                pool.wait_ge(kdec_ready, t + 1)
                pool.wait_ge(qk_transposed, t + 1)
                hold(pool)
                stage(t + 1)
            gains(T - 1)
            pool.wait_ge(gated_T, T + 1)
            pool.wait_ge(kv_out, 32 * T + 1)
            pool.wait_ge(S_out, 32)
            for i in range(T):
                pool.wait_ge(qp_copied, 2 * i + 2)
                q3 = q_tok.rearrange("p (h e) -> p h e", h=H)[:, :, NOPE:QK]
                r3 = q_rt.rearrange("p (h e) -> p h e", h=H)
                hr = ROPE // 2
                cs, sn = (rope[:, i, v:v + 1, :].to_broadcast([P, H, ROPE]) for v in range(2))
                nc.gpsimd.tensor_tensor(r3[:, :, 0:hr], q3[:, :, hr:ROPE], sn[:, :, 0:hr], ALU.mult).then_inc(rope_step, 1)
                nc.gpsimd.tensor_tensor(r3[:, :, hr:ROPE], q3[:, :, 0:hr], sn[:, :, hr:ROPE], ALU.mult).then_inc(rope_step, 1)
                pool.wait_ge(rope_step, 3 * i + 2)
                nc.gpsimd.tensor_tensor(q3, q3, cs, ALU.mult).then_inc(rope_step, 1)
                pool.wait_ge(rope_step, 3 * i + 3)
                nc.gpsimd.tensor_tensor(q3, q3, r3, ALU.add).then_inc(q_roped, 1)

            pool.wait_ge(p_pt, 16 * 4 * NB)
            pool.wait_ge(const_in, N_CONST)
            nc.gpsimd.tensor_scalar(idx[:], pt_i[:], float(SUBS), sub[:, 0:1], ALU.mult, ALU.add).then_inc(p_idx, 1)
            pool.wait_ge(mixed, len(STEPS) // 2)
            for v in (qls, qrs, s_cqT, s_qz):
                nc.gpsimd.memset(v, 0.0).then_inc(p_padded, 1)
            nc.gpsimd.tensor_tensor(s_kz, zs[:, W_GK:W_GV].unsqueeze(1).to_broadcast([NB, NB, 256]),
                                    own8[:].unsqueeze(2).to_broadcast([NB, NB, 256]), ALU.mult).then_inc(p_kz, 1)
            pool.wait_ge(p_idx, 1)

            def gather(n, u):
                nc.gpsimd.tensor_copy(idx_st[u][:], idx[:, bass.ds(n * HALF, HALF)]).then_inc(f_idx, 1)
                pool.wait_ge(f_idx, n + 1)
                hold(pool)
                for bb in range(HALF):
                    at = bass.IndirectOffsetOnAxis(ap=idx_st[u][:, bb:bb + 1], axis=0)
                    nc.gpsimd.indirect_dma_start(lat[u][:, bb, :], None, lat_rows, at).then_inc(f_in[u], 16)
                    nc.gpsimd.indirect_dma_start(kro[u][:, bb, :], None, kro_rows, at).then_inc(f_in[u], 16)

            for u in range(SLOTS):
                gather(u, u)
            with pool.Fori(0, NSTEPS // SLOTS - 1, 1) as j:
                for u in range(SLOTS):
                    pool.wait_ge(f_o, j * SLOTS + (u + 1))
                    gather(j * SLOTS + (u + SLOTS), u)
            pool.wait_ge(p_o, 1)
            pool.wait_ge(p_out, 64)
            for t in range(2):
                if t == 1:
                    pool.wait_ge(f_on, 2)
                nc.gpsimd.tensor_copy(mst[t], mixT[:, :, P * t:P * t + P]).then_inc(m_staged, 1)
            with pool.Fori(1, T // 2, 1) as j:
                for u in range(2):
                    pool.wait_ge(y_proj, j * 2 + u)
                    nc.gpsimd.tensor_copy(mst[u], mixT[:, :, bass.ds(j * (2 * P) + u * P, P)]).then_inc(m_staged, 1)

        @block.scalar
        def _(act):
            act.wait_ge(early_in, N_EARLY)
            nc.scalar.activation(c_act, c_in, ACT.Silu).then_inc(silu_done, 1)
            def split_w(slot):
                nc.scalar.activation(w_hi[slot], w_raw[slot], ACT.Copy).then_inc(w_hi_ready, 1)

            act.wait_ge(c_transposed, 1)
            act.wait_ge(w_in_in[0], 16)
            split_w(0)
            for n in range(2 * KT):
                k, half = n % KT, slice(512 * (n // KT), 512 * (n // KT) + 512)
                if n < KT:
                    act.wait_ge(hf_ready, n + 1)
                else:
                    act.wait_ge(hf2_ready, n - KT + 1)
                nc.scalar.activation(h_hi[:, k, half], hT[:, k, half], ACT.Copy).then_inc(h_hi_ready, 1)

            def copy_chunk(c, slot, arrived, func=ACT.Copy):
                for t in range(T):
                    act.wait_ge(proj_done, 8 * c + t + 1)
                    hold(act)
                    nc.scalar.activation(z[:, t, bass.ds(c * CH, CH)], banks[:, t % 6, 0:CH], func).then_inc(proj_copied, 1)
                    if t == 2:
                        act.wait_ge(sproj_done, 2 * c + 2)
                        hold(act)
                        nc.scalar.activation(zs[:, bass.ds(c * CH, CH)], banks[0:NB, 7, 0:CH], func).then_inc(sproj_copied, 1)
                        if arrived is not None:
                            act.wait_ge(w_in_in[1 - slot], arrived)
                            split_w(1 - slot)

            def silu(c0, c1, chunks):
                act.wait_ge(proj_copied, T * chunks)
                act.wait_ge(sproj_copied, chunks)
                nc.scalar.activation(z[:, :, c0:c1], z[:, :, c0:c1], ACT.Silu).then_inc(silu_done, 1)
                nc.scalar.activation(zs[:, c0:c1], zs[:, c0:c1], ACT.Silu).then_inc(silu_done, 1)

            assert NCH % 2 == 0 and (NCH - 2) * CH >= W_GG > (NCH - 3) * CH >= W_GQ
            copy_chunk(0, 0, 16)
            with act.Fori(0, (NCH - 4) // 2, 1) as i:
                for u in range(2):
                    copy_chunk(i * 2 + (u + 1), 1 - u, i * 16 + 32)
            silu(W_GM, W_GQ, NCH - 3)
            for c in range(NCH - 3, NCH):
                copy_chunk(c, c % 2, 16 * ((c + 1) // 2 + 1) if c + 1 < NCH else None,
                           ACT.Silu if c >= NCH - 2 else ACT.Copy)
            silu(W_GG, (NCH - 2) * CH, NCH - 2)
            act.wait_ge(proj_copied, T * NCH)
            act.wait_ge(sproj_copied, NCH)
            act.wait_ge(silu_done, 5)
            act.wait_ge(padded, 3)
            act.add_instruction(mybir.InstLoadActFuncSet(name=nc.get_next_instruction_name(), act_func_set_id=LN_EXP_SET,
                                                         ins=[], outs=[]))

            def rms(k, n0):
                nc.scalar.activation(junk[:, 0:QR], z[:, bass.ds(k, 1), W_CQ:W_CKV], ACT.Square, accum_out=ss[:, 0:1]).then_inc(chain_a, 1)
                nc.scalar.activation(junk[:, QR:QR + KVR], z[:, bass.ds(k, 1), W_CKV:W_KR], ACT.Square, accum_out=ss[:, 1:2]).then_inc(chain_a, 1)
                act.wait_ge(chain_a, n0 + 2)
                nc.scalar.activation(lnss[:, 0:1], ss[:, 0:1], ACT.Ln, bias=eps_t[:], scale=1.0 / QR).then_inc(chain_a, 1)
                nc.scalar.activation(lnss[:, 1:2], ss[:, 1:2], ACT.Ln, bias=eps_t[:], scale=1.0 / KVR).then_inc(chain_a, 1)
                act.wait_ge(chain_a, n0 + 4)
                act.wait_ge(normed, k + 1)
                nc.scalar.activation(rstd, lnss, ACT.Exp, scale=-0.5).then_inc(rstd_ready, 1)

            def tile(t, last):
                act.wait_ge(a_transposed, t + 2)
                act.wait_ge(kv_done, t + 1)
                nc.scalar.activation(ckvT, banks[:, 0, QR:QR + P], ACT.Copy).then_inc(a_copied, 1)
                act.wait_ge(zneg_ready, t + 1)
                nc.scalar.activation(zneg, zneg, ACT.Exp).then_inc(chain_a, 1)
                act.wait_ge(chain_a, t * 7 + 5)
                nc.scalar.activation(zneg, zneg, ACT.Ln, bias=1.0).then_inc(lnz_ready, 1)
                nc.scalar.activation(z[:, bass.ds(t, 1), 0:QR], banks[:, 0, 0:QR], ACT.Copy).then_inc(a_copied, 1)
                nc.scalar.activation(KTh[NOPE:QK, :, bass.ds(t * P, P)],
                                     banks[NOPE:QK, 0, 384:512].unsqueeze(1).to_broadcast([ROPE, H, P]), ACT.Copy).then_inc(a_copied, 1)
                act.wait_ge(k_done, t + 1)
                hold(act)
                for q in range(2):
                    nc.scalar.activation(KTh[0:NOPE, 4 * q:4 * q + 4, bass.ds(t * P, P)],
                                         banks[0:NOPE, 3 + q, :].rearrange("p (h s) -> p h s", h=4), ACT.Copy).then_inc(k_copied, 1)
                act.wait_ge(bT_copied, t + 1)
                act.wait_ge(cum_done, t + 2)
                nc.scalar.activation(eb, bT, ACT.Exp).then_inc(e_ready, 1)
                nc.scalar.activation(esuf, banks[:, 6, 256:512], ACT.Exp).then_inc(e_ready, 1)
                act.wait_ge(kv_done, t + 2)
                act.wait_ge(staged, t * 2 + 2)
                hold(act)
                nc.scalar.activation(z[:, bass.ds(t, 1), W_GQ:W_GV], banks[:, 5, :], ACT.Copy).then_inc(v_copied, 1)
                for lv in range(LEVELS):
                    act.wait_ge(d_ready, t * LEVELS + lv + 1)
                    nc.scalar.activation(dl[lv % 2], dl[lv % 2], ACT.Exp).then_inc(el_ready, 1)
                n0 = t * 7 + 5
                if not last:
                    rms(t + 1, n0)
                    n0 = t * 7 + 9
                act.wait_ge(o_done, t + 1)
                for h in range(GH):
                    done = nc.scalar.activation(junk[:, P * h:P * h + P], gla_out(h), ACT.Square, accum_out=ss4[:, h:h + 1])
                    if h == GH - 1:
                        done.then_inc(chain_a, 1)
                act.wait_ge(chain_a, n0 + 1)
                nc.scalar.activation(ss4, ss4, ACT.Ln, bias=eps_t[:], scale=1.0 / DV).then_inc(chain_a, 1)
                act.wait_ge(chain_a, n0 + 2)
                act.wait_ge(gated_ready, t + 1)
                nc.scalar.activation(rstd4, ss4, ACT.Exp, scale=-0.5).then_inc(r4_ready, 1)
                act.wait_ge(gated_T, t + 2)
                hold(act)
                nc.scalar.activation(mixT[:, 4:8, bass.ds(t * P, P)], banks[:, 6, :].rearrange("p (h s) -> p h s", h=4), ACT.Copy).then_inc(mix_copied, 1)

            rms(0, 0)
            with act.Fori(0, T - 1, 1) as t:
                tile(t, False)
            tile(T - 1, True)

            def q_half(i, q):
                act.wait_ge(qp_done, 2 * i + q + 1)
                if i > 0:
                    act.wait_ge(qt_done, 2 * i)
                nc.scalar.activation(q_tok[:, 384 * q:384 * q + 384], banks[:, 7, 0:384], ACT.Copy).then_inc(qp_copied, 1)

            def qt_half(i, q):
                act.wait_ge(qt_done, 2 * i + q + 1)
                if i > 1:
                    act.wait_ge(sc_done, H * (i - 1))
                nc.scalar.activation(QTb[i % 2][:, 4 * q:4 * q + 4, :], banks[0:QK, 7, :].rearrange("p (h s) -> p h s", h=4),
                                     ACT.Copy).then_inc(qt_copied, 1)

            act.wait_ge(gated_T, T + 1)
            act.wait_ge(kv_out, 32 * T + 1)
            act.wait_ge(S_out, 32)
            for q in range(2):
                q_half(0, q)
            for q in range(2):
                qt_half(0, q)
            for s in range(len(STEPS) + LAG):
                if s < len(STEPS):
                    i, h = STEPS[s]
                    w = P * (i + 1)
                    if h == 0:
                        act.wait_ge(gt_done, i + 1)
                        nc.scalar.activation(gT(i), banks[:, 7, :].rearrange("p (h s) -> p h s", h=4), ACT.Copy).then_inc(gt_copied, 1)
                    act.wait_ge(mx_ready, s + 1)
                    if s >= 3:
                        act.wait_ge(pt_done, groups(s - 2))
                    nc.scalar.activation(Pm[s % 3][:, 0:w], score_bank(s)[:, 0:w], ACT.Exp, bias=nmx[:, s % 4:s % 4 + 1],
                                         scale=MLA_SCALE, accum_out=rsum[:, s % 4:s % 4 + 1]).then_inc(p_ready, 1)
                if s >= LAG:
                    r = s - LAG
                    i1 = STEPS[r][0]
                    if r >= 3:
                        act.wait_ge(pv_done, (r - 3) // 2 + 1)
                    for g in range(i1 // 4 + 1):
                        n = min(4, i1 + 1 - 4 * g)
                        act.wait_ge(pt_done, groups(r) + g + 1)
                        nc.scalar.activation(PTb[r % 3][:, 4 * g:4 * g + n, :],
                                             banks[:, 4 + (groups(r) + g) % 2, 0:P * n].rearrange("p (j q) -> p j q", j=n),
                                             ACT.Copy).then_inc(pt_copied, 1)
                if s < len(STEPS) and i + 1 < T:
                    if h in (2, 3):
                        q_half(i + 1, h - 2)
                    if h in (5, 6):
                        qt_half(i + 1, h - 5)

            act.wait_ge(mixed, len(STEPS) // 2)
            n_a = T * 7
            nc.scalar.activation(s_junk[:, 0:QR], zs[:, W_CQ:W_CKV], ACT.Square, accum_out=s_ss[:, 0:1]).then_inc(chain_a, 1)
            nc.scalar.activation(s_junk[:, QR:QR + KVR], zs[:, W_CKV:W_KR], ACT.Square, accum_out=s_ss[:, 1:2]).then_inc(chain_a, 1)
            act.wait_ge(chain_a, n_a + 2)
            nc.scalar.activation(s_ss[:, 2:3], s_ss[:, 0:1], ACT.Ln, bias=eps_t[0:NB], scale=1.0 / QR).then_inc(chain_a, 1)
            nc.scalar.activation(s_ss[:, 3:4], s_ss[:, 1:2], ACT.Ln, bias=eps_t[0:NB], scale=1.0 / KVR).then_inc(chain_a, 1)
            act.wait_ge(chain_a, n_a + 4)
            nc.scalar.activation(s_ss[:, 4:6], s_ss[:, 2:4], ACT.Exp, scale=-0.5).then_inc(p_rstd, 1)
            act.wait_ge(p_T1, 1)
            for q in range(2):
                nc.scalar.activation(w_ukT[:, 4 * q:4 * q + 4, :], banks[0:NOPE, 1 + q, :].rearrange("p (h r) -> p h r", h=4), ACT.Copy).then_inc(p_wTc, 1)
            act.wait_ge(p_q, 1)
            for q in range(2):
                nc.scalar.activation(sq[:, 384 * q:384 * q + 384], banks[0:NB, 3 + q, 0:384], ACT.Copy).then_inc(p_qc, 1)
            act.wait_ge(p_zn, 1)
            nc.scalar.activation(s_zn, s_zn, ACT.Exp).then_inc(chain_a, 1)
            act.wait_ge(chain_a, n_a + 5)
            nc.scalar.activation(s_zn, s_zn, ACT.Ln, bias=1.0).then_inc(p_ln, 1)
            act.wait_ge(p_la, 1)
            nc.scalar.activation(s_la, s_la, ACT.Exp).then_inc(p_dec, 1)
            act.wait_ge(p_o, 1)
            for h in range(GH):
                nc.scalar.activation(s_junk[:, P * h:P * h + P], banks[0:NB, 5 + h % 2, P * (h // 2):P * (h // 2) + P], ACT.Square,
                                     accum_out=s_ss[:, h:h + 1]).then_inc(chain_a, 1)
            act.wait_ge(chain_a, n_a + 9)
            nc.scalar.activation(s_ss[:, 0:4], s_ss[:, 0:4], ACT.Ln, bias=eps_t[0:NB], scale=1.0 / DV).then_inc(chain_a, 1)
            act.wait_ge(chain_a, n_a + 10)
            nc.scalar.activation(s_ss[:, 4:8], s_ss[:, 0:4], ACT.Exp, scale=-0.5).then_inc(p_r4, 1)

            def keys_out(n, u):
                act.wait_ge(f_T, n * 5 + 1)
                hold(act)
                nc.scalar.activation(latT[u][:, 0, :], banks[:, 0, :], ACT.Copy).then_inc(f_Ta, 1)
                act.wait_ge(f_T, n * 5 + 3)
                hold(act)
                nc.scalar.activation(latT[u][:, 2, :], banks[:, 2, :], ACT.Copy).then_inc(f_Ta, 1)
                act.wait_ge(f_T, n * 5 + 5)
                hold(act)
                nc.scalar.activation(kroT[u], banks[:, 4, :].rearrange("p (b t) -> p b t", b=HALF), ACT.Copy).then_inc(f_Ta, 1)

            def weights(n, hf):
                act.wait_ge(f_mx, n + 1)
                act.wait_ge(f_pT, n + 1)
                nc.scalar.activation(sc, banks[:, 5, :], ACT.Exp, bias=st[:, 2:3], scale=MLA_SCALE, accum_out=st[:, 4:5]).then_inc(f_p, 1)
                nc.scalar.activation(st[:, 3:4], m_run[:, hf:hf + 1], ACT.Exp, bias=st[:, 2:3], scale=MLA_SCALE).then_inc(f_p, 1)

            act.wait_ge(p_out, 64)
            keys_out(0, 0)
            for hf in range(2):
                with act.Fori(4 * hf, 4 * hf + 4 - hf, 1) as j:
                    for u in range(2):
                        weights(j * 2 + u, hf)
                        keys_out(j * 2 + (u + 1), 1 - u)
            weights(NSTEPS - 2, 1)
            keys_out(NSTEPS - 1, 1)
            weights(NSTEPS - 1, 1)

            for q in range(2):
                act.wait_ge(gate_b, 1)
                nc.scalar.activation(gateP[:, 512 * q:512 * q + 512], banks[:, 2 + q, :], ACT.Copy).then_inc(gate_bc, 1)
                nc.scalar.activation(gateS[:, 512 * q:512 * q + 512], banks[0:NB, 4 + q, :], ACT.Copy).then_inc(gate_bc, 1)

            def deviation(t, rows):
                act.wait_ge(y_var, t + 1)
                nc.scalar.activation(lr[0:rows, 0:1], bag[0:rows, 1:2], ACT.Ln, bias=eps_t[0:rows], scale=1.0).then_inc(chain_a, 1)
                act.wait_ge(chain_a, t + (n_a + 11))
                nc.scalar.activation(lr[0:rows, 1:2], lr[0:rows, 0:1], ACT.Exp, scale=-0.5).then_inc(y_rstd, 1)

            with act.Fori(0, T, 1) as t:
                deviation(t, P)
            deviation(T, NB)

        @block.vector
        def _(dve):
            for n in range(2 * KT):
                k, half = n // 2, n % 2
                dve.wait_ge(x_transposed, n + 1)
                nc.vector.tensor_copy(hT[:, k, 512 * half:512 * half + 512], banks[:, n % 4, :]).then_inc(x_copied, 1)
            dve.wait_ge(x_transposed, 2 * KT + 1)
            nc.vector.tensor_copy(xsT, banks[:, 4, 0:KT * NB].rearrange("p (k b) -> p k b", k=KT)).then_inc(x_copied, 1)
            dve.wait_ge(c_transposed, 1)
            dve.wait_ge(padded, 1)
            nc.vector.tensor_copy(cT[:, :, 0:9], banks[:, 5, 0:KT * 9].rearrange("p (k b) -> p k b", k=KT)).then_inc(x_copied, 1)
            dve.wait_ge(ada_used, KT)
            nc.vector.tensor_tensor(modA, banks[:, 6, :], b_adaA, ALU.add).then_inc(mod_ready, 1)
            nc.vector.tensor_tensor(modB[:], banks[0:64, 7, :], b_adaB[0:64, :], ALU.add).then_inc(mod_ready, 1)
            dve.wait_ge(modT_done, 1)
            mt = banks[:, 0, :].rearrange("p (s g r) -> p s g r", s=4, g=4)
            kv = lambda t_: t_.rearrange("p (g s) -> p g s", g=2)
            kvb = lambda t_: t_.rearrange("p (g s) b -> p g s b", g=2)
            nc.vector.tensor_copy(kv(shT), mt[:, :, 0:2, NB].rearrange("p s g -> p g s")).then_inc(chain_d, 1)
            nc.vector.tensor_scalar(kv(scT), mt[:, :, 2:4, NB].rearrange("p s g -> p g s"), 1.0, None, ALU.add).then_inc(chain_d, 1)
            for g in range(2):
                nc.vector.tensor_copy(shsT[:, 4 * g:4 * g + 4, :], mt[:, :, g, 0:NB]).then_inc(chain_d, 1)
                nc.vector.tensor_scalar(scsT[:, 4 * g:4 * g + 4, :], mt[:, :, 2 + g, 0:NB], 1.0, None, ALU.add).then_inc(chain_d, 1)
            dve.wait_ge(chain_d, 6)
            dve.wait_ge(x_copied, 2 * KT + 1)
            nc.vector.tensor_tensor(hs_tmp, xsT, scsT, ALU.mult).then_inc(chain_d, 1)
            dve.wait_ge(chain_d, 7)
            dve.wait_ge(padded, 2)
            nc.vector.tensor_tensor(hsT[:, :, 0:NB], hs_tmp, shsT, ALU.add).then_inc(hs_ready, 1)
            def low_parts(n):
                k, half = n % KT, slice(512 * (n // KT), 512 * (n // KT) + 512)
                dve.wait_ge(h_hi_ready, n + 1)
                if n >= KT:
                    dve.wait_ge(hf2_ready, n - KT + 1)
                nc.vector.tensor_tensor(h_lo[:, k, half], hT[:, k, half], h_hi[:, k, half], ALU.subtract).then_inc(h_ready, 1)

            def fold_chunk(c, slot):
                dve.wait_ge(sproj_done, 2 * c + 1)
                nc.vector.tensor_copy(zs_part, banks[:, 6, 0:CH]).then_inc(sproj_part, 1)
                dve.wait_ge(w_hi_ready, c + 1)
                nc.vector.tensor_tensor(w_lo[slot], w_raw[slot], w_hi[slot], ALU.subtract).then_inc(w_ready, 1)

            for n in range(KT):
                nc.vector.tensor_scalar(hT[:, n, 0:512], hT[:, n, 0:512], scT[:, n:n + 1], shT[:, n:n + 1],
                                        ALU.mult, ALU.add).then_inc(hf_ready, 1)
                if n > 1:
                    low_parts(n - 2)
                if n == 4:
                    fold_chunk(0, 0)
            for n in range(KT - 2, 2 * KT):
                low_parts(n)
            with dve.Fori(0, (NCH - 2) // 2, 1) as i:
                for u in range(2):
                    fold_chunk(i * 2 + (u + 1), 1 - u)
            fold_chunk(NCH - 1, 1)
            n_d = 7
            dve.wait_ge(silu_done, 5)
            dve.wait_ge(proj_copied, T * NCH)
            dve.wait_ge(sproj_copied, NCH)
            dve.wait_ge(const_in, N_CONST)
            dve.wait_ge(padded, 6)
            dve.wait_ge(masks_ready, 1)
            PER_T = 2

            def norm_rows(k):
                tz = bass.ds(k, 1)
                dve.wait_ge(rstd_ready, k + 1)
                dve.wait_ge(a_transposed, k + 1)
                dve.wait_ge(kv_out, k * 32 + 1)
                hold(dve)
                nc.vector.scalar_tensor_tensor(out=cqn, in0=z[:, tz, W_CQ:W_CKV], scalar=rstd[:, 0:1], in1=g_q[:], op0=ALU.mult, op1=ALU.mult)
                nc.vector.scalar_tensor_tensor(out=ckvn, in0=z[:, tz, W_CKV:W_KR], scalar=rstd[:, 1:2], in1=g_kv[:], op0=ALU.mult, op1=ALU.mult)
                kr = z[:, tz, W_KR:W_GM].rearrange("p o e -> p (o e)")
                cs, sn = (rope[:, tz, q, :].rearrange("p o e -> p (o e)") for q in range(2))
                hr = ROPE // 2
                nc.vector.tensor_tensor(kr96[:, NOPE:QK], kr, cs, ALU.mult)
                nc.vector.tensor_tensor(rtmp[:, 0:hr], kr[:, hr:ROPE], sn[:, 0:hr], ALU.mult)
                nc.vector.tensor_tensor(rtmp[:, hr:ROPE], kr[:, 0:hr], sn[:, hr:ROPE], ALU.mult).then_inc(chain_d, 1)
                dve.wait_ge(chain_d, k * PER_T + (n_d + 1))
                nc.vector.tensor_tensor(kr96[:, NOPE:QK], kr96[:, NOPE:QK], rtmp, ALU.add).then_inc(normed, 1)

            def rows_out(k):
                dve.wait_ge(qk_transposed, k + 1)
                nc.vector.tensor_copy(glT, banks[0:GR, 2, 0:P]).then_inc(glT_copied, 1)
                nc.vector.tensor_scalar(qkT[:, 0:2, :], banks[:, 1, 0:256].rearrange("p (a s) -> p a s", a=2), GLA_SCALE, None, ALU.mult)
                nc.vector.tensor_copy(qkT[:, 2:4, :], banks[:, 1, 256:512].rearrange("p (a s) -> p a s", a=2)).then_inc(qkT_copied, 1)

            def gate_parts(k):
                dve.wait_ge(gate_done, k + 1)
                nc.vector.tensor_tensor(zg, banks[:, 2, 256:512], b_gt[:], ALU.add).then_inc(gate_copied, 1)
                dve.wait_ge(gate_copied, k + 1)
                nc.vector.scalar_tensor_tensor(out=zneg, in0=zg, scalar=-1.0, in1=zg, op0=ALU.mult, op1=ALU.min).then_inc(zneg_ready, 1)
                nc.vector.tensor_scalar(zmin, zg, 0.0, 1.0 / TAU, ALU.min, ALU.mult).then_inc(chain_d, 1)

            def tile(t, last_tile):
                dve.wait_ge(lnz_ready, t + 1)
                dve.wait_ge(chain_d, t * PER_T + (n_d + 2))
                dve.wait_ge(cum_done, t + 1)
                nc.vector.scalar_tensor_tensor(out=la, in0=zneg, scalar=-1.0 / TAU, in1=zmin, op0=ALU.mult, op1=ALU.add).then_inc(la_ready, 1)
                dve.wait_ge(cum_done, t + 2)
                nc.vector.tensor_copy(bT, banks[:, 6, 0:256]).then_inc(bT_copied, 1)
                dve.wait_ge(bT_copied, t + 1)
                dve.wait_ge(qkT_copied, t + 1)
                def level_d(lv):
                    s = P >> (lv + 1)
                    b1, b2 = halves(bT, s)
                    d1, d2 = halves(dl[lv % 2], s)
                    ref = b1[:, :, s - 1:s].to_broadcast([P, P // s, s])
                    nc.vector.tensor_tensor(d1, ref, b1, ALU.subtract)
                    nc.vector.tensor_tensor(d2, b2, ref, ALU.subtract).then_inc(d_ready, 1)

                qf = qkT[:, 0:2, :].rearrange("p a s -> p (a s)")
                kf = qkT[:, 2:4, :].rearrange("p a s -> p (a s)")

                def level_x(lv):
                    s = P >> (lv + 1)
                    e1, e2 = halves(dl[lv % 2], s)
                    x1, x2 = halves(xl[lv % 2], s)
                    dve.wait_ge(el_ready, t * LEVELS + lv + 1)
                    if lv >= 2:
                        dve.wait_ge(att_done, t * (LEVELS + 1) + lv)
                    nc.vector.tensor_tensor(x1, e1, halves(kf, s)[0], ALU.mult)
                    nc.vector.tensor_tensor(x2, e2, halves(qf, s)[1], ALU.mult).then_inc(x_ready, 1)

                pair4 = lambda n: (banks[:, 3:5, 0:256] if n % 2 == 0 else banks[:, 5:8:2, 0:256]).rearrange("p b (h i) -> p b h i", h=2)
                mask4 = lambda m: m.unsqueeze(1).unsqueeze(1).to_broadcast([P, 2, 2, P])
                low4 = lambda n: (banks[:, 3:5, 0:64] if n % 2 == 0 else banks[:, 5:8:2, 0:64]).rearrange("p b (h i) -> p b h i", h=2)
                mask_low4 = lambda m: m.unsqueeze(1).unsqueeze(1).to_broadcast([P, 2, 2, 32])
                level_d(0)
                level_d(1)
                dve.wait_ge(att_done, t * (LEVELS + 1) + 1)
                nc.vector.tensor_tensor(attn, low4(0), mask_low4(near[:]), ALU.mult).then_inc(att_copied, 1)
                level_x(0)
                dve.wait_ge(e_ready, t * 2 + 2)
                nc.vector.tensor_tensor(qb, eb, qf, ALU.mult).then_inc(qb_ready, 1)
                nc.vector.tensor_tensor(kdec, esuf, qk_st[:, 256:512], ALU.mult).then_inc(kdec_ready, 1)
                for lv in range(LEVELS):
                    if lv + 1 < LEVELS:
                        level_x(lv + 1)
                    if lv + 2 < LEVELS:
                        dve.wait_ge(x_ready, t * LEVELS + lv + 1)
                        level_d(lv + 2)
                    dve.wait_ge(att_done, t * (LEVELS + 1) + lv + 2)
                    dve.wait_ge(att_copied, t * (LEVELS + 1) + lv + 1)
                    hold(dve)
                    if lv < WIDE:
                        nc.vector.copy_predicated(attm, mask4(pairs[:, lv, :]), pair4(lv + 1)).then_inc(att_copied, 1)
                    else:
                        nc.vector.copy_predicated(attn, mask_low4(pairs_low[:, lv - WIDE, :]), low4(lv + 1)).then_inc(att_copied, 1)
                dve.wait_ge(att_copied, t * (LEVELS + 1) + LEVELS + 1)
                for g in range(4):
                    b32 = slice(32 * g, 32 * g + 32)
                    last = nc.vector.tensor_copy(attm[b32, :, :, b32], attn[b32])
                last.then_inc(blocks_in, 1)
                if not last_tile:
                    norm_rows(t + 1)
                    rows_out(t + 1)
                dve.wait_ge(state_done, t + 2)
                dve.wait_ge(o_done, t + 1)
                for hp in range(2):
                    nc.vector.scalar_tensor_tensor(out=S[:, hp, :], in0=S[:, hp, :], scalar=eb[:, P * hp + P - 1:P * hp + P],
                                                   in1=banks[:, 5, P * hp:P * hp + P], op0=ALU.mult, op1=ALU.add).then_inc(S_ready, 1)
                dve.wait_ge(r4_ready, t + 1)
                dve.wait_ge(vg_ready, t * 2 + 2)
                dve.wait_ge(gated_T, t + 1)
                for h in range(GH):
                    last = nc.vector.scalar_tensor_tensor(out=gated[:, P * h:P * h + P], in0=gla_out(h),
                                                          scalar=rstd4[:, h:h + 1], in1=gg[:, P * h:P * h + P], op0=ALU.mult, op1=ALU.mult)
                last.then_inc(gated_ready, 1)
                if not last_tile:
                    gate_parts(t + 1)

            norm_rows(0)
            rows_out(0)
            gate_parts(0)
            with dve.Fori(0, T - 1, 1) as t:
                tile(t, False)
            tile(T - 1, True)

            n_d = n_d + PER_T * T

            def rotate(q3, tmp3, cs, sn, rows, n0):
                hr = ROPE // 2
                nh = q3.shape[1]
                bc = lambda v: v.unsqueeze(1).to_broadcast([rows, nh, hr])
                nc.vector.tensor_tensor(tmp3[:, :, 0:hr], q3[:, :, hr:ROPE], bc(sn[:, 0:hr]), ALU.mult).then_inc(chain_d, 1)
                nc.vector.tensor_tensor(tmp3[:, :, hr:ROPE], q3[:, :, 0:hr], bc(sn[:, hr:ROPE]), ALU.mult).then_inc(chain_d, 1)
                dve.wait_ge(chain_d, n0 + 2)
                nc.vector.tensor_tensor(q3, q3, cs.unsqueeze(1).to_broadcast([rows, nh, ROPE]), ALU.mult).then_inc(chain_d, 1)
                dve.wait_ge(chain_d, n0 + 3)
                return nc.vector.tensor_tensor(q3, q3, tmp3, ALU.add)

            def mix(p):
                i, hp = p // 4, p % 4
                dve.wait_ge(pv_done, p + 1)
                dve.wait_ge(gt_copied, i + 1)
                nc.vector.tensor_tensor(mixT[:, hp, P * i:P * i + P], banks[:, 6, 0:P], gT(i)[:, hp, :], ALU.mult).then_inc(mixed, 1)

            dve.wait_ge(gated_T, T + 1)
            dve.wait_ge(kv_out, 32 * T + 1)
            dve.wait_ge(S_out, 32)
            for s in range(len(STEPS) + 5):
                if s >= 6 and s % 2 == 0:
                    mix((s - 6) // 2)
                if s < len(STEPS):
                    i, h = STEPS[s]
                    w = P * (i + 1)
                    c = s % 4
                    dve.wait_ge(sc_done, s + 1)
                    diag = score_bank(s)[:, P * i:P * i + P]
                    nc.vector.tensor_tensor(diag, diag, future[:], ALU.add).then_inc(chain_d, 1)
                    dve.wait_ge(chain_d, n_d + 1)
                    nc.vector.reduce_max(nmx[:, c:c + 1], score_bank(s)[:, 0:w], AX_X).then_inc(chain_d, 1)
                    dve.wait_ge(chain_d, n_d + 2)
                    nc.vector.tensor_scalar(nmx[:, c:c + 1], nmx[:, c:c + 1], -MLA_SCALE, None, ALU.mult).then_inc(mx_ready, 1)
                    n_d += 2
                if 1 <= s <= len(STEPS):
                    c, w1 = (s - 1) % 4, P * (STEPS[s - 1][0] + 1)
                    dve.wait_ge(p_ready, s)
                    nc.vector.reciprocal(rinv[:, c:c + 1], rsum[:, c:c + 1]).then_inc(chain_d, 1)
                    n_d += 1
                    dve.wait_ge(chain_d, n_d)
                    nc.vector.tensor_scalar(Pm[(s - 1) % 3][:, 0:w1], Pm[(s - 1) % 3][:, 0:w1], rinv[:, c:c + 1], None, ALU.mult).then_inc(pn_ready, 1)

            r8 = slice(0, NB)
            cs_s, sn_s = rope[0:NB, T, 0, :], rope[0:NB, T, 1, :]
            dve.wait_ge(p_rstd, 1)
            nc.vector.scalar_tensor_tensor(out=s_cqn, in0=zs[:, W_CQ:W_CKV], scalar=s_ss[:, 4:5], in1=g_q[r8], op0=ALU.mult, op1=ALU.mult)
            nc.vector.scalar_tensor_tensor(out=s_ckvn, in0=zs[:, W_CKV:W_KR], scalar=s_ss[:, 5:6], in1=g_kv[r8], op0=ALU.mult, op1=ALU.mult)
            nc.vector.tensor_copy(s_kr, zs[:, W_KR:W_GM]).then_inc(chain_d, 1)
            dve.wait_ge(chain_d, n_d + 1)
            rotate(s_kr.unsqueeze(1), s_kr4[:, 0:1, :], cs_s, sn_s, NB, n_d + 1).then_inc(chain_d, 1)
            n_d += 5
            dve.wait_ge(chain_d, n_d)
            nc.vector.tensor_copy(s_kr4, s_kr.unsqueeze(1).to_broadcast([NB, 4, ROPE])).then_inc(p_norm, 1)
            dve.wait_ge(p_T1, 1)
            dve.wait_ge(p_padded, 4)
            nc.vector.tensor_copy(s_cqT[:, :, 0:NB], banks[:, 0, 0:16].rearrange("p (k b) -> p k b", k=2))
            nc.vector.tensor_copy(knT, banks[:, 0, 16:24])
            nc.vector.tensor_copy(krnT, banks[:, 0, 24:32])
            nc.vector.tensor_copy(s_glT, banks[0:GR, 0, 32:40])
            nc.vector.tensor_copy(s_qgT, banks[:, 0, 96:112].rearrange("p (k b) -> p k b", k=2)).then_inc(chain_d, 1)
            nc.vector.tensor_copy(s_gmT, banks[:, 0, 64:96].rearrange("p (k b) -> p k b", k=4)).then_inc(p_T1c, 1)
            n_d += 1
            dve.wait_ge(p_q, 1)
            nc.vector.tensor_tensor(s_zg, banks[0:NB, 5, 0:256], b_gt[r8], ALU.add).then_inc(chain_d, 1)
            dve.wait_ge(chain_d, n_d + 1)
            nc.vector.scalar_tensor_tensor(out=s_zn, in0=s_zg, scalar=-1.0, in1=s_zg, op0=ALU.mult, op1=ALU.min).then_inc(p_zn, 1)
            nc.vector.tensor_scalar(s_zm, s_zg, 0.0, 1.0 / TAU, ALU.min, ALU.mult).then_inc(chain_d, 1)
            dve.wait_ge(chain_d, n_d + 2)
            dve.wait_ge(p_ln, 1)
            nc.vector.scalar_tensor_tensor(out=s_la, in0=s_zn, scalar=-1.0 / TAU, in1=s_zm, op0=ALU.mult, op1=ALU.add).then_inc(p_la, 1)
            n_d += 2
            dve.wait_ge(p_qc, 2)
            sq3 = sq.rearrange("p (h e) -> p h e", h=H)[:, :, NOPE:QK]
            rotate(sq3, sq_r.rearrange("p (h e) -> p h e", h=H), cs_s, sn_s, NB, n_d).then_inc(chain_d, 1)
            n_d += 4
            dve.wait_ge(chain_d, n_d)
            for r in range(4):
                nc.vector.tensor_copy(sq4[:, :, r, :], sq3).then_inc(p_q4, 1)
            dve.wait_ge(p_qT, 1)
            nc.vector.tensor_copy(s_ql, banks[0:NOPE, 6, 0:64].rearrange("p (h b) -> p h b", h=H)).then_inc(p_qTc, 1)
            for r in range(4):
                nc.vector.tensor_copy(qrs[32 * r:32 * r + 32, :, r, 0:H],
                                      banks[32 * r:32 * r + 32, 7, 0:64].rearrange("p (h b) -> p b h", h=H)).then_inc(p_qTc, 1)
            dve.wait_ge(p_qlat, 1)
            nc.vector.tensor_copy(qls[:, :, 0:H], banks[:, 0, 0:64].rearrange("p (h b) -> p b h", h=H)).then_inc(p_qls, 1)
            dve.wait_ge(p_init, 1)
            nc.vector.tensor_copy(m_run, banks[:, 1, 0:2]).then_inc(p_initc, 1)
            nc.vector.memset(l_run, 1.0).then_inc(p_initc, 1)
            nc.vector.tensor_copy(o_acc, banks[:, 1, 128:384].rearrange("p (f r) -> p f r", f=2)).then_inc(p_initc, 1)
            dve.wait_ge(p_T2, 1)
            nc.vector.tensor_copy(s_decT, banks[:, 0, 0:16].rearrange("p (k b) -> p k b", k=2)).then_inc(chain_d, 1)
            for hp in range(2):
                nc.vector.scalar_tensor_tensor(out=s_qz[:, hp, :, 0:NB], in0=s_qgT[:, hp, :].unsqueeze(1).to_broadcast([P, NB, NB]),
                                               scalar=GLA_SCALE, in1=own[:], op0=ALU.mult, op1=ALU.mult).then_inc(p_T2c, 1)
            n_d += 1
            dve.wait_ge(chain_d, n_d)
            dve.wait_ge(p_kv, 1)
            dve.wait_ge(p_state_in, 32)
            for b in range(NB):
                for hp in range(2):
                    c0 = 256 * (b % 2) + P * hp
                    nc.vector.scalar_tensor_tensor(out=state[:, b, hp, :], in0=state[:, b, hp, :], scalar=s_decT[:, hp, b:b + 1],
                                                   in1=banks[:, 1 + b // 2, c0:c0 + P], op0=ALU.mult, op1=ALU.add).then_inc(p_state, 1)
            dve.wait_ge(p_r4, 1)
            nc.vector.tensor_tensor(s_gg, zs[:, W_GG:W_END], g_gla[r8], ALU.mult).then_inc(chain_d, 1)
            n_d += 1
            dve.wait_ge(chain_d, n_d)
            for h in range(GH):
                nc.vector.scalar_tensor_tensor(out=s_gl[:, P * h:P * h + P], in0=banks[0:NB, 5 + h % 2, P * (h // 2):P * (h // 2) + P],
                                               scalar=s_ss[:, 4 + h:5 + h], in1=s_gg[:, P * h:P * h + P], op0=ALU.mult, op1=ALU.mult).then_inc(p_gl, 1)
            dve.wait_ge(p_T3, 1)
            nc.vector.tensor_copy(mixTs[:, 4:8, 0:NB], banks[:, 0, 0:32].rearrange("p (k b) -> p k b", k=4)).then_inc(p_T3c, 1)

            def keys_out(n, u):
                dve.wait_ge(f_T, n * 5 + 2)
                hold(dve)
                nc.vector.tensor_copy(latT[u][:, 1, :], banks[:, 1, :]).then_inc(f_Td, 1)
                dve.wait_ge(f_T, n * 5 + 4)
                hold(dve)
                nc.vector.tensor_copy(latT[u][:, 3, :], banks[:, 3, :]).then_inc(f_Td, 1)

            def running(n, u, hf, last):
                dve.wait_ge(f_sc, n + 2)
                hold(dve)
                nc.vector.reduce_max(st[:, 0:1], banks[:, 5, :], AX_X).then_inc(chain_d, 1)
                dve.wait_ge(chain_d, n * 3 + (n_d + 1))
                nc.vector.tensor_tensor(st[:, 1:2], st[:, 0:1], m_run[:, hf:hf + 1], ALU.max).then_inc(chain_d, 1)
                dve.wait_ge(chain_d, n * 3 + (n_d + 2))
                nc.vector.tensor_scalar(st[:, 2:3], st[:, 1:2], -MLA_SCALE, None, ALU.mult).then_inc(f_mx, 1)
                if not last:
                    keys_out(n + 1, 1 - u)
                dve.wait_ge(f_p, n * 2 + 3)
                nc.vector.tensor_copy(m_run[:, hf:hf + 1], st[:, 1:2])
                nc.vector.scalar_tensor_tensor(out=l_run[:, hf:hf + 1], in0=l_run[:, hf:hf + 1], scalar=st[:, 3:4], in1=st[:, 4:5],
                                               op0=ALU.mult, op1=ALU.add).then_inc(chain_d, 1)
                dve.wait_ge(f_pT, n + 2)
                nc.vector.tensor_copy(pT, banks[:, 6, :].rearrange("p (r q) -> p r q", r=4)).then_inc(f_pTc, 1)
                dve.wait_ge(f_o, n + 1)
                nc.vector.scalar_tensor_tensor(out=o_acc[:, hf, :], in0=o_acc[:, hf, :], scalar=st[:, 3:4], in1=banks[:, 7, 0:KVR],
                                               op0=ALU.mult, op1=ALU.add).then_inc(f_acc, 1)
                dve.wait_ge(f_acc, n + 2)

            dve.wait_ge(p_out, 64)
            keys_out(0, 0)
            for hf in range(2):
                with dve.Fori(4 * hf, 4 * hf + 4 - hf, 1) as j:
                    for u in range(2):
                        running(j * 2 + u, u, hf, False)
            running(NSTEPS - 2, 0, 1, False)
            running(NSTEPS - 1, 1, 1, True)
            n_d += 3 * 16
            dve.wait_ge(chain_d, n_d)
            nc.vector.reciprocal(st[:, 6:8], l_run).then_inc(chain_d, 1)
            n_d += 1
            dve.wait_ge(chain_d, n_d)
            for hf in range(2):
                nc.vector.tensor_scalar(o_n[:, hf, :], o_acc[:, hf, :], st[:, 6 + hf:7 + hf], None, ALU.mult).then_inc(f_on, 1)
            dve.wait_ge(f_oT, 1)
            nc.vector.tensor_copy(oT_lat, banks[:, 0, 0:256].rearrange("p (f q) -> p f q", f=2)).then_inc(f_oTc, 1)
            dve.wait_ge(f_v, 1)
            nc.vector.tensor_tensor(mixTs[:, 0:4, 0:NB], banks[:, 1, 0:32].rearrange("p (k b) -> p k b", k=4), s_gmT, ALU.mult).then_inc(f_mix, 1)

            dve.wait_ge(p_kv, 1)
            dve.wait_ge(ln_in, 32)
            dve.wait_ge(gate_bc, 4)

            def norm_out(t, rows, gate, bk):
                v = slice(0, rows)
                at = lambda c: t * 5 + (n_d + c)
                dve.wait_ge(y_proj, t + 2)
                nc.vector.tensor_tensor(r_t[v], banks[v, bk:bk + 2, :].rearrange("p b n -> p (b n)"), gate, ALU.mult).then_inc(y_read, 1)
                dve.wait_ge(y_read, t + 2)
                dve.wait_ge(xt_in, t * 16 + 16)
                nc.vector.scalar_tensor_tensor(out=r_t[v], in0=x_t[v], scalar=ALPHA, in1=r_t[v], op0=ALU.mult, op1=ALU.add).then_inc(chain_d, 1)
                dve.wait_ge(chain_d, at(1))
                for q in range(2):
                    nc.vector.bn_stats(bst[v, 6 * q:6 * q + 6], r_t[v, 512 * q:512 * q + 512]).then_inc(chain_d, 1)
                dve.wait_ge(chain_d, at(3))
                hold(dve)
                nc.vector.bn_aggr(bag[v], bst[v]).then_inc(y_var, 1)
                dve.wait_ge(y_rstd, t + 1)
                dve.wait_ge(y_out, t * 16 + 1)
                nc.vector.tensor_scalar(y_t[v], r_t[v], bag[v, 0:1], lr[v, 1:2], ALU.subtract, ALU.mult).then_inc(chain_d, 1)
                dve.wait_ge(chain_d, at(4))
                nc.vector.tensor_tensor(y_t[v], y_t[v], g_ln[v], ALU.mult).then_inc(chain_d, 1)
                dve.wait_ge(chain_d, at(5))
                nc.vector.tensor_tensor(y_t[v], y_t[v], b_ln[v], ALU.add).then_inc(y_ready, 1)

            with dve.Fori(0, T // 2, 1) as j:
                for u in range(2):
                    norm_out(j * 2 + u, P, gateP, 2 * u)
            norm_out(T, NB, gateS, 4)

        @block.tensor
        def _(pe):
            pe.wait_ge(ident_in, 16)
            for n in range(2 * KT):
                k, half = n // 2, n % 2
                if n < 2:
                    pe.wait_ge(x_in[half], 64)
                if n >= 4:
                    pe.wait_ge(x_copied, n - 3)
                for t in range(4):
                    last = nc.tensor.transpose(banks[:, n % 4, P * t:P * t + P],
                                               x_all[:, 4 * half + t, P * k:P * k + P], ident[:])
                last.then_inc(x_transposed, 1)
            pe.wait_ge(early_in, N_EARLY)
            for k in range(KT):
                last = nc.tensor.transpose(banks[:, 4, NB * k:NB * k + NB], x_s[:, P * k:P * k + P], ident[0:NB, 0:NB])
            last.then_inc(x_transposed, 1)
            pe.wait_ge(silu_done, 1)
            for k in range(KT):
                last = nc.tensor.transpose(banks[:, 5, 9 * k:9 * k + 9], c_act[:, P * k:P * k + P], ident[0:9, 0:9])
            last.then_inc(c_transposed, 1)
            pe.wait_ge(x_copied, 2 * KT + 2)
            for k in range(KT):
                pe.wait_ge(ada_in[k % NADA], 16 * (k // NADA + 1))
                for ch in range(6):
                    g = ch % 4
                    last = nc.tensor.matmul(banks[32 * g:32 * g + 32, 6 + ch // 4, :], cT[:, k, :],
                                            ada_ring[k % NADA][:, 512 * ch:512 * ch + 512],
                                            start=(k == 0), stop=(k == KT - 1))
                last.then_inc(ada_used, 1)
            pe.wait_ge(mod_ready, 2)
            for s_ in range(4):
                last = nc.tensor.transpose(banks[:, 0, P * s_:P * s_ + P], modA[:, P * s_:P * s_ + P], ident[:])
            last.then_inc(modT_done, 1)

            def samples_part(slot):
                for kk in range(2):
                    for g in range(4):
                        last = nc.tensor.matmul(banks[32 * g:32 * g + 32, 6, 0:CH], hsT[:, 4 * kk + g, :],
                                                w_raw[slot][:, 4 * kk + g, :], start=(kk == 0), stop=(kk == 1))
                last.then_inc(sproj_done, 1)

            def chunk(c, slot, peeled, arrived):
                pe.wait_ge(w_ready, c + 1)
                for t in range(T):
                    if peeled and t == T // 2:
                        pe.wait_ge(h_ready, 2 * KT)
                    if peeled:
                        if t >= 6:
                            pe.wait_ge(proj_copied, t - 5)
                    elif t < 2:
                        pe.wait_ge(proj_copied, 8 * c + t - 1)
                    elif t < 6:
                        pe.wait_ge(proj_copied, 8 * c + t - 7)
                    else:
                        pe.wait_ge(proj_copied, 8 * c + t - 5)
                    for k in range(KT):
                        if peeled and t == 0:
                            pe.wait_ge(h_ready, k + 1)
                        for n, (h_, w_) in enumerate(((h_hi, w_hi), (h_hi, w_lo), (h_lo, w_hi))):
                            last = nc.tensor.matmul(banks[:, t % 6, 0:CH], h_[:, k, P * t:P * t + P],
                                                    w_[slot][:, k, :], start=(k == 0 and n == 0),
                                                    stop=(k == KT - 1 and n == 2))
                    last.then_inc(proj_done, 1)
                    if t == 0:
                        pe.wait_ge(sproj_part, c + 1)
                        if not peeled:
                            pe.wait_ge(sproj_copied, c)
                        nc.tensor.matmul(banks[0:32, 7, 0:CH], fold[:], zs_part, start=True, stop=True).then_inc(sproj_done, 1)
                    if t == 2 and arrived is not None:
                        pe.wait_ge(w_in_in[1 - slot], arrived)
                        samples_part(1 - slot)

            pe.wait_ge(hs_ready, 1)
            pe.wait_ge(w_in_in[0], 16)
            samples_part(0)
            chunk(0, 0, True, 16)
            with pe.Fori(0, (NCH - 2) // 2, 1) as i:
                for u in range(2):
                    chunk(i * 2 + (u + 1), 1 - u, False, i * 16 + 32)
            chunk(NCH - 1, 1, False, None)
            pe.wait_ge(proj_copied, T * NCH)
            pe.wait_ge(sproj_copied, NCH)

            def latent_rows(k):
                pe.wait_ge(normed, k + 2)
                pe.wait_ge(a_copied, k * 3 + 1)
                for q in range(2):
                    nc.tensor.transpose(banks[:, 0, P * q:P * q + P], cqn[:, P * q:P * q + P], ident[:])
                nc.tensor.transpose(banks[:, 0, 256:384], ckvn, ident[:])
                nc.tensor.transpose(banks[0:QK, 0, 384:512], kr96, ident[:]).then_inc(a_transposed, 1)

            def gated_rows(k, first):
                pe.wait_ge(staged, k * 2 + 2)
                if not first:
                    pe.wait_ge(qkT_copied, k)
                    pe.wait_ge(gate_copied, k)
                for q in range(4):
                    nc.tensor.transpose(banks[:, 1, P * q:P * q + P], qk_st[:, P * q:P * q + P], ident[:])
                nc.tensor.transpose(banks[0:GR, 2, 0:P], gl_st, ident[:]).then_inc(qk_transposed, 1)

            def forget_gate(k):
                pe.wait_ge(glT_copied, k + 1)
                nc.tensor.matmul(banks[:, 2, 256:512], glT, w_gu[:], start=True, stop=True).then_inc(gate_done, 1)

            def tile(t, last_tile):
                pe.wait_ge(a_copied, t * 3 + 2)
                pe.wait_ge(gated_ready, t + 1)
                for h in range(H):
                    last = nc.tensor.matmul(banks[0:NOPE, 3 + h // 4, P * (h % 4):P * (h % 4) + P], w_uk[:, NOPE * h:NOPE * h + NOPE], ckvT,
                                            start=True, stop=True)
                last.then_inc(k_done, 1)
                pe.wait_ge(la_ready, t + 1)
                pe.wait_ge(mix_copied, t + 1)
                for q in range(2):
                    nc.tensor.matmul(banks[:, 6, P * q:P * q + P], la[:, P * q:P * q + P], upto[:], start=True, stop=True)
                nc.tensor.matmul(banks[:, 6, 256:512], after[:], la, start=True, stop=True).then_inc(cum_done, 1)
                pe.wait_ge(S_ready, t * 2 + 1)
                nc.tensor.matmul(banks[:, 5, :], ckvT, w_uv[:], start=True, stop=True).then_inc(kv_done, 1)
                pe.wait_ge(qkT_copied, t + 1)
                pe.wait_ge(k_copied, t * 2 + 2)
                for n in range(LEVELS + 1):
                    if n > 0:
                        pe.wait_ge(x_ready, t * LEVELS + n)
                    if n == 1:
                        pe.wait_ge(v_copied, t + 1)
                    if n >= 2:
                        pe.wait_ge(att_copied, t * (LEVELS + 1) + n - 1)
                    if n == 0 or n > WIDE:
                        hold(pe)
                    for h in range(GH):
                        rows = slice(64 * (h % 2), 64 * (h % 2) + 64)
                        bk = (3, 4)[h % 2] if n % 2 == 0 else (5, 7)[h % 2]
                        c0 = P * (h // 2)
                        left = qkT[rows, 2 + h // 2, :] if n == 0 else xl[(n - 1) % 2][rows, c0:c0 + P]
                        right = qkT[rows, h // 2, :] if n == 0 else left
                        if 1 <= n <= WIDE:
                            last = nc.tensor.matmul(banks[:, bk, c0:c0 + P], left, right, start=True, stop=True)
                        else:
                            for g in range(4):
                                last = nc.tensor.matmul(banks[32 * g:32 * g + 32, bk, 32 * (h // 2):32 * (h // 2) + 32],
                                                        left[:, 32 * g:32 * g + 32], right[:, 32 * g:32 * g + 32], start=True, stop=True)
                    last.then_inc(att_done, 1)
                if not last_tile:
                    gated_rows(t + 1, False)
                pe.wait_ge(blocks_in, t + 1)
                pe.wait_ge(qb_ready, t + 1)
                pe.wait_ge(vg_ready, t * 2 + 1)
                for h in range(GH):
                    rows = slice(64 * (h % 2), 64 * (h % 2) + 64)
                    nc.tensor.matmul(gla_out(h), attm[:, h % 2, h // 2, :], v_st[:, P * h:P * h + P], start=True, stop=False)
                    last = nc.tensor.matmul(gla_out(h), qb[rows, P * (h // 2):P * (h // 2) + P], S[rows, h // 2, :],
                                            start=False, stop=True)
                last.then_inc(o_done, 1)
                pe.wait_ge(kdec_ready, t + 1)
                for h in range(GH):
                    rows = slice(64 * (h % 2), 64 * (h % 2) + 64)
                    last = nc.tensor.matmul(banks[rows, 5, P * (h // 2):P * (h // 2) + P], kdec[:, 64 * h:64 * h + 64],
                                            v_st[:, P * h:P * h + P], start=True, stop=True)
                last.then_inc(state_done, 1)
                if not last_tile:
                    latent_rows(t + 1)
                    forget_gate(t + 1)
                pe.wait_ge(gated_ready, t + 2)
                for h in range(GH):
                    last = nc.tensor.transpose(banks[:, 6, P * h:P * h + P], gated[:, P * h:P * h + P], ident[:])
                last.then_inc(gated_T, 1)

            pe.wait_ge(const_in, N_CONST)
            latent_rows(0)
            gated_rows(0, True)
            forget_gate(0)
            with pe.Fori(0, T - 1, 1) as t:
                tile(t, False)
            tile(T - 1, True)

            pe.wait_ge(mix_copied, T + 1)
            pe.wait_ge(S_ready, 2 * T + 1)

            def q_proj(i, q):
                if i > 0 or q > 0:
                    pe.wait_ge(qp_copied, 2 * i + q)
                if i > 0:
                    pe.wait_ge(qt_copied, 2 * i)
                    pe.wait_ge(gt_copied, i)
                for k in range(2):
                    last = nc.tensor.matmul(banks[:, 7, 0:384], z[:, i, P * k:P * k + P], w_uq[:, k, 384 * q:384 * q + 384],
                                            start=(k == 0), stop=(k == 1))
                last.then_inc(qp_done, 1)

            def q_transpose(i, q):
                pe.wait_ge(q_roped, i + 1)
                if q > 0:
                    pe.wait_ge(qt_copied, 2 * i + q)
                for h in range(4):
                    last = nc.tensor.transpose(banks[0:QK, 7, P * h:P * h + P], q_tok[:, QK * (4 * q + h):QK * (4 * q + h) + QK], ident[:])
                last.then_inc(qt_done, 1)

            def products(p):
                i = STEPS[2 * p][0]
                hp = p % 4
                pe.wait_ge(pt_copied, groups(2 * p + 2))
                if p > 0:
                    pe.wait_ge(mixed, p)
                for j in range(i + 1):
                    for par in range(2):
                        last = nc.tensor.matmul(banks[64 * par:64 * par + 64, 6, 0:P], V(j, 2 * hp + par), PTb[(2 * p + par) % 3][:, j, :],
                                                start=(j == 0), stop=(j == i))
                last.then_inc(pv_done, 1)

            for q in range(2):
                q_proj(0, q)
            for q in range(2):
                q_transpose(0, q)
            for s in range(len(STEPS) + LAG):
                if s < len(STEPS):
                    i, h = STEPS[s]
                    w = P * (i + 1)
                    if h == 0:
                        pe.wait_ge(qt_copied, 2 * i + 2)
                        for q in range(4):
                            last = nc.tensor.transpose(banks[:, 7, P * q:P * q + P], z[:, i, W_GM + P * q:W_GM + P * q + P], ident[:])
                        last.then_inc(gt_done, 1)
                    pe.wait_ge(qt_copied, 2 * i + 2)
                    if s >= 2:
                        pe.wait_ge(p_ready, s - 1)
                    for n0 in range(0, w, 512):
                        n1 = min(w, n0 + 512)
                        last = nc.tensor.matmul(score_bank(s)[:, n0:n1], QTb[i % 2][:, h, :], KTh[:, h, n0:n1], start=True, stop=True)
                    last.then_inc(sc_done, 1)
                if s >= LAG:
                    r = s - LAG
                    i1 = STEPS[r][0]
                    pe.wait_ge(pn_ready, r + 1)
                    for g in range(i1 // 4 + 1):
                        k0 = groups(r) + g
                        if k0 >= 2:
                            pe.wait_ge(pt_copied, k0 - 1)
                        for j in range(4 * g, min(4 * g + 4, i1 + 1)):
                            last = nc.tensor.transpose(banks[:, 4 + k0 % 2, P * (j % 4):P * (j % 4) + P], Pm[r % 3][:, P * j:P * j + P], ident[:])
                        last.then_inc(pt_done, 1)
                    if r % 2 == 0 and r >= 2:
                        products((r - 2) // 2)
                if s < len(STEPS) and i + 1 < T:
                    if h in (2, 3):
                        q_proj(i + 1, h - 2)
                    if h in (5, 6):
                        q_transpose(i + 1, h - 5)
            products(len(STEPS) // 2 - 1)

            pe.wait_ge(p_norm, 1)
            pe.wait_ge(mixed, len(STEPS) // 2)
            i8 = ident[0:NB, 0:NB]
            for q in range(2):
                nc.tensor.transpose(banks[:, 0, NB * q:NB * q + NB], s_cqn[:, P * q:P * q + P], i8)
            nc.tensor.transpose(banks[:, 0, 16:24], s_ckvn, i8)
            nc.tensor.transpose(banks[:, 0, 24:32], s_kr4.rearrange("p a e -> p (a e)"), i8)
            nc.tensor.transpose(banks[0:GR, 0, 32:40], zs[:, W_GL:W_GG], i8)
            for q in range(4):
                nc.tensor.transpose(banks[:, 0, 64 + NB * q:64 + NB * q + NB], zs[:, W_GM + P * q:W_GM + P * q + P], i8)
            for q in range(2):
                nc.tensor.transpose(banks[:, 0, 96 + NB * q:96 + NB * q + NB], zs[:, W_GQ + P * q:W_GQ + P * q + P], i8)
            for h in range(H):
                last = nc.tensor.transpose(banks[0:NOPE, 1 + h // 4, P * (h % 4):P * (h % 4) + P], w_uk[:, NOPE * h:NOPE * h + NOPE], ident[:])
            last.then_inc(p_T1, 1)
            pe.wait_ge(p_T1c, 1)
            for q in range(2):
                for k in range(2):
                    nc.tensor.matmul(banks[0:32, 3 + q, 0:384], s_cqT[:, k, :], w_uq[:, k, 384 * q:384 * q + 384], start=(k == 0), stop=(k == 1))
            nc.tensor.matmul(banks[0:NB, 5, 0:256], s_glT, w_gu[:], start=True, stop=True).then_inc(p_q, 1)
            pe.wait_ge(p_q4, 4)
            for h in range(H):
                nc.tensor.transpose(banks[0:NOPE, 6, NB * h:NB * h + NB], sq[:, QK * h:QK * h + NOPE], i8)
            for h in range(H):
                last = nc.tensor.transpose(banks[:, 7, NB * h:NB * h + NB], sq4[:, h, :, :].rearrange("p a e -> p (a e)"), i8)
            last.then_inc(p_qT, 1)
            pe.wait_ge(p_qTc, 5)
            pe.wait_ge(p_wTc, 2)
            for h in range(H):
                last = nc.tensor.matmul(banks[:, 0, NB * h:NB * h + NB], w_ukT[:, h, :], s_ql[:, h, :], start=True, stop=True)
            last.then_inc(p_qlat, 1)
            pe.wait_ge(p_qls, 1)
            pe.wait_ge(p_tabs, 32)
            for hf in range(2):
                for bb in range(HALF):
                    b = HALF * hf + bb
                    dst = banks[32 * bb:32 * bb + 32, 1, hf:hf + 1]
                    nc.tensor.matmul(dst, qls[:, b, :], knT[:, b:b + 1], start=True, stop=False)
                    nc.tensor.matmul(dst, qrs[:, b, 0, :], krnT[:, b:b + 1], start=False, stop=True)
            for hf in range(2):
                last = nc.tensor.matmul(banks[:, 1, P + P * hf:2 * P + P * hf], spread[:, hf, :], s_ckvn, start=True, stop=True)
            last.then_inc(p_init, 1)
            pe.wait_ge(p_dec, 1)
            for q in range(2):
                last = nc.tensor.transpose(banks[:, 0, NB * q:NB * q + NB], s_la[:, P * q:P * q + P], i8)
            last.then_inc(p_T2, 1)
            pe.wait_ge(p_kz, 1)
            pe.wait_ge(p_initc, 3)
            pe.wait_ge(p_qc, 2)
            for b in range(NB):
                for h in range(GH):
                    rows = slice(64 * (h % 2), 64 * (h % 2) + 64)
                    c0 = 256 * (b % 2) + P * (h // 2)
                    last = nc.tensor.matmul(banks[rows, 1 + b // 2, c0:c0 + P], s_kz[:, b, 64 * h:64 * h + 64],
                                            zs[:, W_GV + P * h:W_GV + P * h + P], start=True, stop=True)
            last.then_inc(p_kv, 1)
            pe.wait_ge(p_T2c, 2)
            pe.wait_ge(p_state, 2 * NB)
            pe.wait_ge(p_zn, 1)
            for par in range(2):
                rows = slice(64 * par, 64 * par + 64)
                for hp in range(2):
                    for b in range(NB):
                        last = nc.tensor.matmul(banks[0:32, 5 + par, P * hp:P * hp + P], s_qz[rows, hp, b, :], state[rows, b, hp, :],
                                                start=(b == 0), stop=(b == NB - 1))
            last.then_inc(p_o, 1)
            pe.wait_ge(p_gl, 4)
            for q in range(4):
                last = nc.tensor.transpose(banks[:, 0, NB * q:NB * q + NB], s_gl[:, P * q:P * q + P], i8)
            last.then_inc(p_T3, 1)
            pe.wait_ge(p_T3c, 1)
            def rows_transposed(n, v):
                for bb in range(HALF):
                    if bb % 2 == 0:
                        pe.wait_ge(f_Ta, n * 3 + 1)
                    else:
                        pe.wait_ge(f_Td, n * 2 + 1)
                    for r in range(ROWS):
                        last = nc.tensor.transpose(banks[:, bb, P * r:P * r + P], lat[v][:, bb, KVR * r:KVR * r + KVR], ident[:])
                    last.then_inc(f_T, 1)
                for bb in range(HALF):
                    last = nc.tensor.transpose(banks[:, 4, P * bb:P * bb + P], kro[v][:, bb, :], ident[:])
                last.then_inc(f_T, 1)

            def scores(n, u, hf):
                pe.wait_ge(f_Ta, n * 3 + 4)
                pe.wait_ge(f_Td, n * 2 + 3)
                pe.wait_ge(f_p, n * 2 + 1)
                for bb in range(HALF):
                    nc.tensor.matmul(banks[32 * bb:32 * bb + 32, 5, :], qls[:, HALF * hf + bb, :], latT[u][:, bb, :], start=True, stop=False)
                for r in range(ROWS):
                    for bb in range(HALF):
                        last = nc.tensor.matmul(banks[32 * bb:32 * bb + 32, 5, P * r:P * r + P], qrs[:, HALF * hf + bb, r, :], kroT[u][:, bb, :],
                                                start=False, stop=(r == ROWS - 1))
                last.then_inc(f_sc, 1)

            def weighted(n, v):
                pe.wait_ge(f_p, n * 2 + 3)
                pe.wait_ge(f_pTc, n + 1)
                for r in range(ROWS):
                    last = nc.tensor.transpose(banks[:, 6, P * r:P * r + P], sc[:, P * r:P * r + P], ident[:])
                last.then_inc(f_pT, 1)
                pe.wait_ge(f_pTc, n + 2)
                pe.wait_ge(f_acc, n + 1)
                for r in range(ROWS):
                    for bb in range(HALF):
                        last = nc.tensor.matmul(banks[32 * bb:32 * bb + 32, 7, 0:KVR], pT[:, r, 32 * bb:32 * bb + 32],
                                                lat[v][:, bb, KVR * r:KVR * r + KVR], start=(r == 0), stop=(r == ROWS - 1))
                last.then_inc(f_o, 1)

            ARRIVED = 16 * 2 * HALF
            pe.wait_ge(f_in[0], ARRIVED)
            rows_transposed(0, 0)
            for hf in range(2):
                with pe.Fori(2 * hf, 2 * hf + 2 - hf, 1) as j:
                    for v in range(SLOTS):
                        n = j * SLOTS + v
                        scores(n, v % 2, hf)
                        pe.wait_ge(f_in[(v + 1) % SLOTS], j * ARRIVED + ARRIVED * (1 + (v + 1) // SLOTS))
                        rows_transposed(n + 1, (v + 1) % SLOTS)
                        weighted(n, v)
            for v in range(SLOTS):
                n = NSTEPS - SLOTS + v
                scores(n, v % 2, 1)
                if v + 1 < SLOTS:
                    pe.wait_ge(f_in[v + 1], ARRIVED * (NSTEPS // SLOTS))
                    rows_transposed(n + 1, v + 1)
                weighted(n, v)
            pe.wait_ge(f_on, 2)
            for hf in range(2):
                last = nc.tensor.transpose(banks[:, 0, P * hf:P * hf + P], o_n[:, hf, :], ident[:])
            last.then_inc(f_oT, 1)
            pe.wait_ge(f_oTc, 1)
            for h in range(H):
                heads = oT_lat.rearrange("p f (b q) -> p f b q", b=HALF)[:, :, :, h].rearrange("p f b -> p (f b)")
                last = nc.tensor.matmul(banks[64 * (h % 2):64 * (h % 2) + 64, 1, NB * (h // 2):NB * (h // 2) + NB],
                                        w_uv[:, VD * h:VD * h + VD], heads, start=True, stop=True)
            last.then_inc(f_v, 1)

            for q in range(2):
                nc.tensor.matmul(banks[:, 2 + q, :], pick[:, q, 0:P], modB[:], start=True, stop=True)
                last = nc.tensor.matmul(banks[0:32, 4 + q, :], pick[:, q, P:P + 32], modB[:], start=True, stop=True)
            last.then_inc(gate_b, 1)
            pe.wait_ge(w_out_in, 16)
            pe.wait_ge(f_mix, 1)
            pe.wait_ge(gate_bc, 4)
            def project_out(t, u, first):
                pe.wait_ge(m_staged, t + 1)
                if not first:
                    pe.wait_ge(y_read, t)
                for q in range(2):
                    for k in range(KT):
                        last = nc.tensor.matmul(banks[:, 2 * u + q, :], mst[u][:, k, :], w_out[:, k, 512 * q:512 * q + 512],
                                                start=(k == 0), stop=(k == KT - 1))
                last.then_inc(y_proj, 1)

            for t in range(2):
                project_out(t, t, True)
            with pe.Fori(1, T // 2, 1) as j:
                for u in range(2):
                    project_out(j * 2 + u, u, False)
            for q in range(2):
                for k in range(KT):
                    last = nc.tensor.matmul(banks[0:32, 4 + q, :], mixTs[:, k, :], w_out[:, k, 512 * q:512 * q + 512], start=(k == 0), stop=(k == KT - 1))
            last.then_inc(y_proj, 1)


_OUTS = [
    ("y_prompt", (1, SEQ, D)), ("y_sample", (NB, 1, D)), ("kv_prompt", (1, 1, SEQ, KVR)),
    ("kr_prompt", (1, 1, SEQ, ROPE)), ("st_prompt", (1, 1, GH, DK, DV)), ("kv_sample", (1, NB, 1, KVR)),
    ("kr_sample", (1, NB, 1, ROPE)), ("st_sample", (1, NB, GH, DK, DV)),
]
_INS = ["x_prompt", "x_sample", "cache_kv_latent", "cache_k_rope", "state_gla", "page_table", "c_prompt",
        "c_sample", "w_ada", "b_ada", "w_in", "q_norm_g", "w_uq", "kv_norm_g", "w_uk", "w_uv", "w_gate_up",
        "b_gate", "gla_norm_g", "w_out", "ln_g", "ln_b"]


def kernel(**inputs):
    import numpy as _np
    import concourse.bacc as _bacc
    from concourse.bass_utils import run_bass_kernel_spmd as _run

    nc = _bacc.Bacc("TRN2", target_bir_lowering=False, num_devices=1,
                    dynamic_dma_scratch_size=8192)
    arrays, args, outs = {}, {}, {}
    given = {n: _np.ascontiguousarray(inputs[n]) for n in _INS}
    given.update({"c_" + n: _np.ascontiguousarray(v) for n, v in shape_constants().items()})
    lead = {"x_prompt", "cache_kv_latent", "cache_k_rope", "state_gla", "w_ada", "w_in", "w_uq", "w_uk", "w_uv",
            "w_gate_up", "gla_norm_g", "w_out"}
    for name, v in given.items():
        arrays["in_" + name] = v
        ap = nc.dram_tensor("in_" + name, v.shape, mybir.dt.from_np(v.dtype), kind="ExternalInput").ap()
        if name in lead:
            ap = ap[0]
        elif name == "x_sample":
            ap = ap.rearrange("b s d -> (b s) d")
        args[name] = ap
    for name, shape in _OUTS:
        outs[name] = nc.dram_tensor("out_" + name, shape, F32, kind="ExternalOutput").ap()
    hybrid_step(nc, args, outs)
    r = _run(nc, [arrays], core_ids=[0])
    return tuple(r.results[0]["out_" + name] for name, _ in _OUTS)
```
